# Optimizing a Trainium2 kernel written in Bass

```python
import math
import jax, jax.numpy as jnp
from jax import lax
import numpy as np
import jax
import jax.numpy as jnp

D_MODEL = 1024
BATCH = 1
SEQ = 512
DEPTH = 2

HEAD_DIM = 64
N_RET = 6
N_NSA = 6
N_KV = 2
HPG = N_NSA // N_KV
N_GM = 4
GM_DIM = 64
RET_W = N_RET * HEAD_DIM
NSA_W = N_NSA * HEAD_DIM
GM_W = N_GM * GM_DIM
MIX_W = RET_W + NSA_W + GM_W
RET_CHUNK = 128
CMP_LEN = 32
CMP_STRIDE = 16
SEL_BLOCK = 64
N_SEL = 16
WINDOW = 512
Q_BLOCK = 128
GM_CHUNK = 128
N_BUCKETS = 32
MAX_DISTANCE = 128
ROPE_THETA = 10000.0
D_FF = -(-8 * D_MODEL // (3 * 256)) * 256
SPLIT_SIZES = (RET_W, RET_W, RET_W, RET_W, NSA_W, 3 * 2 * N_KV * HEAD_DIM, 3 * N_NSA, 2 * GM_W)
IN_W = sum(SPLIT_SIZES)
EPS = 1e-6
BIG = 1e9
NEG = -1e30


def rms_norm(x, gain=None):
    xf = x.astype(jnp.float32)
    y = xf * lax.rsqrt(jnp.mean(xf * xf, axis=-1, keepdims=True) + EPS)
    if gain is not None:
        y = y * gain.astype(jnp.float32)
    return y.astype(x.dtype)

def rope(x, pos):
    half = x.shape[-1] // 2
    inv = ROPE_THETA ** (-jnp.arange(half, dtype=jnp.float32) / half)
    ang = pos.astype(jnp.float32)[:, None] * inv[None, :]
    cos = jnp.cos(ang)[None, :, None, :]
    sin = jnp.sin(ang)[None, :, None, :]
    x1 = x[..., :half].astype(jnp.float32)
    x2 = x[..., half:].astype(jnp.float32)
    return jnp.concatenate([x1 * cos - x2 * sin, x2 * cos + x1 * sin], axis=-1).astype(x.dtype)

def t5_bucket(dist):
    n = jnp.maximum(dist, 0)
    max_exact = N_BUCKETS // 2
    nf = jnp.maximum(n, 1).astype(jnp.float32)
    large = max_exact + (jnp.log(nf / max_exact) / math.log(MAX_DISTANCE / max_exact)
                         * (N_BUCKETS - max_exact)).astype(jnp.int32)
    large = jnp.minimum(large, N_BUCKETS - 1)
    return jnp.where(n < max_exact, n, large)

def masked_softmax(logits, mask):
    s = jnp.where(mask, logits.astype(jnp.float32), NEG)
    return jax.nn.softmax(s, axis=-1) * mask

def retention(q, k, v, g):
    B, T, H, d = q.shape
    C = RET_CHUNK
    nc = T // C
    f32 = jnp.float32
    to_chunks = lambda a: a.astype(f32).reshape(B, nc, C, H, d).transpose(0, 3, 1, 2, 4)
    qc, kc, vc = to_chunks(q), to_chunks(k * d ** -0.5), to_chunks(v)
    log_gamma = jnp.log(1.0 - 2.0 ** (-5.0 - jnp.arange(H, dtype=f32)))
    idx = jnp.arange(C, dtype=f32)
    diff = idx[:, None] - idx[None, :]
    decay = jnp.where(diff >= 0, jnp.exp(jnp.maximum(diff, 0.0)[None] * log_gamma[:, None, None]), 0.0)
    scores = jnp.einsum('bhcnd,bhcmd->bhcnm', qc, kc) * decay[:, None]
    inner = jnp.einsum('bhcnm,bhcme->bhcne', scores, vc)
    zeta = jnp.exp((C - 1 - idx)[None, :] * log_gamma[:, None])
    xi = jnp.exp((idx + 1)[None, :] * log_gamma[:, None])
    chunk_decay = jnp.exp(C * log_gamma)

    def step(R, kv):
        kt, vt = kv
        R_new = chunk_decay[None, :, None, None] * R + jnp.einsum('bhmd,bhme->bhde', kt * zeta[None, :, :, None], vt)
        return R_new, R

    R0 = jnp.zeros((B, H, d, d), f32)
    _, R_prev = lax.scan(step, R0, (kc.transpose(2, 0, 1, 3, 4), vc.transpose(2, 0, 1, 3, 4)))
    cross = jnp.einsum('bhcnd,cbhde->bhcne', qc, R_prev) * xi[None, :, None, :, None]
    o = (inner + cross).transpose(0, 2, 3, 1, 4).reshape(B, T, H, d)
    o = rms_norm(o) * jax.nn.silu(g.astype(f32))
    return o.reshape(B, T, H * d).astype(q.dtype)

def nsa(q, kv, gates, q_gain, k_gain, cmp_pe, cmp_w1, cmp_w2, rel_bias):
    B, T, _, d = q.shape
    out_dtype = q.dtype
    q = rms_norm(q, q_gain) * d ** -0.5
    q = q.reshape(B, T, N_KV, HPG, d).transpose(0, 2, 3, 1, 4)
    kv = kv.transpose(2, 3, 0, 4, 1, 5)

    n_cmp = (T - CMP_LEN) // CMP_STRIDE + 1
    blk_idx = np.arange(n_cmp)[:, None] * CMP_STRIDE + np.arange(CMP_LEN)[None, :]

    def compress(a, j):
        blocks = a[:, :, blk_idx] + cmp_pe[j]
        flat = blocks.reshape(B, N_KV, n_cmp, CMP_LEN * d)
        return jax.nn.gelu(flat @ cmp_w1[j]) @ cmp_w2[j]

    k_cmp = rms_norm(compress(kv[0, 0], 0), k_gain[0])
    v_cmp = compress(kv[0, 1], 1)
    cmp_end = jnp.asarray(blk_idx[:, -1], jnp.int32)

    n_slc = T // SEL_BLOCK
    n_sel = min(N_SEL, n_slc)
    k_sel = rms_norm(kv[1, 0], k_gain[1]).reshape(B, N_KV, n_slc, SEL_BLOCK, d)
    v_sel = kv[1, 1].reshape(B, N_KV, n_slc, SEL_BLOCK, d)
    cs = np.arange(n_cmp)[:, None] * CMP_STRIDE
    ss = np.arange(n_slc)[None, :] * SEL_BLOCK
    overlap = np.clip(np.minimum(cs + CMP_LEN, ss + SEL_BLOCK) - np.maximum(cs, ss), 0, None) // CMP_STRIDE
    overlap = jnp.asarray(overlap, jnp.float32)

    pad = ((0, 0), (0, 0), (WINDOW, 0), (0, 0))
    k_win = jnp.pad(rms_norm(kv[2, 0], k_gain[2]), pad)
    v_win = jnp.pad(kv[2, 1], pad)

    gates_t = jax.nn.sigmoid(gates.astype(jnp.float32)).reshape(B, T, N_KV, HPG, 3).transpose(0, 2, 3, 1, 4)
    bias_tab = rel_bias.reshape(N_BUCKETS, N_KV, HPG)
    bi = jnp.arange(B)[:, None, None, None]
    gi = jnp.arange(N_KV)[None, :, None, None]
    K_SEL = n_sel * SEL_BLOCK

    def block(i):
        q0 = i * Q_BLOCK
        qb = lax.dynamic_slice_in_dim(q, q0, Q_BLOCK, axis=3)
        t = q0 + jnp.arange(Q_BLOCK, dtype=jnp.int32)

        dist_c = t[:, None] - cmp_end[None, :]
        bias_c = bias_tab[t5_bucket(dist_c)].transpose(2, 3, 0, 1)
        s_c = jnp.einsum('bghqd,bgnd->bghqn', qb, k_cmp) + bias_c
        p_c = masked_softmax(s_c, dist_c >= 0)
        o_c = jnp.einsum('bghqn,bgnd->bghqd', p_c, v_cmp)

        imp = jnp.einsum('bghqn,nj->bgqj', p_c, overlap)
        cur = (t // SEL_BLOCK)[:, None]
        j = jnp.arange(n_slc)[None, :]
        imp = jnp.where((j == 0) | (j == cur) | (j == cur - 1), BIG, imp)
        imp = jnp.where(j > cur, -BIG, imp)
        _, sel = lax.top_k(imp, n_sel)
        ks = k_sel[bi, gi, sel].reshape(B, N_KV, Q_BLOCK, K_SEL, d)
        vs = v_sel[bi, gi, sel].reshape(B, N_KV, Q_BLOCK, K_SEL, d)
        pos = sel[..., None] * SEL_BLOCK + jnp.arange(SEL_BLOCK, dtype=jnp.int32)
        dist_s = (t[None, None, :, None, None] - pos).reshape(B, N_KV, Q_BLOCK, K_SEL)
        bias_s = bias_tab[t5_bucket(dist_s), gi].transpose(0, 1, 4, 2, 3)
        s_s = jnp.einsum('bghqd,bgqkd->bghqk', qb, ks) + bias_s
        p_s = masked_softmax(s_s, (dist_s >= 0)[:, :, None])
        o_s = jnp.einsum('bghqk,bgqkd->bghqd', p_s, vs)

        kw = lax.dynamic_slice_in_dim(k_win, q0, WINDOW + Q_BLOCK, axis=2)
        vw = lax.dynamic_slice_in_dim(v_win, q0, WINDOW + Q_BLOCK, axis=2)
        s_pos = q0 - WINDOW + jnp.arange(WINDOW + Q_BLOCK, dtype=jnp.int32)
        dist_w = t[:, None] - s_pos[None, :]
        mask_w = (dist_w >= 0) & (dist_w < WINDOW) & (s_pos[None, :] >= 0)
        bias_w = bias_tab[t5_bucket(dist_w)].transpose(2, 3, 0, 1)
        s_w = jnp.einsum('bghqd,bgkd->bghqk', qb, kw) + bias_w
        p_w = masked_softmax(s_w, mask_w)
        o_w = jnp.einsum('bghqk,bgkd->bghqd', p_w, vw)

        g = lax.dynamic_slice_in_dim(gates_t, q0, Q_BLOCK, axis=3)
        return g[..., 0:1] * o_c + g[..., 1:2] * o_s + g[..., 2:3] * o_w

    out = lax.map(block, jnp.arange(T // Q_BLOCK, dtype=jnp.int32))
    return out.transpose(1, 0, 4, 2, 3, 5).reshape(B, T, N_NSA * d).astype(out_dtype)

def spatial_gating(z, ws, b):
    B, T, _ = z.shape
    nch = T // GM_CHUNK
    z = jax.nn.gelu(z)
    u, v = jnp.split(z, 2, axis=-1)
    v = rms_norm(v.reshape(B, nch, GM_CHUNK, N_GM, GM_DIM))
    causal = jnp.tril(jnp.ones((GM_CHUNK, GM_CHUNK), ws.dtype))
    sv = jnp.einsum('gts,bcsgd->bctgd', ws * causal, v) + b.T[None, None, :, :, None]
    return (u.reshape(B, nch, GM_CHUNK, N_GM, GM_DIM) * sv).reshape(B, T, GM_W)

def first_inputs(seed: int = 0) -> dict:
    key = jax.random.key(seed)
    ks = jax.random.split(key, 16)
    f32 = jnp.float32
    nrm = lambda k, shape, scale: jax.random.normal(k, shape, f32) * scale
    return {
        "x": nrm(ks[0], (BATCH, SEQ, D_MODEL), 1.0),
        "attn_norm": 1.0 + nrm(ks[1], (DEPTH, D_MODEL), 0.02),
        "w_in": nrm(ks[2], (DEPTH, D_MODEL, IN_W), D_MODEL ** -0.5),
        "w_out": nrm(ks[3], (DEPTH, MIX_W, D_MODEL), MIX_W ** -0.5),
        "nsa_q_gain": 1.0 + nrm(ks[4], (DEPTH, HEAD_DIM), 0.02),
        "nsa_k_gain": 1.0 + nrm(ks[5], (DEPTH, 3, HEAD_DIM), 0.02),
        "cmp_pe": nrm(ks[6], (DEPTH, 2, CMP_LEN, HEAD_DIM), 0.1),
        "cmp_w1": nrm(ks[7], (DEPTH, 2, CMP_LEN * HEAD_DIM, HEAD_DIM), (CMP_LEN * HEAD_DIM) ** -0.5),
        "cmp_w2": nrm(ks[8], (DEPTH, 2, HEAD_DIM, HEAD_DIM), HEAD_DIM ** -0.5),
        "gm_ws": nrm(ks[9], (DEPTH, N_GM, GM_CHUNK, GM_CHUNK), GM_CHUNK ** -0.5),
        "gm_b": 1.0 + nrm(ks[10], (DEPTH, N_GM, GM_CHUNK), 0.02),
        "ffn_norm": 1.0 + nrm(ks[11], (DEPTH, D_MODEL), 0.02),
        "w_gate_up": nrm(ks[12], (DEPTH, D_MODEL, 2 * D_FF), D_MODEL ** -0.5),
        "w_down": nrm(ks[13], (DEPTH, D_FF, D_MODEL), D_FF ** -0.5),
        "rel_bias": nrm(ks[14], (N_BUCKETS, N_NSA), 0.5),
    }

def first_block(x, attn_norm, w_in, w_out, nsa_q_gain, nsa_k_gain, cmp_pe, cmp_w1, cmp_w2,
              gm_ws, gm_b, ffn_norm, w_gate_up, w_down, rel_bias):
    B, T, _ = x.shape
    pos = jnp.arange(T, dtype=jnp.int32)
    split_points = [int(s) for s in np.cumsum(SPLIT_SIZES)[:-1]]
    for l in range(DEPTH):
        h = rms_norm(x, attn_norm[l])
        proj = h @ w_in[l]
        r_q, r_k, r_v, r_g, n_q, n_kv, n_g, gm_z = jnp.split(proj, split_points, axis=-1)
        hs = (B, T, N_RET, HEAD_DIM)
        ret_o = retention(rope(r_q.reshape(hs), pos), rope(r_k.reshape(hs), pos),
                          r_v.reshape(hs), r_g.reshape(hs))
        nsa_o = nsa(n_q.reshape(B, T, N_NSA, HEAD_DIM),
                    n_kv.reshape(B, T, 3, 2, N_KV, HEAD_DIM),
                    n_g.reshape(B, T, N_NSA, 3),
                    nsa_q_gain[l], nsa_k_gain[l], cmp_pe[l], cmp_w1[l], cmp_w2[l], rel_bias)
        gm_o = spatial_gating(gm_z, gm_ws[l], gm_b[l])
        mix = jnp.concatenate([ret_o, nsa_o.astype(ret_o.dtype), gm_o.astype(ret_o.dtype)], axis=-1)
        x = x + (mix @ w_out[l]).astype(x.dtype)
        h = rms_norm(x, ffn_norm[l])
        gate, up = jnp.split(h @ w_gate_up[l], 2, axis=-1)
        x = x + ((jax.nn.silu(gate) * up) @ w_down[l]).astype(x.dtype)
    return x


GRID_W = 64
CTX_LEN = 256
N_MIXERS = 2
N_DN_LAYERS = (DEPTH + N_MIXERS - 1) // N_MIXERS
N_DA_LAYERS = DEPTH // N_MIXERS

DN_HEADS = 8
DN_DK = 128
DN_DV = 128
DN_CONV = 5
DN_CHUNK = 64

DA_HEADS = 8
DA_DIM = 64
DA_QBLOCK = 128
ROPE_BASE = 10000.0

FFN_HIDDEN = -(-(8 * D_MODEL) // (3 * 256)) * 256

DEEPNORM_ALPHA = (2.0 * DEPTH) ** 0.25
DEEPNORM_BETA = (8.0 * DEPTH) ** -0.25
LN_EPS = 1e-5
RMS_EPS = 1e-6


def _layernorm(x, g, b):
    xf = x.astype(jnp.float32)
    mu = jnp.mean(xf, axis=-1, keepdims=True)
    var = jnp.mean(jnp.square(xf - mu), axis=-1, keepdims=True)
    return ((xf - mu) * lax.rsqrt(var + LN_EPS)).astype(x.dtype) * g + b

def _rmsnorm(x, g):
    xf = x.astype(jnp.float32)
    y = xf * lax.rsqrt(jnp.mean(jnp.square(xf), axis=-1, keepdims=True) + RMS_EPS)
    return y.astype(x.dtype) * g

def _l2norm(x):
    xf = x.astype(jnp.float32)
    return xf * lax.rsqrt(jnp.sum(jnp.square(xf), axis=-1, keepdims=True) + RMS_EPS)

def _swiglu(h, w_gate, w_up, w_down):
    return (jax.nn.silu(h @ w_gate) * (h @ w_up)) @ w_down

def _centred_dwconv(x, w):
    pad = (DN_CONV - 1) // 2
    return lax.conv_general_dilated(
        x, w[:, None, :].astype(x.dtype), window_strides=(1,), padding=[(pad, pad)],
        dimension_numbers=('NWC', 'WIO', 'NWC'), feature_group_count=x.shape[-1])

def _axial_rope(rows, dtype):
    quarter = DA_DIM // 4
    inv_freq = ROPE_BASE ** (-jnp.arange(quarter, dtype=jnp.float32) / quarter)
    row = jnp.repeat(jnp.arange(rows, dtype=jnp.float32), GRID_W)
    col = jnp.tile(jnp.arange(GRID_W, dtype=jnp.float32), rows)
    ang_r = row[:, None] * inv_freq
    ang_c = col[:, None] * inv_freq
    ang = jnp.concatenate([ang_r, ang_r, ang_c, ang_c], axis=-1)
    return jnp.cos(ang).astype(dtype), jnp.sin(ang).astype(dtype)

def _apply_rope(x, cos, sin):
    quarter = DA_DIM // 4
    half = DA_DIM // 2

    def rot_half(u):
        return jnp.concatenate([-u[..., quarter:], u[..., :quarter]], axis=-1)

    x_rot = jnp.concatenate([rot_half(x[..., :half]), rot_half(x[..., half:])], axis=-1)
    return x * cos + x_rot * sin

def _flip_seq(t, direction):
    return jnp.flip(t, axis=2) if direction == 1 else t

def _chunked_gated_delta(q, k, v, g, beta, s0):
    bsz, nh, L, _ = q.shape
    dv = v.shape[-1]
    nc = L // DN_CHUNK

    def blocks(t):
        return t.reshape(bsz, nh, nc, DN_CHUNK, *t.shape[3:])

    q, k, v, g, beta = (blocks(t) for t in (q, k, v.astype(jnp.float32), g, beta))
    G = jnp.cumsum(g, axis=-1)
    idx = jnp.arange(DN_CHUNK)
    incl = idx[:, None] >= idx[None, :]
    strict = idx[:, None] > idx[None, :]
    gamma = jnp.exp(jnp.where(incl, G[..., :, None] - G[..., None, :], -jnp.inf))
    kb = k * beta[..., None]
    a_low = jnp.where(strict, jnp.einsum('bhnid,bhnjd->bhnij', kb, k) * gamma, 0.0)
    eye = jnp.eye(DN_CHUNK, dtype=jnp.float32)
    rhs = jnp.concatenate([v * beta[..., None], kb * jnp.exp(G)[..., None]], axis=-1)
    uw = lax.linalg.triangular_solve(eye + a_low, rhs, left_side=True, lower=True, unit_diagonal=True)
    u, w = uw[..., :dv], uw[..., dv:]
    qk = jnp.einsum('bhnid,bhnjd->bhnij', q, k) * gamma
    g_last = G[..., -1]
    q_dec = q * jnp.exp(G)[..., None]
    k_dec = k * jnp.exp(g_last[..., None] - G)[..., None]

    def step(s, inp):
        u_n, w_n, qk_n, qd_n, kd_n, gl_n = inp
        v_new = u_n - jnp.einsum('bhck,bhkv->bhcv', w_n, s)
        o_n = jnp.einsum('bhck,bhkv->bhcv', qd_n, s) + jnp.einsum('bhij,bhjv->bhiv', qk_n, v_new)
        s = s * jnp.exp(gl_n)[..., None, None] + jnp.einsum('bhck,bhcv->bhkv', kd_n, v_new)
        return s, o_n

    xs = tuple(jnp.moveaxis(t, 2, 0) for t in (u, w, qk, q_dec, k_dec, g_last))
    s_final, o = lax.scan(step, s0, xs)
    o = jnp.moveaxis(o, 0, 2).reshape(bsz, nh, L, dv)
    return o, s_final

def _gated_deltanet(h_lat, h_ctx, w_in, conv_w, a_log, dt_bias, norm_g, w_out, need_ctx):
    f32 = jnp.float32
    hk = DN_HEADS * DN_DK
    hv = DN_HEADS * DN_DV
    n_qkv = 2 * hk + hv

    def project(h):
        bsz, L, _ = h.shape
        p = h @ w_in
        qkv = jax.nn.silu(_centred_dwconv(p[..., :n_qkv], conv_w))
        q = _l2norm(qkv[..., :hk].reshape(bsz, L, DN_HEADS, DN_DK)) * (DN_DK ** -0.5)
        k = _l2norm(qkv[..., hk:2 * hk].reshape(bsz, L, DN_HEADS, DN_DK))
        v = qkv[..., 2 * hk:].reshape(bsz, L, DN_HEADS, DN_DV).astype(f32)
        z = p[..., n_qkv:n_qkv + hv]
        off = n_qkv + hv
        a = p[..., off:off + 2 * DN_HEADS].reshape(bsz, L, 2, DN_HEADS).astype(f32)
        b = p[..., off + 2 * DN_HEADS:].reshape(bsz, L, 2, DN_HEADS).astype(f32)
        g = -jnp.exp(a_log.astype(f32)) * jax.nn.softplus(a + dt_bias.astype(f32))
        beta = jax.nn.sigmoid(b)
        heads = lambda t: jnp.transpose(t, (0, 2, 1, 3))
        dirs = lambda t: jnp.transpose(t, (2, 0, 3, 1))
        return heads(q), heads(k), heads(v), z, dirs(g), dirs(beta)

    qc, kc, vc, zc, gc, bc = project(h_ctx)
    ql, kl, vl, zl, gl, bl = project(h_lat)
    bsz = h_lat.shape[0]
    outs_lat, outs_ctx = [], []
    for d in range(2):
        s0 = jnp.zeros((bsz, DN_HEADS, DN_DK, DN_DV), f32)
        oc, s_ctx = _chunked_gated_delta(_flip_seq(qc, d), _flip_seq(kc, d), _flip_seq(vc, d),
                                         _flip_seq(gc[d], d), _flip_seq(bc[d], d), s0)
        ol, _ = _chunked_gated_delta(_flip_seq(ql, d), _flip_seq(kl, d), _flip_seq(vl, d),
                                     _flip_seq(gl[d], d), _flip_seq(bl[d], d), s_ctx)
        outs_ctx.append(_flip_seq(oc, d))
        outs_lat.append(_flip_seq(ol, d))

    def out(o, z):
        bsz_, _, L, _ = o.shape
        o = _rmsnorm(jnp.transpose(o, (0, 2, 1, 3)), norm_g.astype(f32))
        o = o.astype(z.dtype) * jax.nn.silu(z.reshape(bsz_, L, DN_HEADS, DN_DV))
        return o.reshape(bsz_, L, hv) @ w_out

    y_ctx = out(outs_ctx[0] + outs_ctx[1], zc) if need_ctx else None
    return out(outs_lat[0] + outs_lat[1], zl), y_ctx

def _diff_attention(h_lat, h_ctx, w_in, lam, subln_g, w_out, lambda_init, rope, need_ctx):
    f32 = jnp.float32
    hq = DA_HEADS * 2 * DA_DIM

    def project(h, use_rope):
        bsz, L, _ = h.shape
        p = h @ w_in
        q = p[..., :hq].reshape(bsz, L, DA_HEADS, 2, DA_DIM).transpose(3, 0, 2, 1, 4)
        k = p[..., hq:2 * hq].reshape(bsz, L, DA_HEADS, 2, DA_DIM).transpose(3, 0, 2, 1, 4)
        v = p[..., 2 * hq:].reshape(bsz, L, DA_HEADS, 2 * DA_DIM).transpose(0, 2, 1, 3)
        if use_rope:
            q = _apply_rope(q, rope[0], rope[1])
            k = _apply_rope(k, rope[0], rope[1])
        return q * (DA_DIM ** -0.5), k, v

    lam_f = lam.astype(f32)
    lam_val = (jnp.exp(jnp.sum(lam_f[0] * lam_f[1])) - jnp.exp(jnp.sum(lam_f[2] * lam_f[3]))
               + lambda_init)

    def attend(q, k, v):
        s = jnp.einsum('cbhqd,cbhkd->cbhqk', q, k).astype(f32)
        p = jax.nn.softmax(s, axis=-1)
        a = p[0] - lam_val * p[1]
        return jnp.einsum('bhqk,bhkv->bhqv', a, v.astype(f32))

    def out(o):
        bsz_, _, L, _ = o.shape
        o = _rmsnorm(jnp.transpose(o, (0, 2, 1, 3)), subln_g.astype(f32)) * (1.0 - lambda_init)
        return o.reshape(bsz_, L, hq).astype(h_lat.dtype) @ w_out

    qc, kc, vc = project(h_ctx, False)
    ql, kl, vl = project(h_lat, True)
    k_all = jnp.concatenate([kl, kc], axis=3)
    v_all = jnp.concatenate([vl, vc], axis=2)
    bsz, L = h_lat.shape[:2]
    nb = L // DA_QBLOCK
    qb = jnp.moveaxis(ql.reshape(2, bsz, DA_HEADS, nb, DA_QBLOCK, DA_DIM), 3, 0)
    ob = lax.map(lambda q_blk: attend(q_blk, k_all, v_all), qb)
    o_lat = jnp.moveaxis(ob, 0, 2).reshape(bsz, DA_HEADS, L, 2 * DA_DIM)
    y_ctx = out(attend(qc, kc, vc)) if need_ctx else None
    return out(o_lat), y_ctx

def second_inputs(seed: int = 0) -> dict:
    key = jax.random.key(seed)
    ks = iter(jax.random.split(key, 32))
    f32 = jnp.float32
    D = D_MODEL
    hk = DN_HEADS * DN_DK
    hv = DN_HEADS * DN_DV
    hq = DA_HEADS * 2 * DA_DIM

    def nrm(shape, scale):
        return jax.random.normal(next(ks), shape, f32) * scale

    inputs = {}
    inputs['x'] = nrm((BATCH, SEQ, D), 1.0)
    inputs['c'] = nrm((BATCH, D), 1.0)
    inputs['ctx'] = nrm((BATCH, CTX_LEN, D), 1.0)
    inputs['c_ctx'] = nrm((D,), 1.0)
    inputs['ada_w'] = nrm((DEPTH, D, 6 * D), D ** -0.5)
    inputs['ada_b'] = nrm((DEPTH, 6 * D), 0.01)
    inputs['ln1_g'] = 1.0 + nrm((DEPTH, D), 0.02)
    inputs['ln1_b'] = nrm((DEPTH, D), 0.02)
    inputs['ln2_g'] = 1.0 + nrm((DEPTH, D), 0.02)
    inputs['ln2_b'] = nrm((DEPTH, D), 0.02)
    inputs['ffn_w_gate'] = nrm((DEPTH, D, FFN_HIDDEN), D ** -0.5)
    inputs['ffn_w_up'] = nrm((DEPTH, D, FFN_HIDDEN), D ** -0.5)
    inputs['ffn_w_down'] = nrm((DEPTH, FFN_HIDDEN, D), FFN_HIDDEN ** -0.5 * DEEPNORM_BETA)
    inputs['dn_w_in'] = jnp.concatenate([
        nrm((N_DN_LAYERS, D, 2 * hk + 2 * hv), D ** -0.5),
        nrm((N_DN_LAYERS, D, 2 * DN_HEADS), 0.1 * D ** -0.5),
        nrm((N_DN_LAYERS, D, 2 * DN_HEADS), D ** -0.5),
    ], axis=-1)
    inputs['dn_conv'] = nrm((N_DN_LAYERS, DN_CONV, 2 * hk + hv), DN_CONV ** -0.5)
    inputs['dn_a_log'] = jnp.log(jax.random.uniform(next(ks), (N_DN_LAYERS, 2, DN_HEADS), f32, 1.0, 16.0))
    dt = jnp.exp(jax.random.uniform(next(ks), (N_DN_LAYERS, 2, DN_HEADS), f32,
                                    math.log(1e-3), math.log(1e-1)))
    inputs['dn_dt_bias'] = dt + jnp.log(-jnp.expm1(-dt))
    inputs['dn_norm_g'] = 1.0 + nrm((N_DN_LAYERS, DN_DV), 0.02)
    inputs['dn_w_out'] = nrm((N_DN_LAYERS, hv, D), hv ** -0.5 * DEEPNORM_BETA)
    inputs['da_w_in'] = nrm((N_DA_LAYERS, D, 3 * hq), D ** -0.5)
    inputs['da_lambda'] = nrm((N_DA_LAYERS, 4, DA_DIM), 0.1)
    inputs['da_subln_g'] = 1.0 + nrm((N_DA_LAYERS, 2 * DA_DIM), 0.02)
    inputs['da_w_out'] = nrm((N_DA_LAYERS, hq, D), hq ** -0.5 * DEEPNORM_BETA)
    return inputs

def second_block(x, c, ctx, c_ctx, ada_w, ada_b, ln1_g, ln1_b, ln2_g, ln2_b,
              ffn_w_gate, ffn_w_up, ffn_w_down,
              dn_w_in, dn_conv, dn_a_log, dn_dt_bias, dn_norm_g, dn_w_out,
              da_w_in, da_lambda, da_subln_g, da_w_out):
    L = x.shape[1]
    rows = L // GRID_W
    rope = _axial_rope(rows, x.dtype)
    s_lat = jax.nn.silu(c)
    s_ctx = jax.nn.silu(c_ctx)
    for i in range(DEPTH):
        last = i == DEPTH - 1
        sh1, sc1, gt1, sh2, sc2, gt2 = jnp.split((s_lat @ ada_w[i] + ada_b[i])[:, None, :], 6, axis=-1)
        sh1c, sc1c, gt1c, sh2c, sc2c, gt2c = jnp.split(s_ctx @ ada_w[i] + ada_b[i], 6, axis=-1)
        h = x * (1.0 + sc1) + sh1
        hc = ctx * (1.0 + sc1c) + sh1c
        j = i // N_MIXERS
        if i % N_MIXERS == 0:
            y, yc = _gated_deltanet(h, hc, dn_w_in[j], dn_conv[j], dn_a_log[j], dn_dt_bias[j],
                                    dn_norm_g[j], dn_w_out[j], not last)
        else:
            y, yc = _diff_attention(h, hc, da_w_in[j], da_lambda[j], da_subln_g[j], da_w_out[j],
                                    0.8 - 0.6 * math.exp(-0.3 * i), rope, not last)
        x = _layernorm(DEEPNORM_ALPHA * x + gt1 * y, ln1_g[i], ln1_b[i])
        x = _layernorm(DEEPNORM_ALPHA * x
                       + gt2 * _swiglu(x * (1.0 + sc2) + sh2, ffn_w_gate[i], ffn_w_up[i], ffn_w_down[i]),
                       ln2_g[i], ln2_b[i])
        if not last:
            ctx = _layernorm(DEEPNORM_ALPHA * ctx + gt1c * yc, ln1_g[i], ln1_b[i])
            ctx = _layernorm(DEEPNORM_ALPHA * ctx
                             + gt2c * _swiglu(ctx * (1.0 + sc2c) + sh2c, ffn_w_gate[i], ffn_w_up[i], ffn_w_down[i]),
                             ln2_g[i], ln2_b[i])
    return x


def setup_inputs(seed=0):
    out = dict(first_inputs(seed))
    for name, value in second_inputs(seed + 1).items():
        if name != "x":
            out[name + "_2"] = value
    return out


def reference(
    x, attn_norm, w_in, w_out, nsa_q_gain, nsa_k_gain, cmp_pe, cmp_w1, cmp_w2, gm_ws, gm_b,
    ffn_norm, w_gate_up, w_down, rel_bias, c_2, ctx_2, c_ctx_2, ada_w_2, ada_b_2, ln1_g_2,
    ln1_b_2, ln2_g_2, ln2_b_2, ffn_w_gate_2, ffn_w_up_2, ffn_w_down_2, dn_w_in_2, dn_conv_2,
    dn_a_log_2, dn_dt_bias_2, dn_norm_g_2, dn_w_out_2, da_w_in_2, da_lambda_2, da_subln_g_2,
    da_w_out_2,
):
    x = first_block(
        x, attn_norm, w_in, w_out, nsa_q_gain, nsa_k_gain, cmp_pe, cmp_w1, cmp_w2, gm_ws, gm_b,
        ffn_norm, w_gate_up, w_down, rel_bias,
    )
    return second_block(
        x, c_2, ctx_2, c_ctx_2, ada_w_2, ada_b_2, ln1_g_2, ln1_b_2, ln2_g_2, ln2_b_2,
        ffn_w_gate_2, ffn_w_up_2, ffn_w_down_2, dn_w_in_2, dn_conv_2, dn_a_log_2, dn_dt_bias_2,
        dn_norm_g_2, dn_w_out_2, da_w_in_2, da_lambda_2, da_subln_g_2, da_w_out_2,
    )


_drawn_inputs = setup_inputs


def setup_inputs(seed=0):
    import zlib

    import numpy as np

    out = dict(_drawn_inputs(seed))
    spreads = {}
    factors = {'nsa_q_gain': 8.0,
     'nsa_k_gain': 8.0,
     'gm_b': 6.254,
     'ffn_norm': 2.891,
     'ada_b_2': 6.155,
     'dn_norm_g_2': 31.318,
     'da_lambda_2': 4.493,
     'da_subln_g_2': 30.404,
     'rel_bias': 2.91}
    for name, (base, spread) in spreads.items():
        noise = np.random.default_rng([zlib.crc32(name.encode()), seed]).standard_normal(out[name].shape)
        drawn = base * np.exp(spread * noise) if base else spread * noise
        out[name] = jnp.asarray(drawn.astype(out[name].dtype))
    for name, factor in factors.items():
        out[name] = (out[name] * factor).astype(out[name].dtype)
    return out
```

```python
import math

import numpy as np

import concourse.bass as bass
from concourse import mybir
from concourse.alu_op_type import AluOpType as ALU

F32 = mybir.dt.float32
ACT = mybir.ActivationFunctionType
AX = mybir.AxisListType
P = 128
EPS = 1e-6

D = 1024
KT = D // P
SEQ = 512
CTX = 256
NT1 = SEQ // P
NT2 = (SEQ + CTX) // P
DEPTH = 2
HD = 64
N_RET = N_NSA = 6
N_CMP = (SEQ - 32) // 16 + 1
F = 2816
FT = F // P
RING = 3
SLAB = 4096
BIG = 1e30
N_SLABS1 = 27
N_SLABS2 = 76
LN_EPS = 1e-5
ALPHA = (2.0 * DEPTH) ** 0.25
HEADS = 8
HALF = 4

SM = {}
_at = 0
for _name, _n in (("attn_norm", 8), ("ffn_norm", 8), ("q_gain", 1), ("k_gain", 3), ("pe", 64),
                  ("w2k", 256), ("w2v", 64), ("ws", 512), ("gm_b", 4)):
    SM[_name] = (_at, _n)
    _at += _n
N_SM = _at

C1 = {}
_at = 0
for _name, _n in (("decay", 3072), ("cos", 512), ("sin", 512), ("causal", 128), ("rot", 128),
                  ("blk", 128), ("flip", 128), ("valid", 1)):
    C1[_name] = (_at, _n)
    _at += _n
N_C1 = _at



def table(*parts):
    out, at = {}, 0
    for name, n in parts:
        out[name] = (at, n)
        at += n
    return out, at


C2, N_C2 = table(("tri", 256), ("gmask", 256), ("imask", 256), ("b16", 128), ("level", 384), ("norm_g", 128))
DN, N_DN = table(("conv", 60), ("wab", 128), ("alog", 8), ("dt", 8))
C3, N_C3 = table(("rot", 128), ("subln", 128))

C0 = {"ident": (0, 128), "ones": (128, 128)}
N_C0 = 256


def t5_bucket(dist):
    n = np.maximum(dist, 0)
    nf = np.maximum(n, 1).astype(np.float32)
    large = 16 + (np.log(nf / np.float32(16)) / np.float32(math.log(8)) * np.float32(16)).astype(np.int32)
    return np.where(n < 16, n, np.minimum(large, 31))


class Arena:

    def __init__(self, tensor, start, end):
        self.tensor, self.at, self.end = tensor, start, end

    def take(self, *shape):
        n = int(np.prod(shape))
        start, self.at = self.at, self.at + n
        assert self.at <= self.end, (self.at, self.end)
        v = self.tensor[:, start:start + n]
        if len(shape) == 2:
            v = v.rearrange("p (a b) -> p a b", b=shape[1])
        elif len(shape) == 3:
            v = v.rearrange("p (a b c) -> p a b c", b=shape[1], c=shape[2])
        return v


class Chained:

    def __init__(self, eng, sem):
        self.eng, self.sem, self.n = eng, sem, 0

    def link(self, instruction):
        self.n += 1
        instruction.then_inc(self.sem, 1)
        self.eng.wait_ge(self.sem, self.n)


def cols(table, tile, name, *shape):
    at, n = table[name]
    v = tile[:, at:at + n]
    if len(shape) == 2:
        v = v.rearrange("p (a b) -> p a b", b=shape[1])
    return v


class Semaphores:

    def __init__(self, nc):
        sem = nc.alloc_semaphore
        self.pe_chain = sem("pe_chain")
        self.act_chain = sem("act_chain")
        self.loaded = sem("loaded")
        self.dve_chain = sem("dve_chain")
        self.pool_chain = sem("pool_chain")
        self.arrived = sem("arrived")
        self.x_loaded = sem("x_loaded")
        self.line_ready = sem("line_ready")
        self.spilled = sem("spilled")
        self.hankel_loaded = sem("hankel_loaded")
        self.line_ps = sem("line_ps")
        self.flip_taken = sem("flip_taken")
        self.flip_ps = sem("flip_ps")
        self.tr_taken_dve = sem("tr_taken_dve")
        self.tr_taken_act = sem("tr_taken_act")
        self.tr_done = sem("tr_done")
        self.normed_ready = sem("normed_ready")
        self.squares_ready = sem("squares_ready")
        self.meansq_ready = sem("meansq_ready")
        self.std_ready = sem("std_ready")
        self.mm_taken = sem("mm_taken")
        self.mm_done = sem("mm_done")
        self.ng_done = sem("ng_done")
        self.gates_ready = sem("gates_ready")
        self.nstd_ready = sem("nstd_ready")
        self.rot_taken = sem("rot_taken")
        self.sq_ready = sem("sq_ready")
        self.stat_done = sem("stat_done")
        self.tok_taken = sem("tok_taken")
        self.tok_done = sem("tok_done")
        self.head_normed = sem("head_normed")
        self.kb_ready = sem("kb_ready")
        self.hid_ps = sem("hid_ps")
        self.v_ready = sem("v_ready")
        self.sv_ps = sem("sv_ps")
        self.hid_ready = sem("hid_ready")
        self.kcv_ps = sem("kcv_ps")
        self.kc_sq = sem("kc_sq")
        self.kn_ps = sem("kn_ps")
        self.vsq_ready = sem("vsq_ready")
        self.vms_ready = sem("vms_ready")
        self.vstd_ready = sem("vstd_ready")
        self.kn_std = sem("kn_std")
        self.st_ready = sem("st_ready")
        self.o_taken = sem("o_taken")
        self.o_ps = sem("o_ps")
        self.st_ps = sem("st_ps")
        self.osq_ready = sem("osq_ready")
        self.oms_ready = sem("oms_ready")
        self.ostd_ready = sem("ostd_ready")
        self.s_ready = sem("s_ready")
        self.s_ps = sem("s_ps")
        self.p_ready = sem("p_ready")
        self.pt_ready = sem("pt_ready")
        self.pt_ps = sem("pt_ps")
        self.ov_taken = sem("ov_taken")
        self.ov_ps = sem("ov_ps")
        self.hid_taken = sem("hid_taken")
        self.gate_ps = sem("gate_ps")
        self.silu_ready = sem("silu_ready")
        self.cond_ready = sem("cond_ready")
        self.aux_taken = sem("aux_taken")
        self.aux_done = sem("aux_done")
        self.ada_b_loaded = sem("ada_b_loaded")
        self.ab_ps = sem("ab_ps")
        self.log_decay_ready = sem("log_decay_ready")
        self.prefix_ps = sem("prefix_ps")
        self.neg_abs_ready = sem("neg_abs_ready")
        self.softplus_ready = sem("softplus_ready")
        self.ab_read = sem("ab_read")
        self.prefix_ready = sem("prefix_ready")
        self.exps_ready = sem("exps_ready")
        self.qk_normed = sem("qk_normed")
        self.qkv_silu = sem("qkv_silu")
        self.padding_ready = sem("padding_ready")
        self.convolved = sem("convolved")
        self.pe_events = sem("pe_events")
        self.act_events = sem("act_events")
        self.dve_events = sem("dve_events")
        self.pool_events = sem("pool_events")
        self.head_sq_summed = sem("head_sq_summed")
        self.head_sq_ready = sem("head_sq_ready")
        self.head_ms_ready = sem("head_ms_ready")
        self.head_std_ready = sem("head_std_ready")
        self.var_ready = sem("var_ready")
        self.dev_ready = sem("dev_ready")
        self.shift_ready = sem("shift_ready")
        self.centred = sem("centred")
        self.lam_loaded = sem("lam_loaded")
        self.lam_sums_ready = sem("lam_sums_ready")
        self.lam_exps_ready = sem("lam_exps_ready")
        self.stage_range = range(self.pe_chain.num, self.lam_exps_ready.num + 1)
        self.go = {"pe": sem("go_pe"), "act": sem("go_act"), "dve": sem("go_dve")}
        self.full = [sem(f"slot_full{i}") for i in range(RING)]
        self.empty = [sem(f"slot_empty{i}") for i in range(RING)]
        self.stored = sem("stored")


class Ctx:
    pass


def build(nc, T):
    k = Ctx()
    k.nc, k.T = nc, T
    k.to_release = None
    S = Semaphores(nc)
    k.S = S
    assert len(S.stage_range) == 91

    total = 53184
    k.sb = nc.alloc_sbuf_tensor("sb", [P, total], F32)
    k.psum = nc.alloc_psum_tensor("psum", [P, 8, 512], F32)
    k.ps = k.psum[:, :, :]
    common = Arena(k.sb, 0, total)
    k.ring = [common.take(SLAB) for _ in range(RING)]
    x_at = common.at
    k.x = common.take(NT2, D)
    xt_at = common.at
    k.xT = common.take(KT, NT2 * P)
    k.c0 = common.take(N_C0)
    k.ident = cols(C0, k.c0, "ident")
    k.ones = cols(C0, k.c0, "ones")
    k.small = common.take(256)
    arena0 = common.at

    k.x1 = k.sb[:, x_at:x_at + NT1 * D].rearrange("p (a b) -> p a b", b=D)
    k.xT1 = k.sb[:, xt_at:xt_at + KT * SEQ].rearrange("p (a b) -> p a b", b=SEQ)
    k.back_x = k.sb[:, x_at + NT1 * D:x_at + NT2 * D]
    k.back_xt = k.sb[:, xt_at + KT * SEQ:xt_at + KT * NT2 * P]
    a = Arena(k.sb, arena0, total)
    k.c1 = a.take(N_C1)
    k.sm = a.take(N_SM)
    k.bias = a.take(N_NSA, 512)
    k.biasc = a.take(N_NSA, NT1, 32)
    k.gates = a.take(NT1, 18)
    k.gains = a.take(8)
    work = a.at
    k.tt = a.take(13, 512)
    k.tok = a.take(NT1, 3, 512)
    k.mix = a.take(NT1, D)
    k.tmp = a.take(total - a.at)
    b = Arena(k.sb, work, total)
    k.hid = b.take(FT, SEQ)
    k.silu = b.take(2, SEQ)
    c = Arena(k.sb, work, total)
    k.hn = c.take(NT1, D)
    k.eps = k.small[:, 255:256]
    bx, bt, tmp = k.back_x, k.back_xt, k.tmp
    k.tmpv = lambda n: bx[:, 512 * (n % 2):512 * (n % 2) + 512]
    k.stdv = lambda n: bx[:, 1024 + 512 * (n % 2):1536 + 512 * (n % 2)]
    k.rstdv, k.rotv = bt[:, 0:512], bt[:, 512:1024]
    k.kb = bx.rearrange("p (a b) -> p a b", b=512)
    k.vsq = bt[:, 0:1024].rearrange("p (t d) -> p t d", d=256)
    k.kc, k.vc = tmp[:, 0:32], tmp[:, 32:160]
    k.hidc = tmp[:, 160:288].rearrange("p (a b) -> p a b", b=32)
    k.kcsq, k.kcstd, k.kcr = tmp[:, 288:320], tmp[:, 320:352], tmp[:, 352:384]
    k.st = lambda h, j: (bx, bt)[h % 2][:, (0, 512, 896, 1152)[j]:(512, 896, 1152, 1280)[j]]
    k.osq = tmp[:, 160:1696].rearrange("p (t d) -> p t d", d=384)
    k.sneg = lambda u: bx[:, 512 * (u % 2):512 * (u % 2) + 512]
    k.pexp = lambda u: bx[:, 1024 + 512 * (u % 2):1536 + 512 * (u % 2)]
    k.ptr = lambda u: bt[:, 512 * (u % 2):512 * (u % 2) + 512]
    k.nmax, k.psums = bt[:, 1024:1096], bt[:, 1096:1168]
    k.onehot = k.tt[0:32, 0:2, :]
    k.negline = k.tt[0:6, 2:4, :]
    k.line = k.tt[0:6, 4:6, :]
    k.relb = k.tt[0:32, 6, 0:6]
    k.hankel = k.sb[:, work + 13 * 512:work + 13 * 512 + 6 * 896].rearrange("p (h c) -> p h c", c=896)
    k.flipped = k.mix[:, 0, 0:896]

    place2(k, total, arena0, x_at)

    slot = [0]

    with nc.Block() as block:
        @block.sync
        def _(sp):
            n = N_SLABS1 * DEPTH + N_SLABS2
            src = T["slabs"]
            for i in range(RING):
                sp.dma_start(k.ring[i], src[i]).then_inc(S.full[i], 16)
            with sp.Fori(1, n // RING) as turn:
                for i in range(RING):
                    sp.wait_ge(S.empty[i], 1)
                    sp.sem_clear(S.empty[i])
                    sp.dma_start(k.ring[i], src[bass.ds(turn * RING + i, 1)]
                                 .rearrange("a p n -> (a p) n")).then_inc(S.full[i], 16)
            for i in range(n % RING):
                sp.wait_ge(S.empty[i], 1)
                sp.sem_clear(S.empty[i])
                sp.dma_start(k.ring[i], src[n // RING * RING + i]).then_inc(S.full[i], 16)

        @block.tensor
        def _(pe):
            e = Chained(pe, S.pe_chain)
            slot[0] = 0
            setup_pe(k, e)
            with pe.Fori(0, DEPTH):
                slot[0] = 0
                for stage_pe in (rms_pe, in_t_pe, in_tok_pe, compress_pe, retention_pe, nsa_pe, mixt_pe,
                                 out_pe, rms_pe, ffn1_pe):
                    stage_pe(k, e, slot)
                    stage_end(k, e, "pe")
            slot[0] = 0
            second_pe(k, e, slot)

        @block.scalar
        def _(act):
            e = Chained(act, S.act_chain)
            setup_act(k, e)
            with act.Fori(0, DEPTH) as layer:
                act.dma_start(k.sm, T["small1"][bass.ds(layer, 1)].rearrange("a p n -> (a p) n")).then_inc(S.loaded, 16)
                act.wait_ge(S.loaded, 16)
                for stage_act, arg in ((rms_act, "attn_norm"), (in_t_act, None), (in_tok_act, None),
                                       (compress_act, None), (retention_act, None), (nsa_act, None),
                                       (mixt_act, None), (out_act, None), (rms_act, "ffn_norm"),
                                       (ffn1_act, None)):
                    stage_act(k, e, arg)
                    stage_end(k, e, "act")
            second_act(k, e)

        @block.vector
        def _(dve):
            e = Chained(dve, S.dve_chain)
            setup_dve(k, e)
            with dve.Fori(0, DEPTH):
                for stage_dve, arg in ((rms_dve, "attn_norm"), (in_t_dve, None), (in_tok_dve, None),
                                       (compress_dve, None), (retention_dve, None), (nsa_dve, None),
                                       (mixt_dve, None), (out_dve, None), (rms_dve, "ffn_norm"),
                                       (ffn1_dve, None)):
                    stage_dve(k, e, arg)
                    stage_end(k, e, "dve")
            second_dve(k, e)

        @block.gpsimd
        def _(pool):
            e = Chained(pool, S.pool_chain)
            setup_pool(k, e)
            with pool.Fori(0, DEPTH):
                for _ in range(10):
                    stage_end_pool(k, e)
            second_pool(k, e)


def stage_end(k, e, name):
    if name == "pe" and k.to_release is not None:
        release(k, e.eng.drain())
    e.eng.drain().then_inc(k.S.arrived, 1)
    e.eng.wait_ge(k.S.go[name], 1)
    e.eng.sem_clear(k.S.go[name])
    e.n = 0


def stage_end_pool(k, e):
    e.eng.drain()
    e.eng.wait_ge(k.S.arrived, 3)
    e.eng.sem_clear(k.S.stage_range)
    for name in ("pe", "act", "dve"):
        e.eng.sem_inc(k.S.go[name], 1)
    e.n = 0


def take_slab(k, pe, slot):
    i = slot[0] % RING
    pe.wait_ge(k.S.full[i], 16)
    pe.sem_clear(k.S.full[i])
    return k.ring[i]


def slab_used(k, slot):
    k.to_release = k.S.empty[slot[0] % RING]
    slot[0] += 1


def release(k, later):
    if k.to_release is not None:
        later.then_inc(k.to_release, 1)
        k.to_release = None


def setup_act(k, e):
    act, S, T = e.eng, k.S, k.T
    act.dma_start(k.x1, T["x"].rearrange("(t p) d -> p t d", p=P)).then_inc(S.x_loaded, 16)
    act.dma_start(k.c0, T["c0"]).then_inc(S.loaded, 16)
    act.dma_start(k.c1, T["c1"]).then_inc(S.loaded, 16)
    act.dma_start(k.onehot, T["onehot"]).then_inc(S.loaded, 16)
    act.dma_start(k.negline, T["negline"]).then_inc(S.loaded, 16)
    act.dma_start(k.relb, T["rel_bias"]).then_inc(S.loaded, 16)
    act.wait_ge(S.line_ready, 2)
    act.dma_start(T["line"].rearrange("h (a b) -> h a b", b=512), k.line).then_inc(S.spilled, 16)
    act.wait_ge(S.spilled, 16)
    line = T["line"]
    for h in range(N_NSA):
        act.dma_start(k.hankel[:, h, :], bass.AP(line.tensor, h * 1024, [[1, P], [1, 896]])).then_inc(S.hankel_loaded, 16)
    act.wait_ge(S.x_loaded, 16)
    stage_end(k, e, "act")


def setup_pe(k, e):
    pe, S = e.eng, k.S
    pe.wait_ge(S.loaded, 16 * 5)
    for i in range(2):
        pe.matmul(k.ps[0:6, i, :], k.relb, k.onehot[:, i, :], start=True, stop=True).then_inc(S.line_ps, 1)
    pe.wait_ge(S.hankel_loaded, 16 * N_NSA)
    flip = cols(C1, k.c1, "flip")
    for h in range(N_NSA):
        for i, (at, n) in enumerate(((0, 512), (512, 384))):
            job = 2 * h + i
            if job >= 4:
                pe.wait_ge(S.flip_taken, job - 3)
            pe.matmul(k.ps[:, 4 + job % 4, 0:n], flip, k.hankel[:, h, at:at + n], start=True,
                      stop=True).then_inc(S.flip_ps, 1)
    stage_end(k, e, "pe")


def setup_dve(k, e):
    dve, S = e.eng, k.S
    e.link(dve.memset(k.eps, EPS))
    for i in range(2):
        dve.wait_ge(S.line_ps, i + 1)
        dve.tensor_tensor(k.line[:, i, :], k.ps[0:6, i, :], k.negline[:, i, :], ALU.add).then_inc(S.line_ready, 1)
    for h in range(N_NSA):
        dve.wait_ge(S.flip_ps, 2 * h + 1)
        dve.tensor_copy(k.flipped[:, 0:512], k.ps[:, 4 + (2 * h) % 4, :]).then_inc(S.flip_taken, 1)
        dve.wait_ge(S.flip_ps, 2 * h + 2)
        dve.tensor_copy(k.flipped[:, 512:896], k.ps[:, 4 + (2 * h + 1) % 4, 0:384]).then_inc(S.flip_taken, 1)
        dve.wait_ge(S.flip_taken, 2 * h + 2)
        dve.tensor_copy(k.bias[:, h, :], k.flipped[:, 0:512])
        for i in range(NT1):
            at = 415 - P * i
            ins = dve.tensor_copy(k.biasc[:, h, i, 0:N_CMP], k.flipped[:, at:at + 16 * (N_CMP - 1) + 1:16])
        e.link(ins)
    stage_end(k, e, "dve")


def setup_pool(k, e):
    stage_end_pool(k, e)


def tr_jobs(nt):
    return [(kt, t0, min(4, nt - t0)) for kt in range(KT) for t0 in range(0, nt, 4)]


def transposes_pe(k, pe, src, nt):
    S = k.S
    for n, (kt, t0, m) in enumerate(tr_jobs(nt)):
        if n >= 4:
            pe.wait_ge((S.tr_taken_dve, S.tr_taken_act)[n % 2], (n - 4) // 2 + 1)
        for t in range(m):
            last = pe.transpose(k.ps[:, n % 4, t * P:(t + 1) * P], src[:, t0 + t, kt * P:(kt + 1) * P], k.ident)
        last.then_inc(S.tr_done, 1)


def transposes_take(k, e, dst, nt, which, scale=None, bias=None):
    S, eng = k.S, e.eng
    for n, (kt, t0, m) in enumerate(tr_jobs(nt)):
        if n % 2 != which:
            continue
        eng.wait_ge(S.tr_done, n + 1)
        out, src = dst[:, kt, t0 * P:(t0 + m) * P], k.ps[:, n % 4, 0:m * P]
        sc = scale(kt, t0) if scale else 1.0
        if which == 0:
            if bias:
                ins = eng.tensor_scalar(out, src, sc, bias(kt, t0), ALU.mult, ALU.add)
            else:
                ins = eng.tensor_scalar(out, src, sc, None, ALU.mult)
            ins.then_inc(S.tr_taken_dve, 1)
        else:
            if bias:
                ins = eng.activation(out, src, ACT.Identity, bias=bias(kt, t0), scale=sc)
            else:
                ins = eng.activation(out, src, ACT.Copy, scale=sc)
            ins.then_inc(S.tr_taken_act, 1)


def rms_pe(k, e, slot):
    e.eng.wait_ge(k.S.normed_ready, NT1)
    transposes_pe(k, e.eng, k.hn, NT1)


def rms_act(k, e, name):
    act, S = e.eng, k.S
    for t in range(NT1):
        act.activation(k.hn[:, t, :], k.x1[:, t, :], ACT.Square,
                       accum_out=k.small[:, t:t + 1]).then_inc(S.squares_ready, 1)
    act.wait_ge(S.meansq_ready, 1)
    act.activation(k.small[:, 12:16], k.small[:, 8:12], ACT.Sqrt).then_inc(S.std_ready, 1)
    g = cols(SM, k.sm, name)
    transposes_take(k, e, k.xT1, NT1, 1, scale=lambda kt, t0: g[:, kt:kt + 1])


def rms_dve(k, e, name):
    dve, S = e.eng, k.S
    dve.wait_ge(S.squares_ready, NT1)
    dve.tensor_scalar(k.small[:, 8:12], k.small[:, 0:4], 1.0 / D, EPS, ALU.mult, ALU.add).then_inc(S.meansq_ready, 1)
    dve.wait_ge(S.std_ready, 1)
    e.link(dve.reciprocal(k.small[:, 16:20], k.small[:, 12:16]))
    for t in range(NT1):
        dve.tensor_scalar(k.hn[:, t, :], k.x1[:, t, :], k.small[:, 16 + t:17 + t], None, ALU.mult).then_inc(S.normed_ready, 1)
    g = cols(SM, k.sm, name)
    transposes_take(k, e, k.xT1, NT1, 0, scale=lambda kt, t0: g[:, kt:kt + 1])


def in_t_pe(k, e, slot):
    pe, S = e.eng, k.S
    for g in range(13):
        if g % 4 == 0:
            w = take_slab(k, pe, slot)
        if g >= 4:
            pe.wait_ge(S.mm_taken, g - 3)
        for kt in range(KT):
            at = (g % 4) * 1024 + kt * P
            last = pe.matmul(k.ps[:, g % 4, :], w[:, at:at + P], k.xT1[:, kt, :], start=kt == 0, stop=kt == KT - 1)
            if kt == 0:
                release(k, last)
        if g % 4 == 3:
            slab_used(k, slot)
        last.then_inc(S.mm_done, 1)
    for t in range(NT1):
        for kt in range(KT):
            last = pe.matmul(k.ps[:, 4, t * 18:(t + 1) * 18], k.xT1[:, kt, t * P:(t + 1) * P],
                             w[:, 1024 + kt * 18:1024 + (kt + 1) * 18], start=kt == 0, stop=kt == KT - 1)
    slab_used(k, slot)
    last.then_inc(S.ng_done, 1)


def in_t_act(k, e, _):
    act, S = e.eng, k.S
    for g in range(13):
        act.wait_ge(S.mm_done, g + 1)
        act.activation(k.tt[:, g, :], k.ps[:, g % 4, :], ACT.Copy).then_inc(S.mm_taken, 1)
    act.wait_ge(S.ng_done, 1)
    act.activation(k.gates[:, :, :], k.ps[:, 4, 0:72].rearrange("p (t c) -> p t c", c=18), ACT.Sigmoid).then_inc(S.gates_ready, 1)


def in_t_dve(k, e, _):
    dve, S = e.eng, k.S
    dve.tensor_scalar(k.gains[:, 0:1], cols(SM, k.sm, "q_gain"), HD ** -0.5, None, ALU.mult)
    dve.tensor_copy(k.gains[:, 1:4], cols(SM, k.sm, "k_gain"))
    ws = cols(SM, k.sm, "ws", 4, P)
    mask = cols(C1, k.c1, "causal")
    for g in range(4):
        dve.tensor_tensor(ws[:, g, :], ws[:, g, :], mask, ALU.mult)
    dve.wait_ge(S.gates_ready, 1)
    for h in range(N_NSA):
        ins = dve.tensor_scalar(k.gates[:, 0, 3 * h:3 * h + 1], k.gates[:, 0, 3 * h:3 * h + 1],
                                cols(C1, k.c1, "valid"), None, ALU.mult)
    e.link(ins)


NORM_GROUPS = [(6, 0), (7, 0), (8, 0), (11, 2), (12, 3)]
N_POST = len(NORM_GROUPS) + 6


def in_tok_pe(k, e, slot):
    pe, S = e.eng, k.S
    nn = len(NORM_GROUPS)
    for n in range(12):
        if n < N_POST:
            if n >= 4:
                if n - 4 < nn:
                    pe.wait_ge(S.nstd_ready, n - 3)
                else:
                    pe.wait_ge(S.rot_taken, n - 4 - nn + 1)
            if n < nn:
                pe.wait_ge(S.sq_ready, n + 1)
                pe.matmul(k.ps[:, n % 4, :], cols(C1, k.c1, "blk"), k.tmpv(n), start=True, stop=True).then_inc(S.stat_done, 1)
            else:
                pe.matmul(k.ps[:, n % 4, :], cols(C1, k.c1, "rot"), k.tt[:, n - nn, :], start=True,
                          stop=True).then_inc(S.stat_done, 1)
        c, t = divmod(n, NT1)
        if t == 0:
            w = take_slab(k, pe, slot).rearrange("p (a b) -> p a b", b=512)
        if n >= 4:
            pe.wait_ge(S.tok_taken, n - 3)
        for kt in range(KT):
            last = pe.matmul(k.ps[:, 4 + n % 4, :], k.xT1[:, kt, t * P:(t + 1) * P], w[:, kt, :],
                             start=kt == 0, stop=kt == KT - 1)
            if kt == 0:
                release(k, last)
        if t == NT1 - 1:
            slab_used(k, slot)
        last.then_inc(S.tok_done, 1)


def in_tok_act(k, e, _):
    act, S = e.eng, k.S
    nn = len(NORM_GROUPS)

    def square(n):
        if n >= 2:
            act.wait_ge(S.stat_done, n - 1)
        act.activation(k.tmpv(n), k.tt[:, NORM_GROUPS[n][0], :], ACT.Square).then_inc(S.sq_ready, 1)

    square(0)
    for n in range(12):
        if n + 1 < nn:
            square(n + 1)
        if n < nn:
            act.wait_ge(S.stat_done, n + 1)
            if n >= 2:
                act.wait_ge(S.head_normed, n - 1)
            act.activation(k.stdv(n), k.ps[:, n % 4, :], ACT.Sqrt, bias=k.eps).then_inc(S.nstd_ready, 1)
        c, t = divmod(n, NT1)
        act.wait_ge(S.tok_done, n + 1)
        out, ps = k.tok[:, t, c, :], k.ps[:, 4 + n % 4, :]
        if c == 0:
            act.activation(out, ps, ACT.Copy).then_inc(S.tok_taken, 1)
        elif c == 1:
            act.activation(out[:, 0:384], ps[:, 0:384], ACT.Silu)
            act.activation(out[:, 384:512], ps[:, 384:512], ACT.Copy).then_inc(S.tok_taken, 1)
        else:
            act.activation(out, ps, ACT.Gelu_apprx_tanh).then_inc(S.tok_taken, 1)


def in_tok_dve(k, e, _):
    dve, S = e.eng, k.S
    nn = len(NORM_GROUPS)
    for n, (g, gain) in enumerate(NORM_GROUPS):
        dve.wait_ge(S.nstd_ready, n + 1)
        e.link(dve.reciprocal(k.rstdv, k.stdv(n)))
        dve.scalar_tensor_tensor(k.tt[:, g, :], k.tt[:, g, :], k.gains[:, gain:gain + 1], k.rstdv,
                                 ALU.mult, ALU.mult).then_inc(S.head_normed, 1)
        dve.wait_ge(S.head_normed, n + 1)
    for r in range(6):
        e.link(dve.tensor_tensor(k.rstdv, k.tt[:, r, :], cols(C1, k.c1, "cos"), ALU.mult))
        dve.wait_ge(S.stat_done, nn + r + 1)
        dve.tensor_tensor(k.rotv, k.ps[:, (nn + r) % 4, :], cols(C1, k.c1, "sin"), ALU.mult).then_inc(S.rot_taken, 1)
        dve.wait_ge(S.rot_taken, r + 1)
        e.link(dve.tensor_tensor(k.tt[:, r, :], k.rstdv, k.rotv, ALU.add))


def compress_pe(k, e, slot):
    pe, S = e.eng, k.S
    w1 = take_slab(k, pe, slot).rearrange("p (j l c) -> p j l c", l=32, c=64)
    pe.wait_ge(S.kb_ready, 4)
    for j in range(2):
        for g in range(2):
            rows = slice(64 * g, 64 * g + 64)
            for l in range(32):
                a, r = divmod(l, 16)
                rhs = k.kb[rows, 2 * j + a, :].rearrange("p (n r) -> p n r", r=16)[:, a:a + N_CMP, r]
                last = pe.matmul(k.ps[0:64, (0, 6)[g], 32 * j:32 * j + N_CMP],
                                 w1[rows, j, l, :], rhs, start=l == 0, stop=l == 31)
    slab_used(k, slot)
    last.then_inc(S.hid_ps, 1)
    ws = cols(SM, k.sm, "ws", 4, P)
    pe.wait_ge(S.v_ready, 1)
    for g in range(4):
        pe.matmul(k.ps[:, 4 + g // 2, (g % 2) * 256:(g % 2) * 256 + 256], ws[:, g, :],
                  k.tok[:, :, 2, 256 + 64 * g:320 + 64 * g], start=True, stop=True).then_inc(S.sv_ps, 1)
    pe.wait_ge(S.hid_ready, 2)
    w2k = cols(SM, k.sm, "w2k", 2, P)
    w2v = cols(SM, k.sm, "w2v")
    for g in range(2):
        pe.matmul(k.ps[:, 1, 0:N_CMP], w2k[0:64, g, :], k.hidc[0:64, g, 0:N_CMP], start=g == 0, stop=g == 1)
    for g in range(2):
        last = pe.matmul(k.ps[0:N_CMP, 2, 64 * g:64 * g + 64], k.hidc[0:64, 2 + g, 0:N_CMP], w2v[0:64, :],
                         start=True, stop=True)
    last.then_inc(S.kcv_ps, 1)
    pe.wait_ge(S.kc_sq, 1)
    pe.matmul(k.ps[:, 3, 0:N_CMP], cols(C1, k.c1, "blk"), k.kcsq[:, 0:N_CMP], start=True, stop=True).then_inc(S.kn_ps, 1)


def compress_act(k, e, _):
    act, S = e.eng, k.S
    v = k.tok[:, :, 2, 256:512]
    act.activation(k.vsq, v, ACT.Square).then_inc(S.vsq_ready, 1)
    act.wait_ge(S.vms_ready, 1)
    act.activation(k.small[:, 64:80], k.small[:, 48:64], ACT.Sqrt).then_inc(S.vstd_ready, 1)
    act.wait_ge(S.hid_ps, 1)
    for g in range(2):
        act.activation(k.hidc[0:64, g:4:2, 0:N_CMP],
                       k.ps[0:64, (0, 6)[g], 0:64].rearrange("p (a b) -> p a b", b=32)[:, :, 0:N_CMP],
                       ACT.Gelu_apprx_tanh).then_inc(S.hid_ready, 1)
    act.wait_ge(S.kcv_ps, 1)
    act.activation(k.kcsq[:, 0:N_CMP], k.ps[:, 1, 0:N_CMP], ACT.Square).then_inc(S.kc_sq, 1)
    act.activation(k.vc[0:N_CMP, :], k.ps[0:N_CMP, 2, 0:P], ACT.Copy)
    act.wait_ge(S.kn_ps, 1)
    act.activation(k.kcstd[:, 0:N_CMP], k.ps[:, 3, 0:N_CMP], ACT.Sqrt, bias=k.eps).then_inc(S.kn_std, 1)


def compress_dve(k, e, _):
    dve, S = e.eng, k.S
    pe_ = cols(SM, k.sm, "pe", 2, 32)
    for j in range(2):
        for a in range(2):
            dve.tensor_tensor(k.kb[:, 2 * j + a, :].rearrange("p (n r) -> p n r", r=16),
                              k.tt[:, 9 + j, :].rearrange("p (n r) -> p n r", r=16),
                              pe_[:, j, 16 * a:16 * a + 16].unsqueeze(1).broadcast_to([P, 32, 16]),
                              ALU.add).then_inc(S.kb_ready, 1)
    dve.wait_ge(S.vsq_ready, 1)
    e.link(dve.tensor_reduce(k.small[:, 32:48], k.vsq.rearrange("p t (g d) -> p t g d", d=64), AX.X, ALU.add))
    dve.tensor_scalar(k.small[:, 48:64], k.small[:, 32:48], 1.0 / HD, EPS, ALU.mult, ALU.add).then_inc(S.vms_ready, 1)
    dve.wait_ge(S.vstd_ready, 1)
    e.link(dve.reciprocal(k.small[:, 80:96], k.small[:, 64:80]))
    for t in range(NT1):
        v = k.tok[:, t, 2, 256:512].rearrange("p (g d) -> p g d", d=64)
        ins = dve.tensor_tensor(v, v, k.small[:, 80 + 4 * t:84 + 4 * t].unsqueeze(2).broadcast_to([P, 4, 64]), ALU.mult)
    ins.then_inc(S.v_ready, 1)
    b = cols(SM, k.sm, "gm_b")
    for g in range(4):
        dve.wait_ge(S.sv_ps, g // 2 * 2 + 2)
        dve.scalar_tensor_tensor(k.mix[:, :, 768 + 64 * g:832 + 64 * g],
                                 k.ps[:, 4 + g // 2, (g % 2) * 256:(g % 2) * 256 + 256].rearrange("p (t d) -> p t d", d=64),
                                 b[:, g:g + 1], k.tok[:, :, 2, 64 * g:64 * g + 64], ALU.add, ALU.mult)
    dve.wait_ge(S.kn_std, 1)
    e.link(dve.reciprocal(k.kcr[:, 0:N_CMP], k.kcstd[:, 0:N_CMP]))
    e.link(dve.scalar_tensor_tensor(k.kc[:, 0:N_CMP], k.ps[:, 1, 0:N_CMP], k.gains[:, 1:2], k.kcr[:, 0:N_CMP],
                                    ALU.mult, ALU.mult))


def retention_pe(k, e, slot):
    pe, S = e.eng, k.S

    def values(h):
        pe.wait_ge(S.st_ready, 4 * (h + 1))
        if h >= 2:
            pe.wait_ge(S.o_taken, h - 1)
        for i in range(NT1):
            for j in range(i + 1):
                last = pe.matmul(k.ps[:, 4 + h % 2, 64 * i:64 * i + 64], k.st(h, j)[:, (i - j) * P:(i - j + 1) * P],
                                 k.tok[:, j, 0, 64 * h:64 * h + 64], start=j == 0, stop=j == i)
        last.then_inc(S.o_ps, 1)

    for h in range(N_RET):
        rows = slice(64 * (h % 2), 64 * (h % 2) + 64)
        for j in range(NT1):
            n = 4 * h + j
            if n >= 4:
                pe.wait_ge(S.st_ready, n - 3)
            pe.matmul(k.ps[:, n % 4, 0:(4 - j) * P], k.tt[rows, 3 + h // 2, j * P:(j + 1) * P],
                      k.tt[rows, h // 2, j * P:SEQ], start=True, stop=True).then_inc(S.st_ps, 1)
        if h:
            values(h - 1)
    values(N_RET - 1)


def retention_act(k, e, _):
    act, S = e.eng, k.S
    for h in range(N_RET):
        act.wait_ge(S.o_ps, h + 1)
        act.activation(k.mix[:, :, 64 * h:64 * h + 64], k.ps[:, 4 + h % 2, 0:256].rearrange("p (t d) -> p t d", d=64),
                       ACT.Copy).then_inc(S.o_taken, 1)
    act.wait_ge(S.o_taken, N_RET)
    act.activation(k.osq, k.mix[:, :, 0:384], ACT.Square).then_inc(S.osq_ready, 1)
    act.wait_ge(S.oms_ready, 1)
    act.activation(k.small[:, 80:104], k.small[:, 56:80], ACT.Sqrt).then_inc(S.ostd_ready, 1)


def retention_dve(k, e, _):
    dve, S = e.eng, k.S
    decay = cols(C1, k.c1, "decay", 6, 512)
    for h in range(N_RET):
        for j in range(NT1):
            n = 4 * h + j
            dve.wait_ge(S.st_ps, n + 1)
            if h >= 2 and j == 0:
                dve.wait_ge(S.o_ps, h - 1)
            m = (4 - j) * P
            dve.tensor_tensor(k.st(h, j)[:, 0:m], k.ps[:, n % 4, 0:m], decay[:, h, 0:m], ALU.mult).then_inc(S.st_ready, 1)
    dve.wait_ge(S.osq_ready, 1)
    e.link(dve.tensor_reduce(k.small[:, 32:56], k.osq.rearrange("p t (h d) -> p t h d", d=64), AX.X, ALU.add))
    dve.tensor_scalar(k.small[:, 56:80], k.small[:, 32:56], 1.0 / HD, EPS, ALU.mult, ALU.add).then_inc(S.oms_ready, 1)
    dve.wait_ge(S.ostd_ready, 1)
    e.link(dve.reciprocal(k.small[:, 104:128], k.small[:, 80:104]))
    for t in range(NT1):
        o = k.mix[:, t, 0:384].rearrange("p (h d) -> p h d", d=64)
        e.link(dve.tensor_tensor(o, o, k.small[:, 104 + 6 * t:110 + 6 * t].unsqueeze(2).broadcast_to([P, 6, 64]), ALU.mult))
        dve.tensor_tensor(k.mix[:, t, 0:384], k.mix[:, t, 0:384], k.tok[:, t, 1, 0:384], ALU.mult)


UNITS = [(h, i, br) for h in range(N_NSA) for i in range(NT1) for br in range(3)]


def unit_keys(u):
    h, i, br = UNITS[u]
    return N_CMP if br == 0 else (i + 1) * P


def nsa_pe(k, e, slot):
    pe, S = e.eng, k.S
    n = len(UNITS)
    for u in range(n + 2):
        if u < n:
            h, i, br = UNITS[u]
            rows = slice(64 * (h // 3), 64 * (h // 3) + 64)
            if u >= 3:
                pe.wait_ge(S.s_ready, u - 2)
            keys = k.kc[rows, 0:N_CMP] if br == 0 else k.tt[rows, 10 + br, 0:(i + 1) * P]
            pe.matmul(k.ps[:, u % 3, 0:unit_keys(u)], k.tt[rows, 6 + h % 3, i * P:(i + 1) * P], keys,
                      start=True, stop=True).then_inc(S.s_ps, 1)
        if 1 <= u <= n:
            v = u - 1
            pe.wait_ge(S.p_ready, v + 1)
            if v >= 2:
                pe.wait_ge(S.pt_ready, v - 1)
            nk = unit_keys(v)
            for j in range(0, nk, P):
                m = min(P, nk - j)
                last = pe.transpose(k.ps[0:m, 3 + v % 2, j:j + P], k.pexp(v)[:, j:j + m], k.ident)
            last.then_inc(S.pt_ps, 1)
        if u >= 2:
            v = u - 2
            h, i, br = UNITS[v]
            pe.wait_ge(S.pt_ready, v + 1)
            if v >= 2:
                pe.wait_ge(S.ov_taken, v - 1)
            out = k.ps[:, 5 + v % 2, 0:64]
            g = h // 3
            if br == 0:
                last = pe.matmul(out, k.ptr(v)[0:N_CMP, 0:P], k.vc[0:N_CMP, 64 * g:64 * g + 64], start=True, stop=True)
            else:
                for j in range(i + 1):
                    last = pe.matmul(out, k.ptr(v)[:, j * P:(j + 1) * P],
                                     k.tok[:, j, br - 1, 384 + 64 * g:448 + 64 * g], start=j == 0, stop=j == i)
            last.then_inc(S.ov_ps, 1)


def nsa_act(k, e, _):
    act, S = e.eng, k.S
    n = len(UNITS)
    for u in range(n + 1):
        if u < n:
            nk = unit_keys(u)
            act.wait_ge(S.s_ready, u + 1)
            if u >= 2:
                act.wait_ge(S.pt_ps, u - 1)
            act.activation(k.pexp(u)[:, 0:nk], k.sneg(u)[:, 0:nk], ACT.Exp, bias=k.nmax[:, u:u + 1], scale=-1.0,
                           accum_out=k.psums[:, u:u + 1]).then_inc(S.p_ready, 1)
        if u >= 1:
            v = u - 1
            nk = unit_keys(v)
            act.wait_ge(S.pt_ps, v + 1)
            if v >= 2:
                act.wait_ge(S.ov_ps, v - 1)
            if nk == N_CMP:
                act.activation(k.ptr(v)[0:N_CMP, 0:P], k.ps[0:N_CMP, 3 + v % 2, 0:P], ACT.Copy).then_inc(S.pt_ready, 1)
            else:
                act.activation(k.ptr(v)[:, 0:nk], k.ps[:, 3 + v % 2, 0:nk], ACT.Copy).then_inc(S.pt_ready, 1)


def nsa_dve(k, e, _):
    dve, S = e.eng, k.S
    n = len(UNITS)
    for u in range(n + 2):
        if u < n:
            h, i, br = UNITS[u]
            nk = unit_keys(u)
            dve.wait_ge(S.s_ps, u + 1)
            if u >= 2:
                dve.wait_ge(S.p_ready, u - 1)
            bias = k.biasc[:, h, i, 0:N_CMP] if br == 0 else k.bias[:, h, 512 - nk:512]
            dve.tensor_tensor_reduce(out=k.sneg(u)[:, 0:nk], in0=k.ps[:, u % 3, 0:nk], in1=bias, scale=-1.0,
                                     scalar=3e38, op0=ALU.add, op1=ALU.min, accum_out=k.nmax[:, u:u + 1]).then_inc(S.s_ready, 1)
        if u >= 2:
            v = u - 2
            h, i, br = UNITS[v]
            dve.wait_ge(S.p_ready, v + 1)
            w = k.small[:, 32 + v % 8:33 + v % 8]
            e.link(dve.reciprocal(w, k.psums[:, v:v + 1]))
            e.link(dve.tensor_tensor(w, w, k.gates[:, i, 3 * h + br:3 * h + br + 1], ALU.mult))
            dve.wait_ge(S.ov_ps, v + 1)
            o = k.mix[:, i, 384 + 64 * h:448 + 64 * h]
            ps = k.ps[:, 5 + v % 2, 0:64]
            if br == 0:
                ins = dve.tensor_scalar(o, ps, w, None, ALU.mult)
            else:
                ins = dve.scalar_tensor_tensor(o, ps, w, o, ALU.mult, ALU.add)
            ins.then_inc(S.ov_taken, 1)
            dve.wait_ge(S.ov_taken, v + 1)


def mixt_pe(k, e, slot):
    transposes_pe(k, e.eng, k.mix, NT1)


def mixt_act(k, e, _):
    transposes_take(k, e, k.xT1, NT1, 1)


def mixt_dve(k, e, _):
    transposes_take(k, e, k.xT1, NT1, 0)


def rows_pe(k, e, slot, xT, nt, chunks):
    pe, S = e.eng, k.S
    for c in range(chunks):
        w = take_slab(k, pe, slot).rearrange("p (a b) -> p a b", b=512)
        for t in range(nt):
            n = c * nt + t
            if n >= 8:
                pe.wait_ge(S.mm_taken, n - 7)
            for kt in range(KT):
                last = pe.matmul(k.ps[:, n % 8, :], xT[:, kt, t * P:(t + 1) * P], w[:, kt, :],
                                 start=kt == 0, stop=kt == KT - 1)
                if kt == 0:
                    release(k, last)
            if t == nt - 1:
                slab_used(k, slot)
            last.then_inc(S.mm_done, 1)


def out_pe(k, e, slot):
    rows_pe(k, e, slot, k.xT1, NT1, 2)


def out_act(k, e, _):
    pass


def out_dve(k, e, _):
    dve, S = e.eng, k.S
    for n in range(2 * NT1):
        c, t = divmod(n, NT1)
        dve.wait_ge(S.mm_done, n + 1)
        xs = k.x1[:, t, 512 * c:512 * c + 512]
        dve.tensor_tensor(xs, k.ps[:, n % 8, :], xs, ALU.add).then_inc(S.mm_taken, 1)


def ffn_pe(k, e, slot, xT, hid, nt):
    pe, S = e.eng, k.S
    segs = [(0, 512)] + ([(512, 256)] if nt > 4 else [])
    for f in range(FT):
        if f % 2 == 0:
            w = take_slab(k, pe, slot)
        base = 2048 * (f % 2)
        if f >= 2:
            pe.wait_ge(S.hid_taken, f - 1)
        b = 3 * (f % 2)
        for s, (at, n) in enumerate(segs):
            for half in range(2):
                out = k.ps[:, b + half, :] if s == 0 else k.ps[:, b + 2, 256 * half:256 * half + 256]
                for kt in range(KT):
                    c = base + 1024 * half + kt * P
                    last = pe.matmul(out, w[:, c:c + P], xT[:, kt, at:at + n], start=kt == 0, stop=kt == KT - 1)
                    if kt == 0:
                        release(k, last)
        if f % 2 == 1:
            slab_used(k, slot)
        last.then_inc(S.gate_ps, 1)
    pe.wait_ge(S.hid_taken, FT)
    for c in range(2):
        for part, (f0, nf) in enumerate(((0, 8), (8, 8), (16, 6))):
            w = take_slab(k, pe, slot).rearrange("p (a b) -> p a b", b=512)
            for t in range(nt):
                n = c * nt + t
                if n >= 8 and part == 0:
                    pe.wait_ge(S.mm_taken, n - 7)
                for f in range(nf):
                    last = pe.matmul(k.ps[:, n % 8, :], hid[:, f0 + f, t * P:(t + 1) * P], w[:, f, :],
                                     start=part == 0 and f == 0, stop=part == 2 and f == nf - 1)
                    if f == 0:
                        release(k, last)
                if t == nt - 1:
                    slab_used(k, slot)
                if part == 2:
                    last.then_inc(S.mm_done, 1)


def ffn_act(k, e, silu, nt):
    act, S = e.eng, k.S
    for f in range(FT):
        act.wait_ge(S.gate_ps, f + 1)
        if f >= 2:
            act.wait_ge(S.hid_taken, f - 1)
        b = 3 * (f % 2)
        ins = act.activation(silu[:, f % 2, 0:512], k.ps[:, b, :], ACT.Silu)
        if nt > 4:
            ins = act.activation(silu[:, f % 2, 512:768], k.ps[:, b + 2, 0:256], ACT.Silu)
        ins.then_inc(S.silu_ready, 1)


def ffn_dve(k, e, silu, hid, nt):
    dve, S = e.eng, k.S
    for f in range(FT):
        dve.wait_ge(S.silu_ready, f + 1)
        b = 3 * (f % 2)
        ins = dve.tensor_tensor(hid[:, f, 0:512], k.ps[:, b + 1, :], silu[:, f % 2, 0:512], ALU.mult)
        if nt > 4:
            ins = dve.tensor_tensor(hid[:, f, 512:768], k.ps[:, b + 2, 256:512], silu[:, f % 2, 512:768], ALU.mult)
        ins.then_inc(S.hid_taken, 1)


def ffn1_pe(k, e, slot):
    ffn_pe(k, e, slot, k.xT1, k.hid, NT1)


def ffn1_act(k, e, _):
    ffn_act(k, e, k.silu, NT1)


def ffn1_dve(k, e, _):
    ffn_dve(k, e, k.silu, k.hid, NT1)
    out_dve(k, e, _)



def place2(k, total, arena0, x_at):
    a = Arena(k.sb, arena0, total)
    k.modcol = a.take(4, KT, 2)
    k.rt = a.take(2, 512)
    k.c2 = a.take(N_C2)
    k.gt = a.take(4, D)
    work = a.at
    a = Arena(k.sb, work, total)
    k.mods = a.take(6 * D)
    k.adab = a.take(6 * D)
    k.cc = a.take(KT, 2)
    k.cs = a.take(KT, 2)
    k.sel = a.take(2, P)
    a = Arena(k.sb, work - 4 * D, total)
    k.qT, k.kT = a.take(HALF, NT2 * P), a.take(HALF, NT2 * P)
    k.kc_, k.vc_ = a.take(NT2, HALF, P), a.take(NT2, HALF, P)
    k.oacc = a.take(NT2, HALF, P)
    k.dn = a.take(N_DN)
    k.stat = a.take(12, NT2 * 8)
    k.state = [a.take(HALF, P) for _ in range(2)]
    left = a.at
    b = Arena(k.sb, x_at, x_at + NT2 * D)
    k.raw = [b.take(776) for _ in range(2)]
    k.conv = [b.take(768) for _ in range(2)]
    k.sqr = [b.take(768) for _ in range(2)]
    b2 = Arena(k.sb, left, total)
    k.nstd = [b2.take(768) for _ in range(2)]
    k.vT = [b2.take(768) for _ in range(2)]
    b = Arena(k.sb, x_at, x_at + NT2 * D)
    b2 = Arena(k.sb, left, total)
    names = "low qg up a1 a2 b1 b2 x t".split()
    k.buf = [{}, {}]
    for d in range(2):
        for n in names:
            k.buf[d][n] = (b if b.at + 512 <= b.end else b2).take(HALF, P)
    a = Arena(k.sb, work, total)
    k.z = a.take(NT2, D)
    k.omix = a.take(NT2, D)
    k.osq2 = a.take(2, D)
    a = Arena(k.sb, work, total)
    k.hid2 = a.take(FT, NT2 * P)
    k.silu2 = a.take(2, NT2 * P)
    k.lnrow = a.take(2, D)
    a = Arena(k.sb, work, total)
    k.aq = a.take(HEADS, SEQ)
    k.ak = a.take(HEADS, NT2 * P)
    k.av = a.take(NT2, D)
    k.amix = a.take(NT1, D)
    k.c3 = a.take(N_C3)
    k.rotary = k.x[:, 5, :].rearrange("p (a b) -> p a b", b=512)
    k.ra = k.x[:, 4, 0:512]
    k.rb = k.x[:, 4, 512:1024]
    flat = k.xT.rearrange("p a b -> p (a b)")
    k.ap = [flat[:, 1536 * i:1536 * i + 1536].rearrange("p (c n) -> p c n", n=768) for i in range(2)]
    k.apt = [flat[:, 3072 + 768 * i:3840 + 768 * i] for i in range(2)]
    k.amax, k.asum, k.arec = flat[:, 4608:4672], flat[:, 4672:4736], flat[:, 4736:4800]
    k.amx2, k.afac = flat[:, 4800:4864], flat[:, 4864:4928]
    k.lamt = k.sb[:, a.at:a.at + 140]


LAMBDA_INIT = 0.8 - 0.6 * math.exp(-0.3 * 1)


def ada_pe(k, e, slot, _):
    pe, S = e.eng, k.S
    pe.wait_ge(S.cond_ready, 1)
    for c in range(12):
        w = take_slab(k, pe, slot).rearrange("p (a b) -> p a b", b=512)
        if c >= 4:
            pe.wait_ge(S.mm_taken, c - 3)
        for kt in range(KT):
            last = pe.matmul(k.ps[0:2, c % 4, :], k.cs[:, kt, :], w[:, kt, :], start=kt == 0, stop=kt == KT - 1)
            if kt == 0:
                release(k, last)
        slab_used(k, slot)
        last.then_inc(S.mm_done, 1)
    pe.wait_ge(S.mm_taken, 12)
    for i, w in enumerate((0, 1, 3, 4)):
        for kt in range(KT):
            at = w * D + kt * P
            last = pe.transpose(k.ps[:, 4, (i * KT + kt) * 2:(i * KT + kt) * 2 + 2], k.mods[0:2, at:at + P],
                                k.ident[0:2, 0:2])
    last.then_inc(S.tr_done, 1)
    for n in range(8):
        w, src, half = (2, 5)[n // 4], n // 2 % 2, n % 2
        if n >= 3:
            pe.wait_ge(S.aux_taken, n - 2)
        at = w * D + 512 * half
        pe.matmul(k.ps[:, 5 + n % 3, :], k.sel[0:2, src, :], k.mods[0:2, at:at + 512], start=True,
                  stop=True).then_inc(S.aux_done, 1)


def ada_act(k, e, layer):
    act, S, T = e.eng, k.S, k.T
    act.dma_start(k.cc, T["cond"]).then_inc(S.loaded, 16)
    act.dma_start(k.adab[0:2, :], T["ada_b"][layer]).then_inc(S.ada_b_loaded, 16)
    act.dma_start(k.sel[0:2, :, :], T["sel"]).then_inc(S.loaded, 16)
    if layer == 0:
        act.dma_start(k.x[:, 4:6, :], T["ctx"].rearrange("(t p) d -> p t d", p=P)).then_inc(S.loaded, 16)
        act.dma_start(k.c2, T["c2"]).then_inc(S.loaded, 16)
    act.wait_ge(S.loaded, 64 if layer == 0 else 32)
    act.activation(k.cs, k.cc, ACT.Silu).then_inc(S.cond_ready, 1)
    for n in range(8):
        act.wait_ge(S.aux_done, n + 1)
        act.activation(k.gt[:, n // 2, 512 * (n % 2):512 * (n % 2) + 512], k.ps[:, 5 + n % 3, :],
                       ACT.Copy).then_inc(S.aux_taken, 1)


def ada_dve(k, e, _):
    dve, S = e.eng, k.S
    dve.wait_ge(S.ada_b_loaded, 16)
    for c in range(12):
        dve.wait_ge(S.mm_done, c + 1)
        dve.tensor_tensor(k.mods[0:2, 512 * c:512 * c + 512], k.ps[0:2, c % 4, :],
                          k.adab[0:2, 512 * c:512 * c + 512], ALU.add).then_inc(S.mm_taken, 1)
    dve.wait_ge(S.tr_done, 1)
    cols_ = k.ps[:, 4, 0:64].rearrange("p (w a b) -> p w a b", a=KT, b=2)
    for i in range(4):
        dve.tensor_scalar(k.modcol[:, i, :, :], cols_[:, i, :, :], float(i % 2), None, ALU.add)


def modt_pe(k, e, slot, arg):
    which, nt = arg
    transposes_pe(k, e.eng, k.x, nt)


def modt_take(k, e, arg, turn):
    which, nt = arg
    transposes_take(k, e, k.xT, nt, turn,
                    scale=lambda kt, t0: k.modcol[:, 2 * which + 1, kt, t0 // 4:t0 // 4 + 1],
                    bias=lambda kt, t0: k.modcol[:, 2 * which, kt, t0 // 4:t0 // 4 + 1])


def modt_act(k, e, arg):
    modt_take(k, e, arg, 1)


def modt_dve(k, e, arg):
    modt_take(k, e, arg, 0)


def nothing_pe(k, e, slot, _):
    pass


def nothing(k, e, _):
    pass


def park_act(k, e, _):
    act, S, T = e.eng, k.S, k.T
    act.dma_start(T["x_park"], k.x).then_inc(S.spilled, 16)
    act.dma_start(T["gt_park"], k.gt).then_inc(S.spilled, 16)
    act.wait_ge(S.spilled, 32)


def fetch_act(k, e, _):
    act, S, T = e.eng, k.S, k.T
    act.dma_start(k.x, T["x_park"]).then_inc(S.loaded, 16)
    act.dma_start(k.gt, T["gt_park"]).then_inc(S.loaded, 16)
    act.dma_start(k.omix.rearrange("p t (h n) -> p t h n", h=2), T["o_park"].rearrange("h p t n -> p t h n")).then_inc(S.loaded, 16)
    act.wait_ge(S.loaded, 48)


G_, BETA, PRE, TOT, EPRE, ETOT, NBE, EKD, NBETA, TA, TB, TC = range(12)


def st_(k, i):
    return k.stat[:, i, :].rearrange("p (t c) -> p t c", c=8)


def gates_pe(k, e, slot, _):
    pe, S = e.eng, k.S
    pe.wait_ge(S.loaded, 16)
    wab = cols(DN, k.dn, "wab", KT, 16)
    for t in range(NT2):
        for kt in range(KT):
            last = pe.matmul(k.ps[:, 0, t * 16:t * 16 + 16], k.xT[:, kt, t * P:(t + 1) * P], wab[:, kt, :],
                             start=kt == 0, stop=kt == KT - 1)
    last.then_inc(S.ab_ps, 1)
    pe.wait_ge(S.log_decay_ready, 1)
    g = st_(k, G_)
    for d in range(2):
        pe.matmul(k.ps[:, 1, 24 * d:24 * d + 24], cols(C2, k.c2, "tri", 2, P)[:, d, :], g[:, :, 4 * d:4 * d + 4],
                  start=True, stop=True)
    pe.matmul(k.ps[:, 1, 48:96], k.ones, g[:, :, :], start=True, stop=True).then_inc(S.prefix_ps, 1)


def gates_act(k, e, _):
    act, S = e.eng, k.S
    half = k.half
    act.dma_start(k.dn, k.T["dn"][bass.ds(half, 1)].rearrange("a p n -> (a p) n")).then_inc(S.loaded, 16)
    act.wait_ge(S.loaded, 16)
    e.link(act.activation(k.small[:, 0:8], cols(DN, k.dn, "alog"), ACT.Exp))
    act.wait_ge(S.neg_abs_ready, 1)
    e.link(act.activation(k.stat[:, TB, :], k.stat[:, TB, :], ACT.Exp))
    act.activation(k.stat[:, TB, :], k.stat[:, TB, :], ACT.Ln, bias=k.ones[:, 0:1]).then_inc(S.softplus_ready, 1)
    act.wait_ge(S.ab_read, 1)
    act.activation(st_(k, BETA), k.ps[:, 0, 0:96].rearrange("p (t c) -> p t c", c=16)[:, :, 8:16],
                   ACT.Sigmoid).then_inc(S.softplus_ready, 1)
    act.wait_ge(S.prefix_ready, 1)
    act.activation(k.stat[:, EPRE, :], k.stat[:, PRE, :], ACT.Exp)
    act.activation(k.stat[:, ETOT, :], k.stat[:, TOT, :], ACT.Exp)
    act.activation(k.stat[:, EKD, :], k.stat[:, TA, :], ACT.Exp).then_inc(S.exps_ready, 1)


def gates_dve(k, e, _):
    dve, S = e.eng, k.S
    dve.wait_ge(S.loaded, 16)
    dve.wait_ge(S.ab_ps, 1)
    y = st_(k, TA)
    dt = cols(DN, k.dn, "dt").unsqueeze(1).broadcast_to([P, NT2, 8])
    ins = dve.tensor_tensor(y, k.ps[:, 0, 0:96].rearrange("p (t c) -> p t c", c=16)[:, :, 0:8], dt, ALU.add)
    ins.then_inc(S.ab_read, 1)
    dve.wait_ge(S.ab_read, 1)
    e.link(dve.tensor_scalar(k.stat[:, TC, :], k.stat[:, TA, :], -1.0, None, ALU.mult))
    dve.tensor_tensor(k.stat[:, TB, :], k.stat[:, TC, :], k.stat[:, TA, :], ALU.min).then_inc(S.neg_abs_ready, 1)
    dve.wait_ge(S.softplus_ready, 1)
    e.link(dve.scalar_tensor_tensor(k.stat[:, TC, :], k.stat[:, TA, :], 0.0, k.stat[:, TB, :], ALU.max, ALU.add))
    e.link(dve.tensor_scalar(k.stat[:, TC, :], k.stat[:, TC, :], -1.0, None, ALU.mult))
    dve.tensor_tensor(st_(k, G_), st_(k, TC), k.small[:, 0:8].unsqueeze(1).broadcast_to([P, NT2, 8]),
                      ALU.mult).then_inc(S.log_decay_ready, 1)
    dve.wait_ge(S.prefix_ps, 1)
    for d in range(2):
        e.link(dve.tensor_copy(st_(k, PRE)[:, :, 4 * d:4 * d + 4],
                               k.ps[:, 1, 24 * d:24 * d + 24].rearrange("p (t c) -> p t c", c=4)))
    e.link(dve.tensor_copy(k.stat[:, TOT, :], k.ps[:, 1, 48:96]))
    dve.tensor_tensor(k.stat[:, TA, :], k.stat[:, TOT, :], k.stat[:, PRE, :], ALU.subtract).then_inc(S.prefix_ready, 1)
    dve.wait_ge(S.softplus_ready, 2)
    e.link(dve.tensor_scalar(k.stat[:, NBETA, :], k.stat[:, BETA, :], -1.0, None, ALU.mult))
    dve.wait_ge(S.exps_ready, 1)
    dve.tensor_tensor(k.stat[:, NBE, :], k.stat[:, NBETA, :], k.stat[:, EPRE, :], ALU.mult)


N_QKV = 3 * HALF
SEGS = ((0, 512, 0), (512, 256, 516))


def qkv_dst(k, n):
    return (k.qT[:, n, :] if n < 4 else k.kT[:, n - 4, :]) if n < 8 else k.vT[n % 2]


def qkv_pe(k, e, slot, _):
    pe, S = e.eng, k.S
    for n in range(N_QKV + 2):
        if n < N_QKV:
            if n % 4 == 0:
                w = take_slab(k, pe, slot).rearrange("p (a b) -> p a b", b=512)
            if n >= 2:
                pe.wait_ge(S.mm_taken, n - 1)
            for s, (at, m, _) in enumerate(SEGS):
                for kt in range(KT):
                    last = pe.matmul(k.ps[:, 2 * (n % 2) + s, 0:m], w[:, kt, (n % 4) * P:(n % 4) * P + P],
                                     k.xT[:, kt, at:at + m], start=kt == 0, stop=kt == KT - 1)
                    if s == 0 and kt == 0:
                        release(k, last)
            if n % 4 == 3:
                slab_used(k, slot)
            last.then_inc(S.mm_done, 1)
        if 1 <= n <= 8:
            v = n - 1
            pe.wait_ge(S.sq_ready, v + 1)
            if v >= 1:
                pe.wait_ge(S.nstd_ready, v)
            for s, (at, m, _) in enumerate(SEGS):
                last = pe.matmul(k.ps[:, 4 + s, 0:m], k.ones, k.sqr[v % 2][:, at:at + m], start=True, stop=True)
            last.then_inc(S.stat_done, 1)
        if n >= 6:
            v = n - 2
            pe.wait_ge(S.qk_normed if v < 8 else S.qkv_silu, v + 1)
            if v >= 5:
                pe.wait_ge(S.tr_taken_act, v - 4)
            for t in range(NT2):
                last = pe.transpose(k.ps[:, 6 + t // 4, (t % 4) * P:(t % 4) * P + P],
                                    qkv_dst(k, v)[:, t * P:(t + 1) * P], k.ident)
            last.then_inc(S.tr_done, 1)


def qkv_act(k, e, _):
    act, S = e.eng, k.S
    act.wait_ge(S.padding_ready, 2)
    for n in range(N_QKV + 3):
        if n < N_QKV:
            act.wait_ge(S.mm_done, n + 1)
            if n >= 2:
                act.wait_ge(S.convolved, n - 1)
            for s, (at, m, to) in enumerate(SEGS):
                last = act.activation(k.raw[n % 2][:, to + 2:to + 2 + m], k.ps[:, 2 * (n % 2) + s, 0:m], ACT.Copy)
            last.then_inc(S.mm_taken, 1)
        if 1 <= n <= N_QKV:
            v = n - 1
            act.wait_ge(S.convolved, v + 1)
            if v >= 10:
                act.wait_ge(S.tr_done, v - 5)
            act.activation(qkv_dst(k, v), k.conv[v % 2], ACT.Silu).then_inc(S.qkv_silu, 1)
            if v < 8:
                act.wait_ge(S.qkv_silu, v + 1)
                if v >= 2:
                    act.wait_ge(S.stat_done, v - 1)
                act.activation(k.sqr[v % 2], qkv_dst(k, v), ACT.Square).then_inc(S.sq_ready, 1)
        if 2 <= n <= 9:
            v = n - 2
            act.wait_ge(S.stat_done, v + 1)
            if v >= 2:
                act.wait_ge(S.qk_normed, v - 1)
            for s, (at, m, _) in enumerate(SEGS):
                last = act.activation(k.nstd[v % 2][:, at:at + m], k.ps[:, 4 + s, 0:m], ACT.Sqrt, bias=k.eps)
            last.then_inc(S.nstd_ready, 1)
        if n >= 7:
            v = n - 3
            dst = k.kc_ if v < 8 else k.vc_
            act.wait_ge(S.tr_done, v - 3)
            act.activation(dst[:, 0:4, v % 4, :], k.ps[:, 6, :].rearrange("p (t c) -> p t c", c=P), ACT.Copy)
            act.activation(dst[:, 4:6, v % 4, :], k.ps[:, 7, 0:256].rearrange("p (t c) -> p t c", c=P),
                           ACT.Copy).then_inc(S.tr_taken_act, 1)


def qkv_dve(k, e, _):
    dve, S = e.eng, k.S
    for i in range(2):
        dve.memset(k.raw[i], 0.0).then_inc(S.padding_ready, 1)
    taps = cols(DN, k.dn, "conv", 12, 5)
    for n in range(N_QKV + 2):
        if n < N_QKV:
            dve.wait_ge(S.mm_taken, n + 1)
            if n >= 2:
                dve.wait_ge(S.qkv_silu, n - 1)
            raw, conv = k.raw[n % 2], k.conv[n % 2]
            for j in range(5):
                for at, m, to in SEGS:
                    if j == 0:
                        ins = dve.tensor_scalar(conv[:, at:at + m], raw[:, to:to + m], taps[:, n, 0:1], None, ALU.mult)
                    else:
                        ins = dve.scalar_tensor_tensor(conv[:, at:at + m], raw[:, to + j:to + j + m],
                                                       taps[:, n, j:j + 1], conv[:, at:at + m], ALU.mult, ALU.add)
                if j < 4:
                    e.link(ins)
            ins.then_inc(S.convolved, 1)
        if 2 <= n <= 9:
            v = n - 2
            dve.wait_ge(S.nstd_ready, v + 1)
            e.link(dve.reciprocal(k.nstd[v % 2], k.nstd[v % 2]))
            x = qkv_dst(k, v)
            dve.scalar_tensor_tensor(x, x, P ** -0.5 if v < 4 else 1.0, k.nstd[v % 2], ALU.mult,
                                     ALU.mult).then_inc(S.qk_normed, 1)


PE_OPS = "gb kk qk ut l2 u2 x2 l4 u4 x4 l8 x8 w y0 z0 xx0 ww0 y1 z1 xx1 ww1 y2 ks xx2 vn o1 o2 su".split()
ACT_OPS = "gam gamt up l2c u2c l4c u4c l8c wc y0c z0c y1c z1c y2c vnc".split()
DVE_OPS = ("diff dlow low0 low qg x2a x4a x8a m0x x0a m0w w0a m1x x1a m1w w1a r1 m2x x2f rr t1 t2 s1 s2").split()
POOL_OPS = "dup ld ud x1 bv kd oa".split()
TAKEN = dict(gb="diff", kk="low0", qk="qg", ut="up", l2="l2c", u2="u2c", x2="x2a", l4="l4c", u4="u4c", x4="x4a",
             l8="l8c", x8="x8a", w="wc", y0="y0c", z0="z0c", xx0="m0x", ww0="m0w", y1="y1c", z1="z1c", xx1="m1x",
             ww1="m1w", y2="y2c", ks="r1", xx2="m2x", vn="vnc", o1="t1", o2="t2", su="s2")
CHUNKS = ((4, 5, 0, 1, 2, 3), (5, 4, 3, 2, 1, 0))
N_STEPS = NT2


def owner(k, name):
    for ops, sem in ((PE_OPS, k.S.pe_events), (ACT_OPS, k.S.act_events), (DVE_OPS, k.S.dve_events), (POOL_OPS, k.S.pool_events)):
        if name in ops:
            return ops, sem


def seen(k, eng, name, s, d):
    if s < 0:
        return
    ops, sem = owner(k, name)
    eng.wait_ge(sem, 2 * (s * len(ops) + ops.index(name)) + d + 1)


def bank(k, d, name):
    return k.ps[:, 4 * d + PE_OPS.index(name) % 4, :].rearrange("p (h c) -> p h c", c=P)


def scan_pe(k, e, slot, _):
    pe = e.eng
    tri = cols(C2, k.c2, "tri", 2, P)

    def product(s, name, lhs, rhs, *needs, transpose=False):
        i = PE_OPS.index(name)
        before = PE_OPS[i - 4]
        for d in range(2):
            seen(k, pe, TAKEN[before], s if i >= 4 else s - 1, d)
            for need in needs:
                seen(k, pe, need, s, d)
            for h in range(HALF):
                out = bank(k, d, name)[:, h, :]
                if transpose:
                    last = pe.transpose(out, lhs(d, h), k.ident)
                else:
                    last = pe.matmul(out, lhs(d, h), rhs(d, h), start=True, stop=True)
            last.then_inc(k.S.pe_events, 1)

    def b(name):
        return lambda d, h: k.buf[d][name][:, h, :]

    for s in range(N_STEPS):
        def chunk(t):
            return lambda d, h: t[:, h, CHUNKS[d][s] * P:(CHUNKS[d][s] + 1) * P]

        g = st_(k, G_)
        product(s, "gb", lambda d, h: g[:, CHUNKS[d][s], 4 * d + h:4 * d + h + 1].broadcast_to([P, P]),
                lambda d, h: tri[:, d, :])
        product(s, "kk", chunk(k.kT), chunk(k.kT))
        product(s, "qk", chunk(k.kT), chunk(k.qT))
        product(s, "ut", b("low"), None, "low", transpose=True)
        product(s, "l2", b("a2"), b("a1"), "ld", "ud")
        product(s, "u2", b("a1"), b("a2"))
        product(s, "x2", b("b1"), b("x"), "l2c", "x1")
        product(s, "l4", b("b2"), b("b1"), "u2c")
        product(s, "u4", b("b1"), b("b2"))
        product(s, "x4", b("a1"), b("x"), "l4c", "x2a")
        product(s, "l8", b("a2"), b("a1"), "u4c")
        product(s, "x8", b("b1"), b("x"), "l8c", "x4a")
        product(s, "w", b("x"), None, "x8a", transpose=True)
        for i in range(2):
            product(s, f"y{i}", b("low"), b("x"), f"x{i - 1}a" if i else "x8a")
            product(s, f"z{i}", b("up"), b("b2"), f"w{i - 1}a" if i else "wc")
            product(s, f"xx{i}", b("b2"), b("a1"), f"y{i}c")
            product(s, f"ww{i}", b("x"), b("a2"), f"z{i}c")
        product(s, "y2", b("low"), b("x"), "x1a")
        for d in range(2):
            seen(k, pe, "s2", s - 1, d)
        product(s, "ks", chunk(k.kT), lambda d, h: k.state[d][:, h, :])
        product(s, "xx2", b("b2"), b("a1"), "w1a", "y2c")
        product(s, "vn", b("x"), b("b1"), "x2f", "rr")
        product(s, "o1", chunk(k.qT), lambda d, h: k.state[d][:, h, :])
        product(s, "o2", b("qg"), b("a1"), "qg", "vnc")
        product(s, "su", b("a2"), b("a1"), "kd")


def scan_act(k, e, _):
    act = e.eng

    def op(s, name, dst, src, needs, func=ACT.Copy, **kw):
        for d in range(2):
            for need, back in needs:
                seen(k, act, need, s - back, d)
            act.activation(k.buf[d][dst], src(d), func, **kw).then_inc(k.S.act_events, 1)

    for s in range(N_STEPS):
        op(s, "gam", "low", lambda d: k.buf[d]["low"], [("dlow", 0)], ACT.Exp, scale=-1.0)
        op(s, "gamt", "qg", lambda d: k.buf[d]["qg"], [("dup", 0)], ACT.Exp)
        for name, dst, src in (("up", "up", "ut"), ("l2c", "b1", "l2"), ("u2c", "b2", "u2"), ("l4c", "a1", "l4"),
                               ("u4c", "a2", "u4"), ("l8c", "b1", "l8"), ("wc", "b2", "w"), ("y0c", "a1", "y0"),
                               ("z0c", "a2", "z0"), ("y1c", "a1", "y1"), ("z1c", "a2", "z1"), ("y2c", "a1", "y2"),
                               ("vnc", "a1", "vn")):
            op(s, name, dst, lambda d, src=src: bank(k, d, src), [(src, 0)])


def scan_dve(k, e, _):
    dve = e.eng
    gmask = cols(C2, k.c2, "gmask", 2, P)
    level = cols(C2, k.c2, "level", 3, P)
    for d in range(2):
        e.link(dve.memset(k.state[d], 0.0))

    def heads(v):
        return v.unsqueeze(1).broadcast_to([P, HALF, P])

    def op(s, name, f, *needs):
        for d in range(2):
            for need in needs:
                back = need.startswith("-")
                seen(k, dve, need.lstrip("-"), s - back, d)
            f(d).then_inc(k.S.dve_events, 1)

    for s in range(N_STEPS):
        def col(i, d):
            return st_(k, i)[:, CHUNKS[d][s], 4 * d:4 * d + 4].unsqueeze(2).broadcast_to([P, HALF, P])

        def tt(dst, a, b, o):
            return lambda d: dve.tensor_tensor(dst(d), a(d), b(d), o)

        def B(n):
            return lambda d: k.buf[d][n]

        def ps(n):
            return lambda d: bank(k, d, n)

        T = B("t")
        op(s, "diff", tt(T, ps("gb"), lambda d: col(PRE, d), ALU.subtract), "gb", "-oa")
        op(s, "dlow", tt(B("low"), T, lambda d: heads(gmask[:, d, :]), ALU.add), "diff", "-y2")
        op(s, "low0", tt(B("low"), ps("kk"), B("low"), ALU.mult), "kk", "gam")
        op(s, "low", tt(B("low"), B("low"), lambda d: col(NBETA, d), ALU.mult), "low0")
        op(s, "qg", tt(B("qg"), ps("qk"), B("qg"), ALU.mult), "qk", "gamt")
        op(s, "x2a", tt(B("x"), ps("x2"), B("x"), ALU.add), "x2")
        op(s, "x4a", tt(B("x"), ps("x4"), B("x"), ALU.add), "x4")
        op(s, "x8a", tt(B("x"), ps("x8"), B("x"), ALU.add), "x8")
        for i in range(2):
            op(s, f"m{i}x", tt(T, ps(f"xx{i}"), lambda d: heads(level[:, i, :]), ALU.mult), f"xx{i}", f"w{i-1}a" if i else "x8a")
            op(s, f"x{i}a", tt(B("x"), B("x"), T, ALU.add), f"m{i}x", f"ww{i}")
            op(s, f"m{i}w", tt(T, ps(f"ww{i}"), lambda d: heads(level[:, i, :]), ALU.mult), f"x{i}a", f"ww{i}")
            op(s, f"w{i}a", tt(B("b2"), B("b2"), T, ALU.add), f"m{i}w")
        op(s, "r1", tt(T, ps("ks"), lambda d: col(NBE, d), ALU.mult), "ks", "w1a")
        op(s, "m2x", tt(B("up"), ps("xx2"), lambda d: heads(level[:, 2, :]), ALU.mult), "xx2")
        op(s, "x2f", tt(B("x"), B("x"), B("up"), ALU.add), "m2x")
        op(s, "rr", tt(B("b1"), B("b1"), T, ALU.add), "r1", "bv")
        op(s, "t1", tt(T, ps("o1"), lambda d: col(EPRE, d), ALU.mult), "o1", "rr")
        op(s, "t2", tt(T, ps("o2"), T, ALU.add), "o2", "t1")
        op(s, "s1", tt(lambda d: k.state[d], lambda d: k.state[d], lambda d: col(ETOT, d), ALU.mult), "o1")
        op(s, "s2", tt(lambda d: k.state[d], ps("su"), lambda d: k.state[d], ALU.add), "su", "s1")


def scan_pool(k, e):
    pool = e.eng
    imask = cols(C2, k.c2, "imask", 2, P)
    b16 = cols(C2, k.c2, "b16")
    e.link(pool.memset(k.oacc, 0.0))

    def heads(v):
        return v.unsqueeze(1).broadcast_to([P, HALF, P])

    for s in range(N_STEPS):
        def col(i, d):
            return st_(k, i)[:, CHUNKS[d][s], 4 * d:4 * d + 4].unsqueeze(2).broadcast_to([P, HALF, P])

        def op(name, dst, a, b, o, *needs):
            for d in range(2):
                for need in needs:
                    back = need.startswith("-")
                    seen(k, pool, need.lstrip("-"), s - back, d)
                pool.tensor_tensor(dst(d), a(d), b(d), o).then_inc(k.S.pool_events, 1)

        def B(n):
            return lambda d: k.buf[d][n]

        op("dup", B("qg"), B("t"), lambda d: heads(imask[:, d, :]), ALU.add, "diff", "-o2")
        op("ld", B("a1"), B("low"), lambda d: heads(b16), ALU.mult, "low", "-su")
        op("ud", B("a2"), B("up"), lambda d: heads(b16), ALU.mult, "up")
        op("x1", B("x"), B("a2"), lambda d: heads(k.ident), ALU.add, "ud")
        op("bv", B("b1"), lambda d: k.vc_[:, CHUNKS[d][s], :, :], lambda d: col(BETA, d), ALU.mult, "x8")
        op("kd", B("a2"), lambda d: k.kc_[:, CHUNKS[d][s], :, :], lambda d: col(EKD, d), ALU.mult, "ww1")
        for d in range(2):
            seen(k, pool, "t2", s, d)
            if s or d:
                seen(k, pool, "oa", s - (d == 0), 1 - d)
            o = k.oacc[:, CHUNKS[d][s], :, :]
            pool.tensor_tensor(o, o, k.buf[d]["t"], ALU.add).then_inc(k.S.pool_events, 1)


def opark_act(k, e, _):
    act, S = e.eng, k.S
    act.dma_start(k.T["o_park"][bass.ds(k.half, 1)].rearrange("a p t n -> (a p) t n"),
                  k.oacc.rearrange("p t h c -> p t (h c)")).then_inc(S.spilled, 16)
    act.wait_ge(S.spilled, 16)


def head_norm_act(k, e, mix, nt, sq):
    act, S = e.eng, k.S
    for t in range(nt):
        if t >= 2:
            act.wait_ge(S.head_sq_summed, t - 1)
        act.activation(sq[:, t % 2, :], mix[:, t, :], ACT.Square).then_inc(S.head_sq_ready, 1)
    act.wait_ge(S.head_ms_ready, 1)
    act.activation(k.small[:, 64:64 + 8 * nt], k.small[:, 64:64 + 8 * nt], ACT.Sqrt).then_inc(S.head_std_ready, 1)


def head_norm_dve(k, e, mix, nt, sq, gain, factor):
    dve, S = e.eng, k.S
    for t in range(nt):
        dve.wait_ge(S.head_sq_ready, t + 1)
        dve.tensor_reduce(k.small[:, 8 * t:8 * t + 8], sq[:, t % 2, :].rearrange("p (h c) -> p h c", c=P), AX.X,
                          ALU.add).then_inc(S.head_sq_summed, 1)
    dve.wait_ge(S.head_sq_summed, nt)
    dve.tensor_scalar(k.small[:, 64:64 + 8 * nt], k.small[:, 0:8 * nt], 1.0 / P, EPS, ALU.mult, ALU.add).then_inc(S.head_ms_ready, 1)
    dve.wait_ge(S.head_std_ready, 1)
    e.link(dve.reciprocal(k.small[:, 0:8 * nt], k.small[:, 64:64 + 8 * nt]))
    if factor != 1.0:
        e.link(dve.tensor_scalar(k.small[:, 0:8 * nt], k.small[:, 0:8 * nt], factor, None, ALU.mult))
    for t in range(nt):
        o = mix[:, t, :].rearrange("p (h c) -> p h c", c=P)
        e.link(dve.tensor_tensor(o, o, k.small[:, 8 * t:8 * t + 8].unsqueeze(2).broadcast_to([P, 8, P]), ALU.mult))
        e.link(dve.tensor_tensor(o, o, gain.unsqueeze(1).broadcast_to([P, 8, P]), ALU.mult))


def z_pe(k, e, slot, _):
    rows_pe(k, e, slot, k.xT, NT2, 2)


def z_act(k, e, _):
    act, S = e.eng, k.S
    head_norm_act(k, e, k.omix, NT2, k.osq2)
    for n in range(2 * NT2):
        c, t = divmod(n, NT2)
        act.wait_ge(S.mm_done, n + 1)
        act.activation(k.z[:, t, 512 * c:512 * c + 512], k.ps[:, n % 8, :], ACT.Silu).then_inc(S.mm_taken, 1)


def z_dve(k, e, _):
    dve, S = e.eng, k.S
    head_norm_dve(k, e, k.omix, NT2, k.osq2, cols(C2, k.c2, "norm_g"), 1.0)
    for n in range(2 * NT2):
        c, t = divmod(n, NT2)
        dve.wait_ge(S.mm_taken, n + 1)
        o = k.omix[:, t, 512 * c:512 * c + 512]
        dve.tensor_tensor(o, o, k.z[:, t, 512 * c:512 * c + 512], ALU.mult)


def omt_pe(k, e, slot, _):
    transposes_pe(k, e.eng, k.omix, NT2)


def omt_act(k, e, _):
    transposes_take(k, e, k.xT, NT2, 1)


def omt_dve(k, e, _):
    transposes_take(k, e, k.xT, NT2, 0)


def proj_pe(k, e, slot, arg):
    rows_pe(k, e, slot, k.xT, arg[1], 2)


def proj_dve(k, e, arg):
    dve, S = e.eng, k.S
    gate, nt = arg[0], arg[1]
    for n in range(2 * nt):
        c, t = divmod(n, nt)
        dve.wait_ge(S.mm_done, n + 1)
        row = k.gt[:, gate + t // 4, 512 * c:512 * c + 512]
        dve.tensor_tensor(k.rt[:, n % 2, :], k.ps[:, n % 8, :], row, ALU.mult).then_inc(S.mm_taken, 1)
        dve.wait_ge(S.mm_taken, n + 1)
        xs = k.x[:, t, 512 * c:512 * c + 512]
        dve.scalar_tensor_tensor(xs, xs, ALPHA, k.rt[:, n % 2, :], ALU.mult, ALU.add)


def ln_act(k, e, arg):
    act, S = e.eng, k.S
    index, nt = arg
    act.dma_start(k.lnrow, k.T["ln"][index:index + 1].broadcast_to([P, 2, D])).then_inc(S.loaded, 16)
    act.wait_ge(S.var_ready, 1)
    act.activation(k.small[:, 120:120 + nt], k.small[:, 112:112 + nt], ACT.Sqrt).then_inc(S.dev_ready, 1)
    act.wait_ge(S.loaded, 16)
    for t in range(nt):
        act.wait_ge(S.shift_ready, t + 1)
        act.activation(k.x[:, t, :], k.x[:, t, :], ACT.Identity, bias=k.small[:, 136 + t:137 + t],
                       scale=k.small[:, 128 + t:129 + t]).then_inc(S.centred, 1)


def ln_dve(k, e, arg):
    dve, S = e.eng, k.S
    index, nt = arg
    for t in range(nt):
        for i in range(2):
            ins = dve.bn_stats(k.small[:, 12 * t + 6 * i:12 * t + 6 * i + 6], k.x[:, t, 512 * i:512 * i + 512])
        e.link(ins)
        ins = dve.bn_aggr(k.small[:, 80 + 2 * t:82 + 2 * t], k.small[:, 12 * t:12 * t + 12])
    e.link(ins)
    var = k.small[:, 80:80 + 2 * nt].rearrange("p (t b) -> p t b", b=2)
    dve.tensor_scalar(k.small[:, 112:112 + nt], var[:, :, 1], LN_EPS, None, ALU.add).then_inc(S.var_ready, 1)
    dve.wait_ge(S.dev_ready, 1)
    e.link(dve.reciprocal(k.small[:, 128:128 + nt], k.small[:, 120:120 + nt]))
    for t in range(nt):
        dve.scalar_tensor_tensor(k.small[:, 136 + t:137 + t], k.small[:, 80 + 2 * t:81 + 2 * t], -1.0,
                                 k.small[:, 128 + t:129 + t], ALU.mult, ALU.mult).then_inc(S.shift_ready, 1)
    dve.wait_ge(S.loaded, 16)
    for t in range(nt):
        dve.wait_ge(S.centred, t + 1)
        e.link(dve.tensor_tensor(k.x[:, t, :], k.x[:, t, :], k.lnrow[:, 0, :], ALU.mult))
        dve.tensor_tensor(k.x[:, t, :], k.x[:, t, :], k.lnrow[:, 1, :], ALU.add)


def ffn2_pe(k, e, slot, arg):
    ffn_pe(k, e, slot, k.xT, k.hid2, arg[1])


def ffn2_act(k, e, arg):
    ffn_act(k, e, k.silu2, arg[1])


def ffn2_dve(k, e, arg):
    ffn_dve(k, e, k.silu2, k.hid2, arg[1])
    proj_dve(k, e, arg)


def dap_pe(k, e, slot, _):
    pe, S = e.eng, k.S
    for n in range(16):
        if n % 4 == 0:
            w = take_slab(k, pe, slot).rearrange("p (a b) -> p a b", b=512)
        if n >= 2:
            pe.wait_ge(S.mm_taken, n - 1)
        for s, (at, m, _) in enumerate(SEGS if n >= 8 else SEGS[:1]):
            for kt in range(KT):
                last = pe.matmul(k.ps[:, 2 * (n % 2) + s, 0:m], w[:, kt, (n % 4) * P:(n % 4) * P + P],
                                 k.xT[:, kt, at:at + m], start=kt == 0, stop=kt == KT - 1)
                if s == 0 and kt == 0:
                    release(k, last)
        if n % 4 == 3:
            slab_used(k, slot)
        last.then_inc(S.mm_done, 1)
        if n >= 1:
            da_rotate_pe(k, pe, n - 1)
    da_rotate_pe(k, pe, 15)
    for c in range(2):
        w = take_slab(k, pe, slot).rearrange("p (a b) -> p a b", b=512)
        for t in range(NT2):
            n = c * NT2 + t
            if n >= 2:
                pe.wait_ge(S.tok_taken, n - 1)
            for kt in range(KT):
                last = pe.matmul(k.ps[:, 6 + n % 2, :], k.xT[:, kt, t * P:(t + 1) * P], w[:, kt, :],
                                 start=kt == 0, stop=kt == KT - 1)
                if kt == 0:
                    release(k, last)
            if t == NT2 - 1:
                slab_used(k, slot)
            last.then_inc(S.tok_done, 1)


def da_dst(k, n):
    return k.aq[:, n, :] if n < 8 else k.ak[:, n - 8, :]


def da_rotate_pe(k, pe, n):
    S = k.S
    pe.wait_ge(S.mm_taken, n + 1)
    if n >= 2:
        pe.wait_ge(S.rot_taken, n - 1)
    pe.matmul(k.ps[:, 4 + n % 2, :], cols(C3, k.c3, "rot"), da_dst(k, n)[:, 0:512], start=True,
              stop=True).then_inc(S.stat_done, 1)


def dap_act(k, e, _):
    act, S, T = e.eng, k.S, k.T
    act.dma_start(k.c3, T["c3"]).then_inc(S.loaded, 16)
    act.dma_start(k.rotary, T["rotary"]).then_inc(S.loaded, 16)
    act.dma_start(k.lamt[:, 0:128].rearrange("p (a b) -> p a b", b=64), T["lam"][0:1].broadcast_to([P, 2, 64])).then_inc(S.lam_loaded, 16)
    act.dma_start(k.rb.rearrange("p (a b) -> p a b", b=64)[:, 0:2, :], T["lam"][1:2].broadcast_to([P, 2, 64])).then_inc(S.lam_loaded, 16)
    act.wait_ge(S.loaded, 32)
    for n in range(16):
        act.wait_ge(S.mm_done, n + 1)
        ins = act.activation(da_dst(k, n)[:, 0:512], k.ps[:, 2 * (n % 2), :], ACT.Copy)
        if n >= 8:
            ins = act.activation(da_dst(k, n)[:, 512:768], k.ps[:, 2 * (n % 2) + 1, 0:256], ACT.Copy)
        ins.then_inc(S.mm_taken, 1)
    for n in range(2 * NT2):
        c, t = divmod(n, NT2)
        act.wait_ge(S.tok_done, n + 1)
        act.activation(k.av[:, t, 512 * c:512 * c + 512], k.ps[:, 6 + n % 2, :], ACT.Copy).then_inc(S.tok_taken, 1)
    act.wait_ge(S.lam_sums_ready, 1)
    act.activation(k.lamt[:, 130:132], k.lamt[:, 128:130], ACT.Exp).then_inc(S.lam_exps_ready, 1)


def dap_dve(k, e, _):
    dve, S = e.eng, k.S
    dve.wait_ge(S.lam_loaded, 32)
    lam = k.lamt[:, 0:128].rearrange("p (a b) -> p a b", b=64)
    e.link(dve.tensor_tensor(lam, lam, k.rb.rearrange("p (a b) -> p a b", b=64)[:, 0:2, :], ALU.mult))
    dve.tensor_reduce(k.lamt[:, 128:130], lam, AX.X, ALU.add).then_inc(S.lam_sums_ready, 1)
    for n in range(16):
        x = da_dst(k, n)[:, 0:512]
        dve.wait_ge(S.stat_done, n + 1)
        e.link(dve.tensor_tensor(k.ra, x, k.rotary[:, 0, :], ALU.mult))
        dve.tensor_tensor(k.rb, k.ps[:, 4 + n % 2, :], k.rotary[:, 1, :], ALU.mult).then_inc(S.rot_taken, 1)
        dve.wait_ge(S.rot_taken, n + 1)
        e.link(dve.tensor_tensor(x, k.ra, k.rb, ALU.add))
    dve.wait_ge(S.lam_exps_ready, 1)
    e.link(dve.tensor_tensor(k.lamt[:, 132:133], k.lamt[:, 131:132], k.lamt[:, 130:131], ALU.subtract))
    e.link(dve.tensor_scalar(k.lamt[:, 133:134], k.lamt[:, 132:133], -LAMBDA_INIT, None, ALU.add))


AUNITS = [(h, i) for h in range(HEADS) for i in range(NT1)]
KEYS = NT2 * P


def da_pe(k, e, slot, _):
    pe, S = e.eng, k.S
    for u in range(len(AUNITS) + 1):
        if u < len(AUNITS):
            h, i = AUNITS[u]
            if u:
                pe.wait_ge(S.p_ready, 2 * u)
            for c in range(2):
                rows = slice(64 * c, 64 * c + 64)
                for s, (at, m, _) in enumerate(SEGS):
                    last = pe.matmul(k.ps[:, 2 * c + s, 0:m], k.aq[rows, h, i * P:(i + 1) * P],
                                     k.ak[rows, h, at:at + m], start=True, stop=True)
                last.then_inc(S.s_ps, 1)
        if u:
            v = u - 1
            h, i = AUNITS[v]
            pe.wait_ge(S.s_ready, v + 1)
            if v:
                pe.wait_ge(S.pt_ready, v)
            for j in range(NT2):
                last = pe.transpose(k.ps[:, 4 + j // 4, (j % 4) * P:(j % 4) * P + P],
                                    k.ap[v % 2][:, 0, j * P:(j + 1) * P], k.ident)
            last.then_inc(S.pt_ps, 1)
            pe.wait_ge(S.pt_ready, v + 1)
            if v >= 2:
                pe.wait_ge(S.ov_taken, v - 1)
            for j in range(NT2):
                last = pe.matmul(k.ps[:, 6 + v % 2, 0:P], k.apt[v % 2][:, j * P:(j + 1) * P],
                                 k.av[:, j, h * P:(h + 1) * P], start=j == 0, stop=j == NT2 - 1)
            last.then_inc(S.ov_ps, 1)


def da_act(k, e, _):
    act, S = e.eng, k.S
    for u in range(len(AUNITS) + 1):
        if u < len(AUNITS):
            act.wait_ge(S.o_ps, u + 1)
            if u >= 2:
                act.wait_ge(S.pt_ps, u - 1)
            for c in range(2):
                act.activation(k.ap[u % 2][:, c, :], k.ps[:, 2 * c:2 * c + 2, :].rearrange("p a b -> p (a b)")[:, 0:KEYS],
                               ACT.Exp, bias=k.amx2[:, 2 * u + c:2 * u + c + 1], scale=HD ** -0.5,
                               accum_out=k.asum[:, 2 * u + c:2 * u + c + 1]).then_inc(S.p_ready, 1)
        if u:
            v = u - 1
            act.wait_ge(S.pt_ps, v + 1)
            if v >= 2:
                act.wait_ge(S.ov_ps, v - 1)
            act.activation(k.apt[v % 2], k.ps[:, 4:6, :].rearrange("p a b -> p (a b)")[:, 0:KEYS],
                           ACT.Copy).then_inc(S.pt_ready, 1)


def da_dve(k, e, _):
    dve, S = e.eng, k.S
    for u in range(len(AUNITS) + 2):
        if u < len(AUNITS):
            h, i = AUNITS[u]
            dve.wait_ge(S.s_ps, 2 * u + 2)
            s = k.ps[:, 0:4, :].rearrange("p (c a) b -> p c (a b)", c=2)[:, :, 0:KEYS]
            e.link(dve.tensor_reduce(k.amax[:, 2 * u:2 * u + 2], s, AX.X, ALU.max))
            dve.tensor_scalar(k.amx2[:, 2 * u:2 * u + 2], k.amax[:, 2 * u:2 * u + 2], -HD ** -0.5, None,
                              ALU.mult).then_inc(S.o_ps, 1)
            dve.wait_ge(S.p_ready, 2 * u + 2)
            rec, fac = k.arec[:, 2 * u:2 * u + 2], k.afac[:, u:u + 1]
            e.link(dve.reciprocal(rec, k.asum[:, 2 * u:2 * u + 2]))
            e.link(dve.tensor_tensor(fac, rec[:, 1:2], k.asum[:, 2 * u:2 * u + 1], ALU.mult))
            e.link(dve.tensor_tensor(fac, fac, k.lamt[:, 133:134], ALU.mult))
            p = k.ap[u % 2]
            dve.scalar_tensor_tensor(p[:, 0, :], p[:, 1, :], fac, p[:, 0, :], ALU.mult, ALU.add).then_inc(S.s_ready, 1)
        if u >= 2:
            v = u - 2
            h, i = AUNITS[v]
            dve.wait_ge(S.ov_ps, v + 1)
            dve.tensor_scalar(k.amix[:, i, h * P:(h + 1) * P], k.ps[:, 6 + v % 2, 0:P], k.arec[:, 2 * v:2 * v + 1],
                              None, ALU.mult).then_inc(S.ov_taken, 1)


def dan_act(k, e, _):
    head_norm_act(k, e, k.amix, NT1, k.av[:, 0:2, :])


def dan_dve(k, e, _):
    head_norm_dve(k, e, k.amix, NT1, k.av[:, 0:2, :], cols(C3, k.c3, "subln"), 1.0 - LAMBDA_INIT)


def amt_pe(k, e, slot, _):
    transposes_pe(k, e.eng, k.amix, NT1)


def amt_act(k, e, _):
    transposes_take(k, e, k.xT, NT1, 1)


def amt_dve(k, e, _):
    transposes_take(k, e, k.xT, NT1, 0)


BEFORE = [(ada_pe, ada_act, ada_dve, 0), (modt_pe, modt_act, modt_dve, (0, NT2)),
          (nothing_pe, park_act, nothing, None)]
PER_HALF = [(gates_pe, gates_act, gates_dve, None), (qkv_pe, qkv_act, qkv_dve, None),
            (scan_pe, scan_act, scan_dve, None), (nothing_pe, opark_act, nothing, None)]
AFTER = [(nothing_pe, fetch_act, nothing, None), (z_pe, z_act, z_dve, None), (omt_pe, omt_act, omt_dve, None),
         (proj_pe, nothing, proj_dve, (0, NT2)), (nothing_pe, ln_act, ln_dve, (0, NT2)),
         (modt_pe, modt_act, modt_dve, (1, NT2)), (ffn2_pe, ffn2_act, ffn2_dve, (2, NT2)),
         (nothing_pe, ln_act, ln_dve, (1, NT2)),
         (ada_pe, ada_act, ada_dve, 1), (modt_pe, modt_act, modt_dve, (0, NT2)),
         (dap_pe, dap_act, dap_dve, None), (da_pe, da_act, da_dve, None), (nothing_pe, dan_act, dan_dve, None),
         (amt_pe, amt_act, amt_dve, None), (proj_pe, nothing, proj_dve, (0, NT1)),
         (nothing_pe, ln_act, ln_dve, (2, NT1)), (modt_pe, modt_act, modt_dve, (1, NT1)),
         (ffn2_pe, ffn2_act, ffn2_dve, (2, NT1)), (nothing_pe, ln_act, ln_dve, (3, NT1))]


def second_pe(k, e, slot):
    for f, _, _, arg in BEFORE:
        f(k, e, slot, arg)
        stage_end(k, e, "pe")
    with e.eng.Fori(0, 2):
        for f, _, _, arg in PER_HALF:
            f(k, e, slot, arg)
            stage_end(k, e, "pe")
    slot[0] += 3
    for f, _, _, arg in AFTER:
        f(k, e, slot, arg)
        stage_end(k, e, "pe")


def second_act(k, e):
    for _, f, _, arg in BEFORE:
        f(k, e, arg)
        stage_end(k, e, "act")
    with e.eng.Fori(0, 2) as k.half:
        for _, f, _, arg in PER_HALF:
            f(k, e, arg)
            stage_end(k, e, "act")
    for _, f, _, arg in AFTER:
        f(k, e, arg)
        stage_end(k, e, "act")
    e.eng.dma_start(k.T["out"].rearrange("(t p) d -> p t d", p=P), k.x[:, 0:NT1, :]).then_inc(k.S.stored, 16)
    e.eng.wait_ge(k.S.stored, 16)


def second_dve(k, e):
    for _, _, f, arg in BEFORE:
        f(k, e, arg)
        stage_end(k, e, "dve")
    with e.eng.Fori(0, 2):
        for _, _, f, arg in PER_HALF:
            f(k, e, arg)
            stage_end(k, e, "dve")
    for _, _, f, arg in AFTER:
        f(k, e, arg)
        stage_end(k, e, "dve")


def second_pool(k, e):
    for _ in BEFORE:
        stage_end_pool(k, e)
    with e.eng.Fori(0, 2):
        for f, _, _, _ in PER_HALF:
            if f is scan_pe:
                scan_pool(k, e)
            stage_end_pool(k, e)
    for _ in AFTER:
        stage_end_pool(k, e)


def k_tiles(w):
    return w.reshape(-1, P, w.shape[1]).transpose(1, 0, 2)


def chunk_slabs(w):
    return [k_tiles(w[:, c:c + 512]).reshape(P, SLAB) for c in range(0, w.shape[1], 512)]


def ffn_slabs(gate, up, down):
    out = []
    for f in range(0, FT, 2):
        out.append(np.concatenate([k_tiles(m[:, (f + i) * P:(f + i + 1) * P]).reshape(P, KT * P)
                                   for i in range(2) for m in (gate, up)], axis=1))
    for c in range(2):
        for f0, nf in ((0, 8), (8, 8), (16, 6)):
            part = k_tiles(down[f0 * P:(f0 + nf) * P, 512 * c:512 * c + 512]).reshape(P, nf * 512)
            out.append(np.concatenate([part, np.zeros((P, SLAB - nf * 512), np.float32)], axis=1))
    return out


def layer_slabs(w_in, w_out, gate_up, w_down, w1):
    nq = [w_in[:, 1536 + 64 * h:1600 + 64 * h] for h in range(N_NSA)]
    kv = [w_in[:, 1920 + P * i:1920 + P * (i + 1)] for i in range(6)]
    groups = [w_in[:, P * i:P * (i + 1)] for i in range(6)]
    groups += [np.concatenate([nq[i], nq[i + 3]], axis=1) for i in range(3)]
    groups += [kv[0], kv[1], kv[2], kv[4]]
    tiles = [k_tiles(g).reshape(P, 1024) for g in groups]
    ng = k_tiles(w_in[:, 2688:2706]).reshape(P, KT * 18)
    out = [np.concatenate(tiles[4 * i:4 * i + 4], axis=1) for i in range(3)]
    out.append(np.concatenate([tiles[12], ng, np.zeros((P, SLAB - 1024 - KT * 18), np.float32)], axis=1))
    out += chunk_slabs(np.concatenate([w_in[:, 768:1152], kv[3], w_in[:, 1152:1536], kv[5], w_in[:, 2706:3218]], axis=1))
    one = w1.reshape(2, 32, 64, 64).transpose(2, 0, 1, 3).reshape(64, SLAB)
    out.append(np.concatenate([one, one], axis=0))
    out += chunk_slabs(w_out)
    out += ffn_slabs(gate_up[:, :F], gate_up[:, F:], w_down)
    return out


def fill(table, n, rows=P):
    return np.zeros((rows, n), np.float32)


def constants1():
    c = np.zeros((P, N_C1), np.float32)

    def put(name, v):
        at, n = C1[name]
        c[:, at:at + n] = v

    m = np.arange(P)[:, None]
    f = np.arange(512)[None, :]
    for h in range(N_RET):
        gamma = math.log(1.0 - 2.0 ** (-5.0 - h))
        c[:, 512 * h:512 * h + 512] = np.where(f >= m, np.exp(np.maximum(f - m, 0) * gamma) * HD ** -0.5, 0.0)
    d = np.arange(P) % 32
    inv = (np.float32(10000.0) ** (-np.arange(32, dtype=np.float32) / np.float32(32))).astype(np.float32)
    ang = np.arange(512, dtype=np.float32)[None, :] * inv[d][:, None]
    put("cos", np.cos(ang.astype(np.float64)))
    put("sin", np.sin(ang.astype(np.float64)))
    q = np.arange(P)
    put("causal", (q[:, None] <= q[None, :]))
    rot = np.zeros((P, P))
    for j in range(P):
        if j % 64 < 32:
            rot[j + 32, j] = -1.0
        else:
            rot[j - 32, j] = 1.0
    put("rot", rot)
    put("blk", (q[:, None] // 64 == q[None, :] // 64) / 64.0)
    put("flip", q[:, None] + q[None, :] == P - 1)
    put("valid", (q[:, None] >= 31))
    return c


def bias_line():
    dist = 511 - np.arange(1024)
    hot = np.zeros((32, 1024), np.float32)
    hot[t5_bucket(dist), np.arange(1024)] = 1.0
    neg = np.broadcast_to(np.where(dist < 0, -BIG, 0.0).astype(np.float32), (6, 1024))
    return hot.reshape(32, 2, 512), np.ascontiguousarray(neg).reshape(6, 2, 512)


def small_params(v):
    out = np.zeros((DEPTH, P, N_SM), np.float32)
    for l in range(DEPTH):
        def put(name, a, rows=P):
            at, n = SM[name]
            out[l, :rows, at:at + n] = a
        put("attn_norm", v["attn_norm"][l].reshape(8, P).T)
        put("ffn_norm", v["ffn_norm"][l].reshape(8, P).T)
        put("q_gain", np.concatenate([v["nsa_q_gain"][l]] * 2)[:, None])
        put("k_gain", np.concatenate([v["nsa_k_gain"][l].T] * 2, axis=0))
        pe = v["cmp_pe"][l].transpose(2, 0, 1).reshape(64, 64)
        put("pe", np.concatenate([pe, pe], axis=0))
        at = SM["w2k"][0]
        out[l, 0:64, at:at + 64] = v["cmp_w2"][l, 0]
        out[l, 0:64, at + 192:at + 256] = v["cmp_w2"][l, 0]
        put("w2v", v["cmp_w2"][l, 1], 64)
        put("ws", v["gm_ws"][l].transpose(2, 0, 1).reshape(P, 512))
        put("gm_b", v["gm_b"][l].T)
    return out


def constants2(norm_g):
    p, f = np.arange(P)[:, None], np.arange(P)[None, :]
    parts = [(p <= f), (p >= f)]
    parts += [np.where(p > f, 0.0, BIG), np.where(p < f, 0.0, BIG)]
    parts += [np.where(p <= f, 0.0, -BIG), np.where(p >= f, 0.0, -BIG)]
    parts += [p // 16 == f // 16]
    parts += [(p // n == f // n) & (p // (n // 2) != f // (n // 2)) for n in (32, 64, 128)]
    parts += [np.broadcast_to(norm_g, (P, P))]
    return np.concatenate([np.asarray(a, np.float32) for a in parts], axis=1)


def constants3(subln):
    quarter = HD // 4
    inv = (np.float32(10000.0) ** (-np.arange(quarter, dtype=np.float32) / np.float32(quarter))).astype(np.float32)
    t = np.arange(SEQ)
    row, col = (t // 64).astype(np.float32), (t % 64).astype(np.float32)
    d = np.arange(P) % HD
    ang = np.where((d < 32)[:, None], row[None, :], col[None, :]).astype(np.float32) * inv[d % quarter][:, None]
    rot = np.zeros((P, P))
    for j in range(P):
        if j % 32 < 16:
            rot[j + 16, j] = -1.0
        else:
            rot[j - 16, j] = 1.0
    ang = ang.astype(np.float64)
    rotary = np.stack([np.cos(ang), np.sin(ang)], axis=1).astype(np.float32)
    return rotary, np.concatenate([rot, np.broadcast_to(subln, (P, P))], axis=1).astype(np.float32)


def half_params(v):
    out = []
    w = v["dn_w_in_2"][0]
    conv = v["dn_conv_2"][0]
    for half in range(2):
        heads = [half * HALF + h for h in range(HALF)]
        taps = np.stack([conv[:, base + P * h:base + P * (h + 1)].T for base in (0, D, 2 * D) for h in heads], axis=1)
        at = 4 * D
        pick = [at + 16 * m + 8 * d + h for m in range(2) for d in range(2) for h in heads]
        wab = k_tiles(w[:, pick]).reshape(P, KT * 16)
        alog = np.broadcast_to(np.concatenate([v["dn_a_log_2"][0, d, heads] for d in range(2)]), (P, 8))
        dt = np.broadcast_to(np.concatenate([v["dn_dt_bias_2"][0, d, heads] for d in range(2)]), (P, 8))
        out.append(np.concatenate([taps.reshape(P, 60), wab, alog, dt], axis=1))
    return np.stack(out)


def second_slabs(v):
    w = v["dn_w_in_2"][0]
    out = chunk_slabs(v["ada_w_2"][0])
    for half in range(2):
        for base in (0, D, 2 * D):
            out += chunk_slabs(w[:, base + 512 * half:base + 512 * half + 512])
    out += chunk_slabs(w[:, 3 * D:4 * D])
    out += chunk_slabs(v["dn_w_out_2"][0])
    out += ffn_slabs(v["ffn_w_gate_2"][0], v["ffn_w_up_2"][0], v["ffn_w_down_2"][0])
    out += chunk_slabs(v["ada_w_2"][1])
    out += chunk_slabs(v["da_w_in_2"][0])
    out += chunk_slabs(v["da_w_out_2"][0])
    out += ffn_slabs(v["ffn_w_gate_2"][1], v["ffn_w_up_2"][1], v["ffn_w_down_2"][1])
    return out


def kernel(**inputs):
    import concourse.bacc as bacc
    from concourse.bass_utils import run_bass_kernel_spmd

    v = {name: np.asarray(a) for name, a in inputs.items()}
    slabs = []
    for l in range(DEPTH):
        slabs += layer_slabs(v["w_in"][l], v["w_out"][l], v["w_gate_up"][l], v["w_down"][l], v["cmp_w1"][l])
    slabs += second_slabs(v)
    hot, neg = bias_line()
    cond = np.stack([v["c_2"][0].reshape(KT, P).T, v["c_ctx_2"].reshape(KT, P).T], axis=2)
    ln = np.stack([np.stack([v[f"ln{n}_g_2"][l], v[f"ln{n}_b_2"][l]]) for l in range(DEPTH) for n in (1, 2)])
    sel = np.zeros((2, 2, P), np.float32)
    sel[0, 0], sel[1, 1] = 1.0, 1.0
    lam = v["da_lambda_2"][0]
    rotary, c3 = constants3(v["da_subln_g_2"][0])
    c0 = np.concatenate([np.eye(P, dtype=np.float32), np.ones((P, P), np.float32)], axis=1)
    arrays = {
        "slabs": np.stack(slabs), "x": v["x"].reshape(SEQ, D), "c0": c0, "c1": constants1(), "onehot": hot,
        "negline": neg, "rel_bias": v["rel_bias"], "small1": small_params(v),
        "cond": cond, "ctx": v["ctx_2"].reshape(CTX, D), "ada_b": np.stack([v["ada_b_2"], v["ada_b_2"]], axis=1),
        "sel": sel, "ln": ln, "c2": constants2(v["dn_norm_g_2"][0]), "rotary": rotary, "c3": c3,
        "dn": half_params(v), "lam": np.stack([lam[0::2], lam[1::2]]),
    }
    nc = bacc.Bacc("TRN2", target_bir_lowering=False, num_devices=1)
    T = {}
    for name, a in arrays.items():
        arrays[name] = np.ascontiguousarray(a)
        T[name] = nc.dram_tensor(name, a.shape, F32, kind="ExternalInput").ap()
    T["out"] = nc.dram_tensor("out", (SEQ, D), F32, kind="ExternalOutput").ap()
    T["line"] = nc.dram_tensor("line", (N_NSA, 1024), F32).ap()
    T["x_park"] = nc.dram_tensor("x_park", (P, NT2, D), F32).ap()
    T["gt_park"] = nc.dram_tensor("gt_park", (P, 4, D), F32).ap()
    T["o_park"] = nc.dram_tensor("o_park", (2, P, NT2, HALF * P), F32).ap()
    build(nc, T)
    r = run_bass_kernel_spmd(nc, [arrays], core_ids=[0])
    return r.results[0]["out"].reshape(1, SEQ, D)
```

```python
import math

import numpy as np

import concourse.bass as bass
from concourse import mybir
from concourse.alu_op_type import AluOpType as ALU

F32 = mybir.dt.float32
F32R = mybir.dt.float32r
ACT = mybir.ActivationFunctionType
AX = mybir.AxisListType
P = 128
EPS = 1e-6

D = 1024
KT = D // P
SEQ = 512
CTX = 256
NT1 = SEQ // P
NT2 = (SEQ + CTX) // P
DEPTH = 2
HD = 64
N_RET = N_NSA = 6
N_CMP = (SEQ - 32) // 16 + 1
F = 2816
FT = F // P
RING = 3
SLAB = 4096
PIECE = SLAB // 2
ARENA = 24512
BIG = 1e30
N_PIECES = 2 * (27 * DEPTH + 93)
LN_EPS = 1e-5
ALPHA = (2.0 * DEPTH) ** 0.25
HEADS = 8
HALF = 4

SM = {}
_at = 0
for _name, _n in (("attn_norm", 8), ("ffn_norm", 8), ("q_gain", 1), ("k_gain", 3), ("pe", 64),
                  ("w2k", 256), ("w2v", 64), ("ws", 512), ("gm_b", 4)):
    SM[_name] = (_at, _n)
    _at += _n
N_SM = _at

C1 = {}
_at = 0
for _name, _n in (("decay", 3072), ("cos", 512), ("sin", 512), ("causal", 128), ("rot", 128),
                  ("blk", 128), ("flip", 128), ("valid", 1)):
    C1[_name] = (_at, _n)
    _at += _n
N_C1 = _at


def table(*parts):
    out, at = {}, 0
    for name, n in parts:
        out[name] = (at, n)
        at += n
    return out, at


C2, N_C2 = table(("tri", 256), ("gmask", 256), ("imask", 256), ("b16", 128), ("level", 384), ("norm_g", 128))
DN, N_DN = table(("conv", 60), ("wab", 128), ("alog", 8), ("dt", 8))
C3, N_C3 = table(("rot", 128), ("subln", 128))

C0 = {"ident": (0, 128), "ones": (128, 128)}
N_C0 = 256


def t5_bucket(dist):
    n = np.maximum(dist, 0)
    nf = np.maximum(n, 1).astype(np.float32)
    large = 16 + (np.log(nf / np.float32(16)) / np.float32(math.log(8)) * np.float32(16)).astype(np.int32)
    return np.where(n < 16, n, np.minimum(large, 31))


class Arena:

    def __init__(self, tensor, start, end):
        self.tensor, self.at, self.end = tensor, start, end

    def take(self, *shape):
        n = int(np.prod(shape))
        start, self.at = self.at, self.at + n
        assert self.at <= self.end, (self.at, self.end)
        v = self.tensor[:, start:start + n]
        if len(shape) == 2:
            v = v.rearrange("p (a b) -> p a b", b=shape[1])
        elif len(shape) == 3:
            v = v.rearrange("p (a b c) -> p a b c", b=shape[1], c=shape[2])
        return v


class Chained:

    def __init__(self, eng, sem):
        self.eng, self.sem, self.n = eng, sem, 0

    def link(self, instruction):
        self.n += 1
        instruction.then_inc(self.sem, 1)
        self.eng.wait_ge(self.sem, self.n)


def cols(table, tile, name, *shape):
    at, n = table[name]
    v = tile[:, at:at + n]
    if len(shape) == 2:
        v = v.rearrange("p (a b) -> p a b", b=shape[1])
    return v


class Semaphores:

    def __init__(self, nc):
        sem = nc.alloc_semaphore
        self.pe_chain = sem("pe_chain")
        self.act_chain = sem("act_chain")
        self.loaded = sem("loaded")
        self.dve_chain = sem("dve_chain")
        self.pool_chain = sem("pool_chain")
        self.arrived = sem("arrived")
        self.lo_ready = sem("lo_ready")
        self.piece_used = sem("piece_used")
        self.x_hi_ready = sem("x_hi_ready")
        self.hs_hi_ready = sem("hs_hi_ready")
        self.hs_ready = sem("hs_ready")
        self.hs_used = sem("hs_used")
        self.c1_loaded = sem("c1_loaded")
        self.x_loaded = sem("x_loaded")
        self.line_ready = sem("line_ready")
        self.spilled = sem("spilled")
        self.hankel_loaded = sem("hankel_loaded")
        self.line_ps = sem("line_ps")
        self.flip_taken = sem("flip_taken")
        self.flip_ps = sem("flip_ps")
        self.tr_taken_dve = sem("tr_taken_dve")
        self.tr_taken_act = sem("tr_taken_act")
        self.tr_done = sem("tr_done")
        self.normed_ready = sem("normed_ready")
        self.squares_ready = sem("squares_ready")
        self.meansq_ready = sem("meansq_ready")
        self.std_ready = sem("std_ready")
        self.mm_taken = sem("mm_taken")
        self.mm_done = sem("mm_done")
        self.ng_done = sem("ng_done")
        self.gates_ready = sem("gates_ready")
        self.nstd_ready = sem("nstd_ready")
        self.rot_taken = sem("rot_taken")
        self.sq_ready = sem("sq_ready")
        self.stat_done = sem("stat_done")
        self.tok_taken = sem("tok_taken")
        self.tok_done = sem("tok_done")
        self.head_normed = sem("head_normed")
        self.kb_ready = sem("kb_ready")
        self.hid_ps = sem("hid_ps")
        self.v_ready = sem("v_ready")
        self.sv_ps = sem("sv_ps")
        self.hid_ready = sem("hid_ready")
        self.kcv_ps = sem("kcv_ps")
        self.kc_sq = sem("kc_sq")
        self.kn_ps = sem("kn_ps")
        self.vsq_ready = sem("vsq_ready")
        self.vms_ready = sem("vms_ready")
        self.vstd_ready = sem("vstd_ready")
        self.kn_std = sem("kn_std")
        self.st_ready = sem("st_ready")
        self.o_taken = sem("o_taken")
        self.o_ps = sem("o_ps")
        self.st_ps = sem("st_ps")
        self.osq_ready = sem("osq_ready")
        self.oms_ready = sem("oms_ready")
        self.ostd_ready = sem("ostd_ready")
        self.s_ready = sem("s_ready")
        self.s_ps = sem("s_ps")
        self.p_ready = sem("p_ready")
        self.pt_ready = sem("pt_ready")
        self.pt_ps = sem("pt_ps")
        self.ov_taken = sem("ov_taken")
        self.ov_ps = sem("ov_ps")
        self.hid_taken = sem("hid_taken")
        self.gate_ps = sem("gate_ps")
        self.silu_ready = sem("silu_ready")
        self.cond_ready = sem("cond_ready")
        self.aux_taken = sem("aux_taken")
        self.aux_done = sem("aux_done")
        self.ada_b_loaded = sem("ada_b_loaded")
        self.ab_ps = sem("ab_ps")
        self.log_decay_ready = sem("log_decay_ready")
        self.prefix_ps = sem("prefix_ps")
        self.neg_abs_ready = sem("neg_abs_ready")
        self.softplus_ready = sem("softplus_ready")
        self.ab_read = sem("ab_read")
        self.prefix_ready = sem("prefix_ready")
        self.exps_ready = sem("exps_ready")
        self.qk_normed = sem("qk_normed")
        self.qkv_silu = sem("qkv_silu")
        self.padding_ready = sem("padding_ready")
        self.convolved = sem("convolved")
        self.pe_events = sem("pe_events")
        self.act_events = sem("act_events")
        self.dve_events = sem("dve_events")
        self.pool_events = sem("pool_events")
        self.head_sq_summed = sem("head_sq_summed")
        self.head_sq_ready = sem("head_sq_ready")
        self.head_ms_ready = sem("head_ms_ready")
        self.head_std_ready = sem("head_std_ready")
        self.var_ready = sem("var_ready")
        self.dev_ready = sem("dev_ready")
        self.shift_ready = sem("shift_ready")
        self.centred = sem("centred")
        self.lam_loaded = sem("lam_loaded")
        self.lam_sums_ready = sem("lam_sums_ready")
        self.lam_exps_ready = sem("lam_exps_ready")
        self.stage_range = range(self.pe_chain.num, self.lam_exps_ready.num + 1)
        self.go = {"pe": sem("go_pe"), "act": sem("go_act"), "dve": sem("go_dve")}
        self.full = [sem(f"slot_full{i}") for i in range(RING)]
        self.empty = [sem(f"slot_empty{i}") for i in range(RING)]
        self.stored = sem("stored")
        self.parked = sem("parked")
        self.x_back = sem("x_back")


class Ctx:
    pass


def build(nc, T):
    k = Ctx()
    k.nc, k.T = nc, T
    k.later = []
    k.dve_piece = 0
    S = Semaphores(nc)
    k.S = S
    assert len(S.stage_range) == 98

    def place(name, n, dtype=F32):
        return nc.alloc_sbuf_tensor(name, [P, n], dtype)

    with nc.sbuf_tensor("pieces_in", [P, RING * PIECE], F32) as pieces_in:
        pass
    pieces_lo = place("pieces_lo", RING * PIECE, F32R)
    pieces_hi = place("pieces_hi", 2 * PIECE, F32R)
    x_mem = place("x_mem", NT2 * D)
    with nc.sbuf_tensor("xt_values", [P, 2 * KT * NT2 * P], F32) as xt_mem:
        pass
    xt_operands = place("xt_operands", 2 * KT * NT2 * P, F32R)
    with nc.sbuf_tensor("arena", [P, ARENA], F32) as arena:
        pass
    hidden_operands = place("hidden_operands", 4 * SEQ, F32R)
    place("arena_behind_hidden_operands", ARENA - 4 * SEQ)
    k.psum = nc.alloc_psum_tensor("psum", [P, 8, 512], F32)
    k.ps = k.psum[:, :, :]
    k.ring, k.ring_lo, k.hi = [[v[:, PIECE * i:PIECE * (i + 1)] for i in range(n)]
                               for v, n in ((pieces_in, RING), (pieces_lo, RING), (pieces_hi, 2))]
    k.x = Arena(x_mem, 0, NT2 * D).take(NT2, D)
    xr = Arena(xt_operands, 0, 2 * KT * NT2 * P)
    k.xTh, k.xTl = xr.take(KT, NT2 * P), xr.take(KT, NT2 * P)
    k.value = lambda v: bass.AP(xt_mem, v.offset, v.ap)
    k.hs = Arena(hidden_operands, 0, 4 * SEQ).take(4, SEQ).rearrange("p (a b) c -> p a b c", b=2)
    k.hs_short = Arena(hidden_operands, 0, 4 * SEQ).take(8, 2 * P).rearrange("p (a b) c -> p a b c", b=2)
    common = Arena(arena, ARENA - N_C0 - 256, ARENA)
    arena_end = common.at
    k.c0 = common.take(N_C0)
    k.ident = cols(C0, k.c0, "ident")
    k.ones = cols(C0, k.c0, "ones")
    k.small = common.take(256)

    k.x1 = k.x[:, 0:NT1, :]
    xr = Arena(xt_operands, 0, 2 * KT * SEQ)
    k.x1h, k.x1l = xr.take(KT, SEQ), xr.take(KT, SEQ)
    k.mix = Arena(xt_mem, xr.at, xr.at + NT1 * D).take(NT1, D)
    k.back_x = x_mem[:, NT1 * D:NT2 * D]
    k.back_xt = xt_mem[:, 0:2 * KT * SEQ]
    lasting = Arena(arena, arena_end - N_C1 - N_SM - N_NSA * (512 + NT1 * 32) - NT1 * 18 - 8, arena_end)
    work_end = lasting.at
    k.c1 = lasting.take(N_C1)
    k.sm = lasting.take(N_SM)
    k.bias = lasting.take(N_NSA, 512)
    k.biasc = lasting.take(N_NSA, NT1, 32)
    k.gates = lasting.take(NT1, 18)
    k.gains = lasting.take(8)
    a = Arena(arena, 0, work_end)
    k.tt = a.take(13, 512)
    k.tok = a.take(NT1, 3, 512)
    k.tmp = a.take(work_end - a.at)
    b = Arena(arena, 4 * SEQ, work_end)
    k.hid = b.take(FT, SEQ)
    k.silu = b.take(2, SEQ)
    k.hn = Arena(arena, 0, work_end).take(NT1, D)
    k.eps = k.small[:, 255:256]
    k.both = lambda nt: (k.xTh, k.xTl) if nt > NT1 else (k.x1h, k.x1l)
    bx, bt, tmp = k.back_x, k.back_xt, k.tmp
    k.tmpv = lambda n: bx[:, 512 * (n % 2):512 * (n % 2) + 512]
    k.stdv = lambda n: bx[:, 1024 + 512 * (n % 2):1536 + 512 * (n % 2)]
    k.rstdv, k.rotv = k.mix[:, 0, 0:512], k.mix[:, 0, 512:1024]
    k.kb = bx.rearrange("p (a b) -> p a b", b=512)
    k.vsq = bt[:, 0:1024].rearrange("p (t d) -> p t d", d=256)
    k.kc, k.vc = tmp[:, 0:32], tmp[:, 32:160]
    k.hidc = tmp[:, 160:288].rearrange("p (a b) -> p a b", b=32)
    k.kcsq, k.kcstd, k.kcr = tmp[:, 288:320], tmp[:, 320:352], tmp[:, 352:384]
    k.st = lambda h, j: (bx, bt)[h % 2][:, (0, 512, 896, 1152)[j]:(512, 896, 1152, 1280)[j]]
    k.osq = tmp[:, 160:1696].rearrange("p (t d) -> p t d", d=384)
    k.sneg = lambda u: bx[:, 512 * (u % 3):512 * (u % 3) + 512]
    k.pexp = lambda u: bt[:, 512 * (u % 3):512 * (u % 3) + 512]
    k.ptr = lambda u: bt[:, 1536 + 512 * (u % 3):2048 + 512 * (u % 3)]
    k.nmax, k.psums = bt[:, 3072:3144], bt[:, 3144:3216]
    k.onehot = k.tt[0:32, 0:2, :]
    k.negline = k.tt[0:6, 2:4, :]
    k.line = k.tt[0:6, 4:6, :]
    k.relb = k.tt[0:32, 6, 0:6]
    k.hankel = arena[:, 13 * 512:13 * 512 + 6 * 896].rearrange("p (h c) -> p h c", c=896)
    k.flipped = k.mix[:, 0, 0:896]

    place2(k, arena, arena_end, x_mem)

    slot = [0]

    with nc.Block() as block:
        @block.sync
        def _(sp):
            src = T["pieces"]
            for i in range(RING):
                sp.dma_start(k.ring[i], src[i]).then_inc(S.full[i], 16)
            with sp.Fori(1, N_PIECES // RING) as turn:
                for i in range(RING):
                    sp.wait_ge(S.empty[i], 1)
                    sp.sem_clear(S.empty[i])
                    sp.dma_start(k.ring[i], src[bass.ds(turn * RING + i, 1)]
                                 .rearrange("a p n -> (a p) n")).then_inc(S.full[i], 16)

        @block.tensor
        def _(pe):
            e = Chained(pe, S.pe_chain)
            slot[0] = 0
            setup_pe(k, e)
            with pe.Fori(0, DEPTH):
                slot[0] = 0
                for stage_pe in (rms_pe, in_t_pe, in_tok_pe, compress_pe, retention_pe, nsa_pe, mixt_pe,
                                 out_pe, rms_pe, ffn1_pe):
                    stage_pe(k, e, slot)
                    stage_end(k, e, "pe")
            slot[0] = 0
            second_pe(k, e, slot)

        @block.scalar
        def _(act):
            e = Chained(act, S.act_chain)
            setup_act(k, e)
            with act.Fori(0, DEPTH) as layer:
                act.dma_start(k.sm, T["small1"][bass.ds(layer, 1)].rearrange("a p n -> (a p) n")).then_inc(S.loaded, 16)
                act.wait_ge(S.loaded, 16)
                for stage_act, arg in ((rms_act, "attn_norm"), (in_t_act, None), (in_tok_act, None),
                                       (compress_act, None), (retention_act, None), (nsa_act, None),
                                       (mixt_act, None), (out_act, None), (rms_act, "ffn_norm"),
                                       (ffn1_act, None)):
                    stage_act(k, e, arg)
                    stage_end(k, e, "act")
            second_act(k, e)

        @block.vector
        def _(dve):
            e = Chained(dve, S.dve_chain)
            setup_dve(k, e)
            with dve.Fori(0, DEPTH):
                for stage_dve, arg in ((rms_dve, "attn_norm"), (in_t_dve, None), (in_tok_dve, None),
                                       (compress_dve, None), (retention_dve, None), (nsa_dve, None),
                                       (mixt_dve, None), (out_dve, None), (rms_dve, "ffn_norm"),
                                       (ffn1_dve, None)):
                    stage_dve(k, e, arg)
                    stage_end(k, e, "dve")
            second_dve(k, e)

        @block.gpsimd
        def _(pool):
            e = Chained(pool, S.pool_chain)
            setup_pool(k, e)
            with pool.Fori(0, DEPTH):
                for stage_pool in (xt_pool, no_pool, no_pool, no_pool, no_pool, no_pool,
                                   xt_pool, no_pool, xt_pool, no_pool):
                    stage_pool(k, e)
                    stage_end_pool(k, e)
            second_pool(k, e)


def stage_end(k, e, name):
    while name == "pe" and k.later:
        signal_later(k, e.eng.drain())
    e.eng.drain().then_inc(k.S.arrived, 1)
    e.eng.wait_ge(k.S.go[name], 1)
    e.eng.sem_clear(k.S.go[name])
    e.n = 0


def stage_end_pool(k, e):
    e.eng.drain()
    e.eng.wait_ge(k.S.arrived, 3)
    e.eng.sem_clear(k.S.stage_range)
    for name in ("pe", "act", "dve"):
        e.eng.sem_inc(k.S.go[name], 1)
    e.n = 0


def take_raw(k, pe, slot):
    i = slot[0] % RING
    pe.wait_ge(k.S.full[i], 16)
    pe.sem_clear(k.S.full[i])
    return k.ring[i]


def take_split(k, pe, slot, n):
    pe.wait_ge(k.S.lo_ready, n + 1)
    return k.hi[n % 2], k.ring_lo[slot[0] % RING]


def piece_used(k, slot, split=True):
    k.later.append(k.S.empty[slot[0] % RING])
    if split:
        k.later.append(k.S.piece_used)
    slot[0] += 1


def signal_later(k, instruction):
    if k.later:
        instruction.then_inc(k.later.pop(0), 1)


def product3(k, pe, out, stationary, moving, start, stop):
    (sh, sl), (mh, ml) = stationary, moving
    signal_later(k, pe.matmul(out, sh, mh, start=start, stop=False))
    signal_later(k, pe.matmul(out, sh, ml, start=False, stop=False))
    return pe.matmul(out, sl, mh, start=False, stop=stop)


def split_dve(k, e, n, with_lo=True):
    dve, S = e.eng, k.S
    i = k.dve_piece % RING
    k.dve_piece += 1
    dve.wait_ge(S.full[i], 16)
    dve.sem_clear(S.full[i])
    if n >= 2:
        dve.wait_ge(S.piece_used, n - 1)
    e.link(dve.tensor_copy(k.hi[n % 2], k.ring[i]))
    if with_lo:
        split_lo_dve(k, e, n, i)
    return i


def split_lo_dve(k, e, n, i):
    e.eng.tensor_tensor(k.ring_lo[i], k.ring[i], k.hi[n % 2].bitcast(F32), ALU.subtract).then_inc(k.S.lo_ready, 1)


def xt_pool(k, e, _=None):
    transposes_pool(k, e, k.both(NT1), NT1)


def no_pool(k, e, _=None):
    pass


def setup_act(k, e):
    act, S, T = e.eng, k.S, k.T
    act.dma_start(k.onehot, T["onehot"]).then_inc(S.loaded, 16)
    act.dma_start(k.negline, T["negline"]).then_inc(S.loaded, 16)
    act.dma_start(k.relb, T["rel_bias"]).then_inc(S.loaded, 16)
    act.dma_start(k.c0, T["c0"]).then_inc(S.loaded, 16)
    act.dma_start(k.c1, T["c1"]).then_inc(S.c1_loaded, 16)
    act.dma_start(k.x1, T["x"].rearrange("(t p) d -> p t d", p=P)).then_inc(S.x_loaded, 16)
    act.wait_ge(S.line_ready, 2)
    act.dma_start(T["line"].rearrange("h (a b) -> h a b", b=512), k.line).then_inc(S.spilled, 16)
    act.wait_ge(S.spilled, 16)
    line = T["line"]
    for h in range(N_NSA):
        act.dma_start(k.hankel[:, h, :], bass.AP(line.tensor, h * 1024, [[1, P], [1, 896]])).then_inc(S.hankel_loaded, 16)
    act.wait_ge(S.x_loaded, 16)
    stage_end(k, e, "act")


def setup_pe(k, e):
    pe, S = e.eng, k.S
    pe.wait_ge(S.loaded, 16 * 4)
    for i in range(2):
        pe.matmul(k.ps[0:6, i, :], k.relb, k.onehot[:, i, :], start=True, stop=True).then_inc(S.line_ps, 1)
    pe.wait_ge(S.c1_loaded, 16)
    pe.wait_ge(S.hankel_loaded, 16 * N_NSA)
    flip = cols(C1, k.c1, "flip")
    for h in range(N_NSA):
        for i, (at, n) in enumerate(((0, 512), (512, 384))):
            job = 2 * h + i
            if job >= 4:
                pe.wait_ge(S.flip_taken, job - 3)
            pe.matmul(k.ps[:, 4 + job % 4, 0:n], flip, k.hankel[:, h, at:at + n], start=True,
                      stop=True).then_inc(S.flip_ps, 1)
    stage_end(k, e, "pe")


def setup_dve(k, e):
    dve, S = e.eng, k.S
    e.link(dve.memset(k.eps, EPS))
    for i in range(2):
        dve.wait_ge(S.line_ps, i + 1)
        dve.tensor_tensor(k.line[:, i, :], k.ps[0:6, i, :], k.negline[:, i, :], ALU.add).then_inc(S.line_ready, 1)
    for h in range(N_NSA):
        dve.wait_ge(S.flip_ps, 2 * h + 1)
        dve.tensor_copy(k.flipped[:, 0:512], k.ps[:, 4 + (2 * h) % 4, :]).then_inc(S.flip_taken, 1)
        dve.wait_ge(S.flip_ps, 2 * h + 2)
        dve.tensor_copy(k.flipped[:, 512:896], k.ps[:, 4 + (2 * h + 1) % 4, 0:384]).then_inc(S.flip_taken, 1)
        dve.wait_ge(S.flip_taken, 2 * h + 2)
        dve.tensor_copy(k.bias[:, h, :], k.flipped[:, 0:512])
        for i in range(NT1):
            at = 415 - P * i
            ins = dve.tensor_copy(k.biasc[:, h, i, 0:N_CMP], k.flipped[:, at:at + 16 * (N_CMP - 1) + 1:16])
        e.link(ins)
    stage_end(k, e, "dve")


def setup_pool(k, e):
    stage_end_pool(k, e)


def tr_jobs(nt):
    return [(kt, t0, min(4, nt - t0)) for kt in range(KT) for t0 in range(0, nt, 4)]


def transposes_pe(k, pe, src, nt):
    S = k.S
    for n, (kt, t0, m) in enumerate(tr_jobs(nt)):
        if n >= 4:
            pe.wait_ge((S.tr_taken_dve, S.tr_taken_act)[n % 2], (n - 4) // 2 + 1)
        for t in range(m):
            last = pe.transpose(k.ps[:, n % 4, t * P:(t + 1) * P], src[:, t0 + t, kt * P:(kt + 1) * P], k.ident)
        last.then_inc(S.tr_done, 1)


def transposes_take(k, e, dst, nt, which, scale=None, bias=None):
    S, eng = k.S, e.eng
    for n, (kt, t0, m) in enumerate(tr_jobs(nt)):
        span = slice(t0 * P, (t0 + m) * P)
        hi, out, src = dst[0][:, kt, span], k.value(dst[1][:, kt, span]), k.ps[:, n % 4, 0:m * P]
        if n % 2 == which:
            eng.wait_ge(S.tr_done, n + 1)
            sc = scale(kt, t0) if scale else 1.0
            if which == 0:
                if bias:
                    ins = eng.tensor_scalar(out, src, sc, bias(kt, t0), ALU.mult, ALU.add)
                else:
                    ins = eng.tensor_scalar(out, src, sc, None, ALU.mult)
                ins.then_inc(S.tr_taken_dve, 1)
            else:
                if bias:
                    ins = eng.activation(out, src, ACT.Identity, bias=bias(kt, t0), scale=sc)
                else:
                    ins = eng.activation(out, src, ACT.Copy, scale=sc)
                ins.then_inc(S.tr_taken_act, 1)
        if which == 0:
            eng.wait_ge((S.tr_taken_dve, S.tr_taken_act)[n % 2], n // 2 + 1)
            eng.tensor_copy(hi, out).then_inc(S.x_hi_ready, 1)


def transposes_pool(k, e, dst, nt):
    for n, (kt, t0, m) in enumerate(tr_jobs(nt)):
        span = slice(t0 * P, (t0 + m) * P)
        e.eng.wait_ge(k.S.x_hi_ready, n + 1)
        lo = dst[1][:, kt, span]
        e.eng.tensor_tensor(lo, k.value(lo), dst[0][:, kt, span].bitcast(F32), ALU.subtract)


def rms_pe(k, e, slot):
    e.eng.wait_ge(k.S.normed_ready, NT1)
    transposes_pe(k, e.eng, k.hn, NT1)


def rms_act(k, e, name):
    act, S = e.eng, k.S
    for t in range(NT1):
        act.activation(k.hn[:, t, :], k.x1[:, t, :], ACT.Square,
                       accum_out=k.small[:, t:t + 1]).then_inc(S.squares_ready, 1)
    act.wait_ge(S.meansq_ready, 1)
    act.activation(k.small[:, 12:16], k.small[:, 8:12], ACT.Sqrt).then_inc(S.std_ready, 1)
    g = cols(SM, k.sm, name)
    transposes_take(k, e, (k.x1h, k.x1l), NT1, 1, scale=lambda kt, t0: g[:, kt:kt + 1])


def rms_dve(k, e, name):
    dve, S = e.eng, k.S
    dve.wait_ge(S.squares_ready, NT1)
    dve.tensor_scalar(k.small[:, 8:12], k.small[:, 0:4], 1.0 / D, EPS, ALU.mult, ALU.add).then_inc(S.meansq_ready, 1)
    dve.wait_ge(S.std_ready, 1)
    e.link(dve.reciprocal(k.small[:, 16:20], k.small[:, 12:16]))
    for t in range(NT1):
        dve.tensor_scalar(k.hn[:, t, :], k.x1[:, t, :], k.small[:, 16 + t:17 + t], None, ALU.mult).then_inc(S.normed_ready, 1)
    g = cols(SM, k.sm, name)
    transposes_take(k, e, (k.x1h, k.x1l), NT1, 0, scale=lambda kt, t0: g[:, kt:kt + 1])


def in_t_pe(k, e, slot):
    pe, S = e.eng, k.S
    for g in range(13):
        if g % 2 == 0:
            w = take_split(k, pe, slot, g // 2)
        if g >= 4:
            pe.wait_ge(S.mm_taken, g - 3)
        for kt in range(KT):
            at = (g % 2) * 1024 + kt * P
            last = product3(k, pe, k.ps[:, g % 4, :], pair(w, slice(at, at + P)), pair((k.x1h, k.x1l), kt),
                            kt == 0, kt == KT - 1)
        if g % 2 == 1:
            piece_used(k, slot)
        last.then_inc(S.mm_done, 1)
    for t in range(NT1):
        for kt in range(KT):
            last = product3(k, pe, k.ps[:, 4, t * 18:(t + 1) * 18], pair((k.x1h, k.x1l), kt, slice(t * P, (t + 1) * P)),
                            pair(w, slice(1024 + kt * 18, 1024 + (kt + 1) * 18)), kt == 0, kt == KT - 1)
    piece_used(k, slot)
    last.then_inc(S.ng_done, 1)
    take_raw(k, pe, slot)
    piece_used(k, slot, split=False)


def pair(v, *index):
    return tuple(part[(slice(None),) + index] for part in v)


def in_t_act(k, e, _):
    act, S = e.eng, k.S
    for g in range(13):
        act.wait_ge(S.mm_done, g + 1)
        act.activation(k.tt[:, g, :], k.ps[:, g % 4, :], ACT.Copy).then_inc(S.mm_taken, 1)
    act.wait_ge(S.ng_done, 1)
    act.activation(k.gates[:, :, :], k.ps[:, 4, 0:72].rearrange("p (t c) -> p t c", c=18), ACT.Sigmoid).then_inc(S.gates_ready, 1)


def in_t_dve(k, e, _):
    dve, S = e.eng, k.S
    for n in range(7):
        split_dve(k, e, n)
    k.dve_piece += 1
    dve.tensor_scalar(k.gains[:, 0:1], cols(SM, k.sm, "q_gain"), HD ** -0.5, None, ALU.mult)
    dve.tensor_copy(k.gains[:, 1:4], cols(SM, k.sm, "k_gain"))
    ws = cols(SM, k.sm, "ws", 4, P)
    mask = cols(C1, k.c1, "causal")
    for g in range(4):
        dve.tensor_tensor(ws[:, g, :], ws[:, g, :], mask, ALU.mult)
    dve.wait_ge(S.gates_ready, 1)
    for h in range(N_NSA):
        ins = dve.tensor_scalar(k.gates[:, 0, 3 * h:3 * h + 1], k.gates[:, 0, 3 * h:3 * h + 1],
                                cols(C1, k.c1, "valid"), None, ALU.mult)
    e.link(ins)


NORM_GROUPS = [(6, 0), (7, 0), (8, 0), (11, 2), (12, 3)]
N_POST = len(NORM_GROUPS) + 6


def in_tok_pe(k, e, slot):
    pe, S = e.eng, k.S
    nn = len(NORM_GROUPS)

    def statistics_or_rotation(n):
        if n >= 4:
            if n - 4 < nn:
                pe.wait_ge(S.nstd_ready, n - 3)
            else:
                pe.wait_ge(S.rot_taken, n - 4 - nn + 1)
        if n < nn:
            pe.wait_ge(S.sq_ready, n + 1)
            pe.matmul(k.ps[:, n % 4, :], cols(C1, k.c1, "blk"), k.tmpv(n), start=True, stop=True).then_inc(S.stat_done, 1)
        else:
            pe.matmul(k.ps[:, n % 4, :], cols(C1, k.c1, "rot"), k.tt[:, n - nn, :], start=True,
                      stop=True).then_inc(S.stat_done, 1)

    for c in range(3):
        for part in range(2):
            w = take_split(k, pe, slot, 2 * c + part)
            for t in range(NT1):
                n = NT1 * c + t
                if part == 1 and n < N_POST:
                    statistics_or_rotation(n)
                if part == 0 and n >= 4:
                    pe.wait_ge(S.tok_taken, n - 3)
                for i in range(4):
                    last = product3(k, pe, k.ps[:, 4 + t, :], pair((k.x1h, k.x1l), 4 * part + i, slice(t * P, (t + 1) * P)),
                                    pair(w, slice(512 * i, 512 * i + 512)), part == 0 and i == 0, part == 1 and i == 3)
                if part == 1:
                    last.then_inc(S.tok_done, 1)
            piece_used(k, slot)


def in_tok_act(k, e, _):
    act, S = e.eng, k.S
    nn = len(NORM_GROUPS)

    def square(n):
        if n >= 2:
            act.wait_ge(S.stat_done, n - 1)
        act.activation(k.tmpv(n), k.tt[:, NORM_GROUPS[n][0], :], ACT.Square).then_inc(S.sq_ready, 1)

    square(0)
    for n in range(12):
        if n + 1 < nn:
            square(n + 1)
        if n < nn:
            act.wait_ge(S.stat_done, n + 1)
            if n >= 2:
                act.wait_ge(S.head_normed, n - 1)
            act.activation(k.stdv(n), k.ps[:, n % 4, :], ACT.Sqrt, bias=k.eps).then_inc(S.nstd_ready, 1)
        c, t = divmod(n, NT1)
        act.wait_ge(S.tok_done, n + 1)
        out, ps = k.tok[:, t, c, :], k.ps[:, 4 + n % 4, :]
        if c == 0:
            act.activation(out, ps, ACT.Copy).then_inc(S.tok_taken, 1)
        elif c == 1:
            act.activation(out[:, 0:384], ps[:, 0:384], ACT.Silu)
            act.activation(out[:, 384:512], ps[:, 384:512], ACT.Copy).then_inc(S.tok_taken, 1)
        else:
            act.activation(out, ps, ACT.Gelu_apprx_tanh).then_inc(S.tok_taken, 1)


def in_tok_dve(k, e, _):
    dve, S = e.eng, k.S
    nn = len(NORM_GROUPS)

    def normalise(n):
        g, gain = NORM_GROUPS[n]
        dve.wait_ge(S.nstd_ready, n + 1)
        e.link(dve.reciprocal(k.rstdv, k.stdv(n)))
        dve.scalar_tensor_tensor(k.tt[:, g, :], k.tt[:, g, :], k.gains[:, gain:gain + 1], k.rstdv,
                                 ALU.mult, ALU.mult).then_inc(S.head_normed, 1)
        dve.wait_ge(S.head_normed, n + 1)

    def rotate(r):
        e.link(dve.tensor_tensor(k.rstdv, k.tt[:, r, :], cols(C1, k.c1, "cos"), ALU.mult))
        dve.wait_ge(S.stat_done, nn + r + 1)
        dve.tensor_tensor(k.rotv, k.ps[:, (nn + r) % 4, :], cols(C1, k.c1, "sin"), ALU.mult).then_inc(S.rot_taken, 1)
        dve.wait_ge(S.rot_taken, r + 1)
        e.link(dve.tensor_tensor(k.tt[:, r, :], k.rstdv, k.rotv, ALU.add))

    split_dve(k, e, 0)
    for n in range(N_POST):
        if n % 2 == 0 and n // 2 + 1 < 6:
            split_dve(k, e, n // 2 + 1)
        if n < nn:
            normalise(n)
        else:
            rotate(n - nn)


def compress_pe(k, e, slot):
    pe, S = e.eng, k.S
    pe.wait_ge(S.kb_ready, 4)
    for j in range(2):
        w1 = take_raw(k, pe, slot).rearrange("p (l c) -> p l c", c=64)
        for g in range(2):
            rows = slice(64 * g, 64 * g + 64)
            for l in range(32):
                a, r = divmod(l, 16)
                rhs = k.kb[rows, 2 * j + a, :].rearrange("p (n r) -> p n r", r=16)[:, a:a + N_CMP, r]
                last = pe.matmul(k.ps[0:64, (0, 6)[g], 32 * j:32 * j + N_CMP],
                                 w1[rows, l, :], rhs, start=l == 0, stop=l == 31)
                if l == 0:
                    signal_later(k, last)
        piece_used(k, slot, split=False)
    last.then_inc(S.hid_ps, 1)
    ws = cols(SM, k.sm, "ws", 4, P)
    pe.wait_ge(S.v_ready, 1)
    for g in range(4):
        pe.matmul(k.ps[:, 4 + g // 2, (g % 2) * 256:(g % 2) * 256 + 256], ws[:, g, :],
                  k.tok[:, :, 2, 256 + 64 * g:320 + 64 * g], start=True, stop=True).then_inc(S.sv_ps, 1)
    pe.wait_ge(S.hid_ready, 2)
    w2k = cols(SM, k.sm, "w2k", 2, P)
    w2v = cols(SM, k.sm, "w2v")
    for g in range(2):
        pe.matmul(k.ps[:, 1, 0:N_CMP], w2k[0:64, g, :], k.hidc[0:64, g, 0:N_CMP], start=g == 0, stop=g == 1)
    for g in range(2):
        last = pe.matmul(k.ps[0:N_CMP, 2, 64 * g:64 * g + 64], k.hidc[0:64, 2 + g, 0:N_CMP], w2v[0:64, :],
                         start=True, stop=True)
    last.then_inc(S.kcv_ps, 1)
    pe.wait_ge(S.kc_sq, 1)
    pe.matmul(k.ps[:, 3, 0:N_CMP], cols(C1, k.c1, "blk"), k.kcsq[:, 0:N_CMP], start=True, stop=True).then_inc(S.kn_ps, 1)


def compress_act(k, e, _):
    act, S = e.eng, k.S
    v = k.tok[:, :, 2, 256:512]
    act.activation(k.vsq, v, ACT.Square).then_inc(S.vsq_ready, 1)
    act.wait_ge(S.vms_ready, 1)
    act.activation(k.small[:, 64:80], k.small[:, 48:64], ACT.Sqrt).then_inc(S.vstd_ready, 1)
    act.wait_ge(S.hid_ps, 1)
    for g in range(2):
        act.activation(k.hidc[0:64, g:4:2, 0:N_CMP],
                       k.ps[0:64, (0, 6)[g], 0:64].rearrange("p (a b) -> p a b", b=32)[:, :, 0:N_CMP],
                       ACT.Gelu_apprx_tanh).then_inc(S.hid_ready, 1)
    act.wait_ge(S.kcv_ps, 1)
    act.activation(k.kcsq[:, 0:N_CMP], k.ps[:, 1, 0:N_CMP], ACT.Square).then_inc(S.kc_sq, 1)
    act.activation(k.vc[0:N_CMP, :], k.ps[0:N_CMP, 2, 0:P], ACT.Copy)
    act.wait_ge(S.kn_ps, 1)
    act.activation(k.kcstd[:, 0:N_CMP], k.ps[:, 3, 0:N_CMP], ACT.Sqrt, bias=k.eps).then_inc(S.kn_std, 1)


def compress_dve(k, e, _):
    dve, S = e.eng, k.S
    k.dve_piece += 2
    pe_ = cols(SM, k.sm, "pe", 2, 32)
    for j in range(2):
        for a in range(2):
            dve.tensor_tensor(k.kb[:, 2 * j + a, :].rearrange("p (n r) -> p n r", r=16),
                              k.tt[:, 9 + j, :].rearrange("p (n r) -> p n r", r=16),
                              pe_[:, j, 16 * a:16 * a + 16].unsqueeze(1).broadcast_to([P, 32, 16]),
                              ALU.add).then_inc(S.kb_ready, 1)
    dve.wait_ge(S.vsq_ready, 1)
    e.link(dve.tensor_reduce(k.small[:, 32:48], k.vsq.rearrange("p t (g d) -> p t g d", d=64), AX.X, ALU.add))
    dve.tensor_scalar(k.small[:, 48:64], k.small[:, 32:48], 1.0 / HD, EPS, ALU.mult, ALU.add).then_inc(S.vms_ready, 1)
    dve.wait_ge(S.vstd_ready, 1)
    e.link(dve.reciprocal(k.small[:, 80:96], k.small[:, 64:80]))
    for t in range(NT1):
        v = k.tok[:, t, 2, 256:512].rearrange("p (g d) -> p g d", d=64)
        ins = dve.tensor_tensor(v, v, k.small[:, 80 + 4 * t:84 + 4 * t].unsqueeze(2).broadcast_to([P, 4, 64]), ALU.mult)
    ins.then_inc(S.v_ready, 1)
    b = cols(SM, k.sm, "gm_b")
    for g in range(4):
        dve.wait_ge(S.sv_ps, g // 2 * 2 + 2)
        dve.scalar_tensor_tensor(k.mix[:, :, 768 + 64 * g:832 + 64 * g],
                                 k.ps[:, 4 + g // 2, (g % 2) * 256:(g % 2) * 256 + 256].rearrange("p (t d) -> p t d", d=64),
                                 b[:, g:g + 1], k.tok[:, :, 2, 64 * g:64 * g + 64], ALU.add, ALU.mult)
    dve.wait_ge(S.kn_std, 1)
    e.link(dve.reciprocal(k.kcr[:, 0:N_CMP], k.kcstd[:, 0:N_CMP]))
    e.link(dve.scalar_tensor_tensor(k.kc[:, 0:N_CMP], k.ps[:, 1, 0:N_CMP], k.gains[:, 1:2], k.kcr[:, 0:N_CMP],
                                    ALU.mult, ALU.mult))


def retention_pe(k, e, slot):
    pe, S = e.eng, k.S

    def values(h):
        pe.wait_ge(S.st_ready, 4 * (h + 1))
        if h >= 2:
            pe.wait_ge(S.o_taken, h - 1)
        for i in range(NT1):
            for j in range(i + 1):
                last = pe.matmul(k.ps[:, 4 + h % 2, 64 * i:64 * i + 64], k.st(h, j)[:, (i - j) * P:(i - j + 1) * P],
                                 k.tok[:, j, 0, 64 * h:64 * h + 64], start=j == 0, stop=j == i)
        last.then_inc(S.o_ps, 1)

    for h in range(N_RET):
        rows = slice(64 * (h % 2), 64 * (h % 2) + 64)
        for j in range(NT1):
            n = 4 * h + j
            if n >= 4:
                pe.wait_ge(S.st_ready, n - 3)
            pe.matmul(k.ps[:, n % 4, 0:(4 - j) * P], k.tt[rows, 3 + h // 2, j * P:(j + 1) * P],
                      k.tt[rows, h // 2, j * P:SEQ], start=True, stop=True).then_inc(S.st_ps, 1)
        if h:
            values(h - 1)
    values(N_RET - 1)


def retention_act(k, e, _):
    act, S = e.eng, k.S
    for h in range(N_RET):
        act.wait_ge(S.o_ps, h + 1)
        act.activation(k.mix[:, :, 64 * h:64 * h + 64], k.ps[:, 4 + h % 2, 0:256].rearrange("p (t d) -> p t d", d=64),
                       ACT.Copy).then_inc(S.o_taken, 1)
    act.wait_ge(S.o_taken, N_RET)
    act.activation(k.osq, k.mix[:, :, 0:384], ACT.Square).then_inc(S.osq_ready, 1)
    act.wait_ge(S.oms_ready, 1)
    act.activation(k.small[:, 80:104], k.small[:, 56:80], ACT.Sqrt).then_inc(S.ostd_ready, 1)


def retention_dve(k, e, _):
    dve, S = e.eng, k.S
    decay = cols(C1, k.c1, "decay", 6, 512)
    for h in range(N_RET):
        for j in range(NT1):
            n = 4 * h + j
            dve.wait_ge(S.st_ps, n + 1)
            if h >= 2 and j == 0:
                dve.wait_ge(S.o_ps, h - 1)
            m = (4 - j) * P
            dve.tensor_tensor(k.st(h, j)[:, 0:m], k.ps[:, n % 4, 0:m], decay[:, h, 0:m], ALU.mult).then_inc(S.st_ready, 1)
    dve.wait_ge(S.osq_ready, 1)
    e.link(dve.tensor_reduce(k.small[:, 32:56], k.osq.rearrange("p t (h d) -> p t h d", d=64), AX.X, ALU.add))
    dve.tensor_scalar(k.small[:, 56:80], k.small[:, 32:56], 1.0 / HD, EPS, ALU.mult, ALU.add).then_inc(S.oms_ready, 1)
    dve.wait_ge(S.ostd_ready, 1)
    e.link(dve.reciprocal(k.small[:, 104:128], k.small[:, 80:104]))
    for t in range(NT1):
        o = k.mix[:, t, 0:384].rearrange("p (h d) -> p h d", d=64)
        e.link(dve.tensor_tensor(o, o, k.small[:, 104 + 6 * t:110 + 6 * t].unsqueeze(2).broadcast_to([P, 6, 64]), ALU.mult))
        dve.tensor_tensor(k.mix[:, t, 0:384], k.mix[:, t, 0:384], k.tok[:, t, 1, 0:384], ALU.mult)


UNITS = [(h, i, br) for h in range(N_NSA) for i in range(NT1) for br in range(3)]


def unit_keys(u):
    h, i, br = UNITS[u]
    return N_CMP if br == 0 else (i + 1) * P


def nsa_pe(k, e, slot):
    pe, S = e.eng, k.S
    n = len(UNITS)
    for u in range(n + 3):
        if u < n:
            h, i, br = UNITS[u]
            rows = slice(64 * (h // 3), 64 * (h // 3) + 64)
            if u >= 3:
                pe.wait_ge(S.s_ready, u - 2)
            keys = k.kc[rows, 0:N_CMP] if br == 0 else k.tt[rows, 10 + br, 0:(i + 1) * P]
            pe.matmul(k.ps[:, u % 3, 0:unit_keys(u)], k.tt[rows, 6 + h % 3, i * P:(i + 1) * P], keys,
                      start=True, stop=True).then_inc(S.s_ps, 1)
        if 2 <= u <= n + 1:
            v = u - 2
            pe.wait_ge(S.p_ready, v + 1)
            if v >= 2:
                pe.wait_ge(S.pt_ready, v - 1)
            nk = unit_keys(v)
            for j in range(0, nk, P):
                m = min(P, nk - j)
                last = pe.transpose(k.ps[0:m, 3 + v % 2, j:j + P], k.pexp(v)[:, j:j + m], k.ident)
            last.then_inc(S.pt_ps, 1)
        if u >= 3:
            v = u - 3
            h, i, br = UNITS[v]
            pe.wait_ge(S.pt_ready, v + 1)
            if v >= 2:
                pe.wait_ge(S.ov_taken, v - 1)
            out = k.ps[:, 5 + v % 2, 0:64]
            g = h // 3
            if br == 0:
                last = pe.matmul(out, k.ptr(v)[0:N_CMP, 0:P], k.vc[0:N_CMP, 64 * g:64 * g + 64], start=True, stop=True)
            else:
                for j in range(i + 1):
                    last = pe.matmul(out, k.ptr(v)[:, j * P:(j + 1) * P],
                                     k.tok[:, j, br - 1, 384 + 64 * g:448 + 64 * g], start=j == 0, stop=j == i)
            last.then_inc(S.ov_ps, 1)


def nsa_act(k, e, _):
    act, S = e.eng, k.S
    n = len(UNITS)
    for u in range(n + 2):
        if u < n:
            nk = unit_keys(u)
            act.wait_ge(S.s_ready, u + 1)
            if u >= 3:
                act.wait_ge(S.pt_ps, u - 2)
            act.activation(k.pexp(u)[:, 0:nk], k.sneg(u)[:, 0:nk], ACT.Exp, bias=k.nmax[:, u:u + 1], scale=-1.0,
                           accum_out=k.psums[:, u:u + 1]).then_inc(S.p_ready, 1)
        if u >= 2:
            v = u - 2
            nk = unit_keys(v)
            act.wait_ge(S.pt_ps, v + 1)
            if v >= 3:
                act.wait_ge(S.ov_ps, v - 2)
            if nk == N_CMP:
                act.activation(k.ptr(v)[0:N_CMP, 0:P], k.ps[0:N_CMP, 3 + v % 2, 0:P], ACT.Copy).then_inc(S.pt_ready, 1)
            else:
                act.activation(k.ptr(v)[:, 0:nk], k.ps[:, 3 + v % 2, 0:nk], ACT.Copy).then_inc(S.pt_ready, 1)


def nsa_dve(k, e, _):
    dve, S = e.eng, k.S
    n = len(UNITS)
    for u in range(n + 4):
        if u < n:
            h, i, br = UNITS[u]
            nk = unit_keys(u)
            dve.wait_ge(S.s_ps, u + 1)
            if u >= 3:
                dve.wait_ge(S.p_ready, u - 2)
            bias = k.biasc[:, h, i, 0:N_CMP] if br == 0 else k.bias[:, h, 512 - nk:512]
            dve.tensor_tensor_reduce(out=k.sneg(u)[:, 0:nk], in0=k.ps[:, u % 3, 0:nk], in1=bias, scale=-1.0,
                                     scalar=3e38, op0=ALU.add, op1=ALU.min, accum_out=k.nmax[:, u:u + 1]).then_inc(S.s_ready, 1)
        if u >= 4:
            v = u - 4
            h, i, br = UNITS[v]
            dve.wait_ge(S.p_ready, v + 1)
            w = k.small[:, 32 + v % 8:33 + v % 8]
            e.link(dve.reciprocal(w, k.psums[:, v:v + 1]))
            e.link(dve.tensor_tensor(w, w, k.gates[:, i, 3 * h + br:3 * h + br + 1], ALU.mult))
            dve.wait_ge(S.ov_ps, v + 1)
            o = k.mix[:, i, 384 + 64 * h:448 + 64 * h]
            ps = k.ps[:, 5 + v % 2, 0:64]
            if br == 0:
                ins = dve.tensor_scalar(o, ps, w, None, ALU.mult)
            else:
                ins = dve.scalar_tensor_tensor(o, ps, w, o, ALU.mult, ALU.add)
            ins.then_inc(S.ov_taken, 1)
            dve.wait_ge(S.ov_taken, v + 1)


def mixt_pe(k, e, slot):
    transposes_pe(k, e.eng, k.mix, NT1)


def mixt_act(k, e, _):
    transposes_take(k, e, (k.x1h, k.x1l), NT1, 1)


def mixt_dve(k, e, _):
    transposes_take(k, e, (k.x1h, k.x1l), NT1, 0)


def rows_pe(k, e, slot, xT, nt, chunks):
    pe, S = e.eng, k.S
    for c in range(chunks):
        for part in range(2):
            w = take_split(k, pe, slot, 2 * c + part)
            for t in range(nt):
                n = c * nt + t
                if part == 0 and n >= 8:
                    pe.wait_ge(S.mm_taken, n - 7)
                for i in range(4):
                    last = product3(k, pe, k.ps[:, n % 8, :], pair(xT, 4 * part + i, slice(t * P, (t + 1) * P)),
                                    pair(w, slice(512 * i, 512 * i + 512)), part == 0 and i == 0, part == 1 and i == 3)
                if part == 1:
                    last.then_inc(S.mm_done, 1)
            piece_used(k, slot)


def rows_split_dve(k, e):
    for n in range(4):
        split_dve(k, e, n)


def out_pe(k, e, slot):
    rows_pe(k, e, slot, (k.x1h, k.x1l), NT1, 2)


def out_act(k, e, _):
    pass


def out_dve(k, e, _):
    rows_split_dve(k, e)
    add_dve(k, e, range(2 * NT1))


def add_dve(k, e, jobs, bank_of=lambda n: n):
    dve, S = e.eng, k.S
    for n in jobs:
        c, t = divmod(n, NT1)
        dve.wait_ge(S.mm_done, n + 1)
        xs = k.x1[:, t, 512 * c:512 * c + 512]
        dve.tensor_tensor(xs, k.ps[:, bank_of(n), :], xs, ALU.add).then_inc(S.mm_taken, 1)


def ffn_pe(k, e, slot, xT, hs, nt):
    pe, S = e.eng, k.S
    buffers = hs.shape[1]
    for f in range(FT):
        w = take_split(k, pe, slot, f)
        if f >= 2:
            pe.wait_ge(S.hid_taken, f - 1)
        for half in range(2):
            for kt in range(KT):
                c = 1024 * half + kt * P
                last = product3(k, pe, k.ps[:, 2 * (f % 2) + half, 0:nt * P], pair(w, slice(c, c + P)), pair(xT, kt),
                                kt == 0, kt == KT - 1)
        piece_used(k, slot)
        last.then_inc(S.gate_ps, 1)
    for c in range(2):
        for part in range(6):
            w = take_split(k, pe, slot, FT + 6 * c + part)
            for i in range(min(4, FT - 4 * part)):
                f = 4 * part + i
                j = FT * c + f
                pe.wait_ge(S.hs_ready, j + 1)
                for t in range(nt):
                    n = c * nt + t
                    if f == 0 and c == 1:
                        pe.wait_ge(S.hid_taken, FT)
                    last = product3(k, pe, k.ps[:, 4 * (1 - c) + t, :],
                                    pair((hs[:, j % buffers, 0], hs[:, j % buffers, 1]), slice(t * P, (t + 1) * P)),
                                    pair(w, slice(512 * i, 512 * i + 512)), f == 0, f == FT - 1)
                    if f == FT - 1:
                        last.then_inc(S.mm_done, 1)
                k.later.append(S.hs_used)
            piece_used(k, slot)


def ffn_act(k, e, silu, hid, hs, nt):
    act, S = e.eng, k.S
    buffers = hs.shape[1]
    for f in range(FT):
        act.wait_ge(S.gate_ps, f + 1)
        if f >= 2:
            act.wait_ge(S.hid_taken, f - 1)
        act.activation(silu[:, f % 2, 0:nt * P], k.ps[:, 2 * (f % 2), 0:nt * P], ACT.Silu).then_inc(S.silu_ready, 1)
    for j in range(2 * FT):
        act.wait_ge(S.hid_taken, j % FT + 1)
        if j >= buffers:
            act.wait_ge(S.hs_used, j - buffers + 1)
        act.activation(hs[:, j % buffers, 0, 0:nt * P], hid[:, j % FT, 0:nt * P],
                       ACT.Copy).then_inc(S.hs_hi_ready, 1)


def ffn_dve(k, e, silu, hid, hs, nt, finish):
    dve, S = e.eng, k.S
    buffers = hs.shape[1]
    split_dve(k, e, 0)
    for f in range(FT):
        split_dve(k, e, f + 1)
        dve.wait_ge(S.silu_ready, f + 1)
        dve.tensor_tensor(hid[:, f, 0:nt * P], k.ps[:, 2 * (f % 2) + 1, 0:nt * P], silu[:, f % 2, 0:nt * P],
                          ALU.mult).then_inc(S.hid_taken, 1)
    for c in range(2):
        for f in range(FT):
            j = FT * c + f
            hi, lo = hs[:, j % buffers, 0, 0:nt * P], hs[:, j % buffers, 1, 0:nt * P]
            dve.wait_ge(S.hs_hi_ready, j + 1)
            dve.tensor_tensor(lo, hid[:, f, 0:nt * P], hi.bitcast(F32), ALU.subtract).then_inc(S.hs_ready, 1)
            n = FT + 6 * c + f // 4 + 1
            if n < FT + 12:
                if f % 4 == 1:
                    piece = split_dve(k, e, n, with_lo=False)
                if f % 4 == 2 or f == FT - 1:
                    split_lo_dve(k, e, n, piece)
            if c == 1 and f == 1:
                finish(range(0, nt))
    finish(range(nt, 2 * nt))


def ffn1_pe(k, e, slot):
    ffn_pe(k, e, slot, k.both(NT1), k.hs, NT1)


def ffn1_act(k, e, _):
    ffn_act(k, e, k.silu, k.hid, k.hs, NT1)


def ffn1_dve(k, e, _):
    ffn_dve(k, e, k.silu, k.hid, k.hs, NT1, lambda jobs: add_dve(k, e, jobs, lambda n: (n + 4) % 8))


def place2(k, arena, arena_end, x_mem):
    lasting = Arena(arena, arena_end - 4 * D - 8 * KT - 1024 - N_C2, arena_end)
    work_end = lasting.at
    k.gt = lasting.take(4, D)
    without_gates = lasting.at
    k.modcol = lasting.take(4, KT, 2)
    k.rt = lasting.take(2, 512)
    k.c2 = lasting.take(N_C2)
    a = Arena(arena, 0, work_end)
    k.mods = a.take(6 * D)
    k.adab = a.take(6 * D)
    k.cc = a.take(KT, 2)
    k.cs = a.take(KT, 2)
    k.sel = a.take(2, P)
    a = Arena(arena, 0, without_gates)
    k.qT, k.kT = a.take(HALF, NT2 * P), a.take(HALF, NT2 * P)
    k.kc_, k.vc_ = a.take(NT2, HALF, P), a.take(NT2, HALF, P)
    k.oacc = a.take(NT2, HALF, P)
    k.dn = a.take(N_DN)
    k.stat = a.take(12, NT2 * 8)
    k.state = [a.take(HALF, P) for _ in range(2)]
    k.wab = k.hs[:, 0, 0, 0:P], k.hs[:, 0, 1, 0:P]
    k.ab = k.oacc.rearrange("p a b c -> p (a b c)")[:, 0:NT2 * P]
    left = a.at
    b = Arena(x_mem, 0, NT2 * D)
    k.raw = [b.take(776) for _ in range(2)]
    k.conv = [b.take(768) for _ in range(2)]
    k.sqr = [b.take(768) for _ in range(2)]
    b2 = Arena(arena, left, without_gates)
    k.vT = [b2.take(768) for _ in range(4)]
    b = Arena(x_mem, 0, NT2 * D)
    b2 = Arena(arena, left, without_gates)
    names = "low qg up a1 a2 b1 b2 x t".split()
    k.buf = [{}, {}]
    for d in range(2):
        for n in names:
            k.buf[d][n] = (b if b.at + 512 <= b.end else b2).take(HALF, P)
    a = Arena(arena, 0, work_end)
    k.z = a.take(NT2, D)
    k.omix = a.take(NT2, D)
    k.osq2 = a.take(2, D)
    k.lnrow = Arena(arena, 0, work_end).take(2, D)
    a = Arena(arena, 4 * SEQ, work_end)
    k.hid2 = a.take(FT, SEQ)
    k.silu2 = a.take(2, SEQ)
    a = Arena(arena, 0, work_end)
    k.aq = a.take(HEADS, SEQ)
    k.ak = a.take(HEADS, NT2 * P)
    k.av = a.take(NT2, D)
    k.amix = k.mix
    k.c3 = a.take(N_C3)
    k.rotary = k.x[:, 5, :].rearrange("p (a b) -> p a b", b=512)
    k.ra = k.x[:, 4, 0:512]
    k.rb = k.x[:, 4, 512:1024]
    flat = k.back_xt
    k.ap = [flat[:, 1536 * i:1536 * i + 1536].rearrange("p (c n) -> p c n", n=768) for i in range(2)]
    k.apt = [flat[:, 3072 + 768 * i:3840 + 768 * i] for i in range(2)]
    k.amax, k.asum, k.arec = flat[:, 4608:4672], flat[:, 4672:4736], flat[:, 4736:4800]
    k.amx2, k.afac = flat[:, 4800:4864], flat[:, 4864:4928]
    k.lamt = a.take(140)


LAMBDA_INIT = 0.8 - 0.6 * math.exp(-0.3 * 1)


def ada_pe(k, e, slot, _):
    pe, S = e.eng, k.S
    pe.wait_ge(S.cond_ready, 1)
    for c in range(12):
        if c >= 4:
            pe.wait_ge(S.mm_taken, c - 3)
        for part in range(2):
            w = take_raw(k, pe, slot).rearrange("p (a b) -> p a b", b=512)
            for i in range(4):
                kt = 4 * part + i
                last = pe.matmul(k.ps[0:2, c % 4, :], k.cs[:, kt, :], w[:, i, :], start=kt == 0, stop=kt == KT - 1)
                if i == 0:
                    signal_later(k, last)
            piece_used(k, slot, split=False)
        last.then_inc(S.mm_done, 1)
    pe.wait_ge(S.mm_taken, 12)
    for i, w in enumerate((0, 1, 3, 4)):
        for kt in range(KT):
            at = w * D + kt * P
            last = pe.transpose(k.ps[:, 4, (i * KT + kt) * 2:(i * KT + kt) * 2 + 2], k.mods[0:2, at:at + P],
                                k.ident[0:2, 0:2])
    last.then_inc(S.tr_done, 1)
    for n in range(8):
        w, src, half = (2, 5)[n // 4], n // 2 % 2, n % 2
        if n >= 3:
            pe.wait_ge(S.aux_taken, n - 2)
        at = w * D + 512 * half
        pe.matmul(k.ps[:, 5 + n % 3, :], k.sel[0:2, src, :], k.mods[0:2, at:at + 512], start=True,
                  stop=True).then_inc(S.aux_done, 1)


def ada_act(k, e, layer):
    act, S, T = e.eng, k.S, k.T
    act.dma_start(k.cc, T["cond"]).then_inc(S.loaded, 16)
    act.dma_start(k.adab[0:2, :], T["ada_b"][layer]).then_inc(S.ada_b_loaded, 16)
    act.dma_start(k.sel[0:2, :, :], T["sel"]).then_inc(S.loaded, 16)
    if layer == 0:
        act.dma_start(k.x[:, 4:6, :], T["ctx"].rearrange("(t p) d -> p t d", p=P)).then_inc(S.loaded, 16)
        act.dma_start(k.c2, T["c2"]).then_inc(S.loaded, 16)
    act.wait_ge(S.loaded, 64 if layer == 0 else 32)
    act.activation(k.cs, k.cc, ACT.Silu).then_inc(S.cond_ready, 1)
    for n in range(8):
        act.wait_ge(S.aux_done, n + 1)
        act.activation(k.gt[:, n // 2, 512 * (n % 2):512 * (n % 2) + 512], k.ps[:, 5 + n % 3, :],
                       ACT.Copy).then_inc(S.aux_taken, 1)


def ada_dve(k, e, _):
    dve, S = e.eng, k.S
    k.dve_piece += 24
    dve.wait_ge(S.ada_b_loaded, 16)
    for c in range(12):
        dve.wait_ge(S.mm_done, c + 1)
        dve.tensor_tensor(k.mods[0:2, 512 * c:512 * c + 512], k.ps[0:2, c % 4, :],
                          k.adab[0:2, 512 * c:512 * c + 512], ALU.add).then_inc(S.mm_taken, 1)
    dve.wait_ge(S.tr_done, 1)
    cols_ = k.ps[:, 4, 0:64].rearrange("p (w a b) -> p w a b", a=KT, b=2)
    for i in range(4):
        dve.tensor_scalar(k.modcol[:, i, :, :], cols_[:, i, :, :], float(i % 2), None, ALU.add)


def modt_pe(k, e, slot, arg):
    which, nt = arg
    transposes_pe(k, e.eng, k.x, nt)


def modt_take(k, e, arg, turn):
    which, nt = arg
    transposes_take(k, e, k.both(nt), nt, turn,
                    scale=lambda kt, t0: k.modcol[:, 2 * which + 1, kt, t0 // 4:t0 // 4 + 1],
                    bias=lambda kt, t0: k.modcol[:, 2 * which, kt, t0 // 4:t0 // 4 + 1])


def modt_act(k, e, arg):
    modt_take(k, e, arg, 1)


def modt_dve(k, e, arg):
    modt_take(k, e, arg, 0)


def modt_pool(k, e, arg):
    transposes_pool(k, e, k.both(arg[1]), arg[1])


def nothing_pe(k, e, slot, _):
    pass


def nothing(k, e, _):
    pass


def park_act(k, e, arg):
    act, S, T = e.eng, k.S, k.T
    act.dma_start(T["x_park"], k.x).then_inc(S.parked, 16)
    act.dma_start(T["gt_park"], k.gt).then_inc(S.parked, 16)
    modt_act(k, e, arg)


G_, BETA, PRE, TOT, EPRE, ETOT, NBE, EKD, NBETA, TA, TB, TC = range(12)


def st_(k, i):
    return k.stat[:, i, :].rearrange("p (t c) -> p t c", c=8)


def gates_pe(k, e, slot, _):
    pe, S = e.eng, k.S
    pe.wait_ge(S.loaded, 16)
    pe.wait_ge(S.hs_ready, 1)
    for s, (at, m, _) in enumerate(SEGS):
        for kt in range(KT):
            last = product3(k, pe, k.ps[0:16, 2 + s, 0:m], pair(k.wab, slice(16 * kt, 16 * kt + 16)),
                            pair((k.xTh, k.xTl), kt, slice(at, at + m)), kt == 0, kt == KT - 1)
    last.then_inc(S.stat_done, 1)
    pe.wait_ge(S.tok_taken, 1)
    for t in range(NT2):
        last = pe.transpose(k.ps[:, 0, t * 16:t * 16 + 16], k.ab[0:16, t * P:(t + 1) * P], k.ident[0:16, 0:16])
    last.then_inc(S.ab_ps, 1)
    pe.wait_ge(S.log_decay_ready, 1)
    g = st_(k, G_)
    for d in range(2):
        pe.matmul(k.ps[:, 1, 24 * d:24 * d + 24], cols(C2, k.c2, "tri", 2, P)[:, d, :], g[:, :, 4 * d:4 * d + 4],
                  start=True, stop=True)
    pe.matmul(k.ps[:, 1, 48:96], k.ones, g[:, :, :], start=True, stop=True).then_inc(S.prefix_ps, 1)


def gates_act(k, e, _):
    act, S = e.eng, k.S
    half = k.half
    act.dma_start(k.dn, k.T["dn"][bass.ds(half, 1)].rearrange("a p n -> (a p) n")).then_inc(S.loaded, 16)
    act.wait_ge(S.loaded, 16)
    act.wait_ge(S.stat_done, 1)
    act.activation(k.ab[0:16, :], k.ps[0:16, 2:4, :].rearrange("p a b -> p (a b)")[:, 0:NT2 * P],
                   ACT.Copy).then_inc(S.tok_taken, 1)
    e.link(act.activation(k.small[:, 0:8], cols(DN, k.dn, "alog"), ACT.Exp))
    act.wait_ge(S.neg_abs_ready, 1)
    e.link(act.activation(k.stat[:, TB, :], k.stat[:, TB, :], ACT.Exp))
    act.activation(k.stat[:, TB, :], k.stat[:, TB, :], ACT.Ln, bias=k.ones[:, 0:1]).then_inc(S.softplus_ready, 1)
    act.wait_ge(S.ab_read, 1)
    act.activation(st_(k, BETA), k.ps[:, 0, 0:96].rearrange("p (t c) -> p t c", c=16)[:, :, 8:16],
                   ACT.Sigmoid).then_inc(S.softplus_ready, 1)
    act.wait_ge(S.prefix_ready, 1)
    act.activation(k.stat[:, EPRE, :], k.stat[:, PRE, :], ACT.Exp)
    act.activation(k.stat[:, ETOT, :], k.stat[:, TOT, :], ACT.Exp)
    act.activation(k.stat[:, EKD, :], k.stat[:, TA, :], ACT.Exp).then_inc(S.exps_ready, 1)
    act.wait_ge(S.parked, 32)


def gates_dve(k, e, _):
    dve, S = e.eng, k.S
    dve.wait_ge(S.loaded, 16)
    wab = cols(DN, k.dn, "wab")
    e.link(dve.tensor_copy(k.wab[0], wab))
    dve.tensor_tensor(k.wab[1], wab, k.wab[0].bitcast(F32), ALU.subtract).then_inc(S.hs_ready, 1)
    dve.wait_ge(S.ab_ps, 1)
    y = st_(k, TA)
    dt = cols(DN, k.dn, "dt").unsqueeze(1).broadcast_to([P, NT2, 8])
    ins = dve.tensor_tensor(y, k.ps[:, 0, 0:96].rearrange("p (t c) -> p t c", c=16)[:, :, 0:8], dt, ALU.add)
    ins.then_inc(S.ab_read, 1)
    dve.wait_ge(S.ab_read, 1)
    e.link(dve.tensor_scalar(k.stat[:, TC, :], k.stat[:, TA, :], -1.0, None, ALU.mult))
    dve.tensor_tensor(k.stat[:, TB, :], k.stat[:, TC, :], k.stat[:, TA, :], ALU.min).then_inc(S.neg_abs_ready, 1)
    dve.wait_ge(S.softplus_ready, 1)
    e.link(dve.scalar_tensor_tensor(k.stat[:, TC, :], k.stat[:, TA, :], 0.0, k.stat[:, TB, :], ALU.max, ALU.add))
    e.link(dve.tensor_scalar(k.stat[:, TC, :], k.stat[:, TC, :], -1.0, None, ALU.mult))
    dve.tensor_tensor(st_(k, G_), st_(k, TC), k.small[:, 0:8].unsqueeze(1).broadcast_to([P, NT2, 8]),
                      ALU.mult).then_inc(S.log_decay_ready, 1)
    dve.wait_ge(S.prefix_ps, 1)
    for d in range(2):
        e.link(dve.tensor_copy(st_(k, PRE)[:, :, 4 * d:4 * d + 4],
                               k.ps[:, 1, 24 * d:24 * d + 24].rearrange("p (t c) -> p t c", c=4)))
    e.link(dve.tensor_copy(k.stat[:, TOT, :], k.ps[:, 1, 48:96]))
    dve.tensor_tensor(k.stat[:, TA, :], k.stat[:, TOT, :], k.stat[:, PRE, :], ALU.subtract).then_inc(S.prefix_ready, 1)
    dve.wait_ge(S.softplus_ready, 2)
    e.link(dve.tensor_scalar(k.stat[:, NBETA, :], k.stat[:, BETA, :], -1.0, None, ALU.mult))
    dve.wait_ge(S.exps_ready, 1)
    dve.tensor_tensor(k.stat[:, NBE, :], k.stat[:, NBETA, :], k.stat[:, EPRE, :], ALU.mult)


N_QKV = 3 * HALF
SEGS = ((0, 512, 0), (512, 256, 516))


def qkv_dst(k, n):
    return (k.qT[:, n, :] if n < 4 else k.kT[:, n - 4, :]) if n < 8 else k.vT[n % 4]


def head_columns_pe(k, pe, slot, n, segs):
    S = k.S
    if n % 2 == 0:
        k.w = take_split(k, pe, slot, n // 2)
    if n >= 2:
        pe.wait_ge(S.mm_taken, n - 1)
    for s, (at, m, _) in enumerate(segs):
        for kt in range(KT):
            col = 256 * kt + P * (n % 2)
            last = product3(k, pe, k.ps[:, 2 * (n % 2) + s, 0:m], pair(k.w, slice(col, col + P)),
                            pair((k.xTh, k.xTl), kt, slice(at, at + m)), kt == 0, kt == KT - 1)
    if n % 2 == 1:
        piece_used(k, slot)
    last.then_inc(S.mm_done, 1)


def qkv_pe(k, e, slot, _):
    pe, S = e.eng, k.S
    for n in range(N_QKV + 6):
        if n < N_QKV:
            if 2 <= n <= 9:
                pe.wait_ge(S.head_ms_ready, n - 1)
            head_columns_pe(k, pe, slot, n, SEGS)
        if 1 <= n <= 8:
            v = n - 1
            pe.wait_ge(S.sq_ready, v + 1)
            for t in range(NT2):
                last = pe.matmul(qkv_sums(k, v)[:, t:t + 1], k.sqr[v % 2][:, t * P:(t + 1) * P], k.ones[:, 0:1],
                                 start=True, stop=True)
            last.then_inc(S.stat_done, 1)
        if 5 <= n <= 12:
            v = n - 5
            pe.wait_ge(S.nstd_ready, v // 4 + 1)
            if v >= 1:
                pe.wait_ge(S.qk_normed, v)
            for t in range(NT2):
                last = pe.matmul(k.ps[:, 4 + t // 4, (t % 4) * P:(t % 4) * P + P],
                                 qkv_factors(k, v)[:, t:t + 1].broadcast_to([P, P]), k.ident, start=True, stop=True)
            last.then_inc(S.prefix_ps, 1)
        if n >= 10:
            v = n - 6
            pe.wait_ge(S.qk_normed if v < 8 else S.qkv_silu, v + 1)
            if v >= 5:
                pe.wait_ge(S.tr_taken_act, v - 4)
            for t in range(NT2):
                last = pe.transpose(k.ps[:, 6 + t // 4, (t % 4) * P:(t % 4) * P + P],
                                    qkv_dst(k, v)[:, t * P:(t + 1) * P], k.ident)
            last.then_inc(S.tr_done, 1)


def qkv_sums(k, v):
    return k.ps[:, 2 * (v % 2) + 1, 256:256 + NT2]


def qkv_factors(k, v):
    return k.small[:, 128 + NT2 * v:128 + NT2 * (v + 1)]


def group_factors(k, g):
    return k.small[:, 128 + HALF * NT2 * g:128 + HALF * NT2 * (g + 1)]


def qkv_act(k, e, _):
    act, S = e.eng, k.S
    act.wait_ge(S.padding_ready, 2)
    for n in range(N_QKV + 6):
        if 1 <= n <= N_QKV:
            v = n - 1
            act.wait_ge(S.convolved, v + 1)
            act.activation(qkv_dst(k, v), k.conv[v % 2], ACT.Silu).then_inc(S.qkv_silu, 1)
            if v < 8:
                act.wait_ge(S.qkv_silu, v + 1)
                if v >= 2:
                    act.wait_ge(S.stat_done, v - 1)
                act.activation(k.sqr[v % 2], qkv_dst(k, v), ACT.Square).then_inc(S.sq_ready, 1)
        if n < N_QKV:
            act.wait_ge(S.mm_done, n + 1)
            if n >= 2:
                act.wait_ge(S.convolved, n - 1)
            for s, (at, m, to) in enumerate(SEGS):
                last = act.activation(k.raw[n % 2][:, to + 2:to + 2 + m], k.ps[:, 2 * (n % 2) + s, 0:m], ACT.Copy)
            last.then_inc(S.mm_taken, 1)
        if n in (4, 8):
            act.wait_ge(S.head_ms_ready, n)
            act.activation(group_factors(k, n // 4 - 1), group_factors(k, n // 4 - 1), ACT.Sqrt).then_inc(S.head_std_ready, 1)
        if n >= 10:
            v = n - 6
            dst = k.kc_ if v < 8 else k.vc_
            act.wait_ge(S.tr_done, v - 3)
            act.activation(dst[:, 0:4, v % 4, :], k.ps[:, 6, :].rearrange("p (t c) -> p t c", c=P), ACT.Copy)
            act.activation(dst[:, 4:6, v % 4, :], k.ps[:, 7, 0:256].rearrange("p (t c) -> p t c", c=P),
                           ACT.Copy).then_inc(S.tr_taken_act, 1)


def qkv_dve(k, e, _):
    dve, S = e.eng, k.S
    for i in range(2):
        dve.memset(k.raw[i], 0.0).then_inc(S.padding_ready, 1)
    taps = cols(DN, k.dn, "conv", 12, 5)
    for n in range(2):
        split_dve(k, e, n)
    for n in range(N_QKV + 1):
        if n % 2 == 0 and 2 <= n < N_QKV - 2:
            split_dve(k, e, n // 2 + 1)
        if 1 <= n <= 8:
            v = n - 1
            dve.wait_ge(S.stat_done, v + 1)
            dve.tensor_scalar(qkv_factors(k, v), qkv_sums(k, v), EPS, None, ALU.add).then_inc(S.head_ms_ready, 1)
        if n < N_QKV:
            dve.wait_ge(S.mm_taken, n + 1)
            if n >= 2:
                dve.wait_ge(S.qkv_silu, n - 1)
            raw, conv = k.raw[n % 2], k.conv[n % 2]
            for j in range(5):
                for at, m, to in SEGS:
                    if j == 0:
                        ins = dve.tensor_scalar(conv[:, at:at + m], raw[:, to:to + m], taps[:, n, 0:1], None, ALU.mult)
                    else:
                        ins = dve.scalar_tensor_tensor(conv[:, at:at + m], raw[:, to + j:to + j + m],
                                                       taps[:, n, j:j + 1], conv[:, at:at + m], ALU.mult, ALU.add)
                if j < 4:
                    e.link(ins)
            ins.then_inc(S.convolved, 1)
        if n in (4, 8):
            dve.wait_ge(S.head_std_ready, n // 4)
            dve.reciprocal(group_factors(k, n // 4 - 1), group_factors(k, n // 4 - 1)).then_inc(S.nstd_ready, 1)
        if 5 <= n <= 12:
            v = n - 5
            dve.wait_ge(S.prefix_ps, v + 1)
            x = qkv_dst(k, v)
            dve.scalar_tensor_tensor(x, x, P ** -0.5 if v < 4 else 1.0,
                                     k.ps[:, 4:6, :].rearrange("p a b -> p (a b)")[:, 0:NT2 * P], ALU.mult,
                                     ALU.mult).then_inc(S.qk_normed, 1)


PE_OPS = "gb kk qk ut l2 u2 x2 l4 u4 x4 l8 x8 w y0 z0 xx0 ww0 y1 z1 xx1 ww1 y2 ks xx2 vn o1 o2 su".split()
ACT_OPS = "gam gamt up l2c u2c l4c u4c l8c wc y0c z0c y1c z1c y2c vnc".split()
DVE_OPS = ("diff dlow low0 low qg x2a x4a x8a m0x x0a m0w w0a m1x x1a m1w w1a r1 m2x x2f rr t1 t2 s1 s2").split()
POOL_OPS = "dup ld ud x1 bv kd oa".split()
TAKEN = dict(gb="diff", kk="low0", qk="qg", ut="up", l2="l2c", u2="u2c", x2="x2a", l4="l4c", u4="u4c", x4="x4a",
             l8="l8c", x8="x8a", w="wc", y0="y0c", z0="z0c", xx0="m0x", ww0="m0w", y1="y1c", z1="z1c", xx1="m1x",
             ww1="m1w", y2="y2c", ks="r1", xx2="m2x", vn="vnc", o1="t1", o2="t2", su="s2")
CHUNKS = ((4, 5, 0, 1, 2, 3), (5, 4, 3, 2, 1, 0))
N_STEPS = NT2


def owner(k, name):
    for ops, sem in ((PE_OPS, k.S.pe_events), (ACT_OPS, k.S.act_events), (DVE_OPS, k.S.dve_events), (POOL_OPS, k.S.pool_events)):
        if name in ops:
            return ops, sem


def seen(k, eng, name, s, d):
    if s < 0:
        return
    ops, sem = owner(k, name)
    eng.wait_ge(sem, 2 * (s * len(ops) + ops.index(name)) + d + 1)


def bank(k, d, name):
    return k.ps[:, 4 * d + PE_OPS.index(name) % 4, :].rearrange("p (h c) -> p h c", c=P)


def scan_pe(k, e, slot, _):
    pe = e.eng
    tri = cols(C2, k.c2, "tri", 2, P)

    def product(s, name, lhs, rhs, *needs, transpose=False):
        i = PE_OPS.index(name)
        before = PE_OPS[i - 4]
        for d in range(2):
            seen(k, pe, TAKEN[before], s if i >= 4 else s - 1, d)
            for need in needs:
                seen(k, pe, need, s, d)
            for h in range(HALF):
                out = bank(k, d, name)[:, h, :]
                if transpose:
                    last = pe.transpose(out, lhs(d, h), k.ident)
                else:
                    last = pe.matmul(out, lhs(d, h), rhs(d, h), start=True, stop=True)
            last.then_inc(k.S.pe_events, 1)

    def b(name):
        return lambda d, h: k.buf[d][name][:, h, :]

    for s in range(N_STEPS):
        def chunk(t):
            return lambda d, h: t[:, h, CHUNKS[d][s] * P:(CHUNKS[d][s] + 1) * P]

        g = st_(k, G_)
        product(s, "gb", lambda d, h: g[:, CHUNKS[d][s], 4 * d + h:4 * d + h + 1].broadcast_to([P, P]),
                lambda d, h: tri[:, d, :])
        product(s, "kk", chunk(k.kT), chunk(k.kT))
        product(s, "qk", chunk(k.kT), chunk(k.qT))
        product(s, "ut", b("low"), None, "low", transpose=True)
        product(s, "l2", b("a2"), b("a1"), "ld", "ud")
        product(s, "u2", b("a1"), b("a2"))
        product(s, "x2", b("b1"), b("x"), "l2c", "x1")
        product(s, "l4", b("b2"), b("b1"), "u2c")
        product(s, "u4", b("b1"), b("b2"))
        product(s, "x4", b("a1"), b("x"), "l4c", "x2a")
        product(s, "l8", b("a2"), b("a1"), "u4c")
        product(s, "x8", b("b1"), b("x"), "l8c", "x4a")
        product(s, "w", b("x"), None, "x8a", transpose=True)
        for i in range(2):
            product(s, f"y{i}", b("low"), b("x"), f"x{i - 1}a" if i else "x8a")
            product(s, f"z{i}", b("up"), b("b2"), f"w{i - 1}a" if i else "wc")
            product(s, f"xx{i}", b("b2"), b("a1"), f"y{i}c")
            product(s, f"ww{i}", b("x"), b("a2"), f"z{i}c")
        product(s, "y2", b("low"), b("x"), "x1a")
        for d in range(2):
            seen(k, pe, "s2", s - 1, d)
        product(s, "ks", chunk(k.kT), lambda d, h: k.state[d][:, h, :])
        product(s, "xx2", b("b2"), b("a1"), "w1a", "y2c")
        product(s, "vn", b("x"), b("b1"), "x2f", "rr")
        product(s, "o1", chunk(k.qT), lambda d, h: k.state[d][:, h, :])
        product(s, "o2", b("qg"), b("a1"), "qg", "vnc")
        product(s, "su", b("a2"), b("a1"), "kd")


def scan_act(k, e, _):
    act = e.eng

    def op(s, name, dst, src, needs, func=ACT.Copy, **kw):
        for d in range(2):
            for need, back in needs:
                seen(k, act, need, s - back, d)
            act.activation(k.buf[d][dst], src(d), func, **kw).then_inc(k.S.act_events, 1)

    for s in range(N_STEPS):
        op(s, "gam", "low", lambda d: k.buf[d]["low"], [("dlow", 0)], ACT.Exp, scale=-1.0)
        op(s, "gamt", "qg", lambda d: k.buf[d]["qg"], [("dup", 0)], ACT.Exp)
        for name, dst, src in (("up", "up", "ut"), ("l2c", "b1", "l2"), ("u2c", "b2", "u2"), ("l4c", "a1", "l4"),
                               ("u4c", "a2", "u4"), ("l8c", "b1", "l8"), ("wc", "b2", "w"), ("y0c", "a1", "y0"),
                               ("z0c", "a2", "z0"), ("y1c", "a1", "y1"), ("z1c", "a2", "z1"), ("y2c", "a1", "y2"),
                               ("vnc", "a1", "vn")):
            op(s, name, dst, lambda d, src=src: bank(k, d, src), [(src, 0)])


def scan_dve(k, e, _):
    dve = e.eng
    gmask = cols(C2, k.c2, "gmask", 2, P)
    level = cols(C2, k.c2, "level", 3, P)
    for d in range(2):
        e.link(dve.memset(k.state[d], 0.0))

    def heads(v):
        return v.unsqueeze(1).broadcast_to([P, HALF, P])

    def op(s, name, f, *needs):
        for d in range(2):
            for need in needs:
                back = need.startswith("-")
                seen(k, dve, need.lstrip("-"), s - back, d)
            f(d).then_inc(k.S.dve_events, 1)

    for s in range(N_STEPS):
        def col(i, d):
            return st_(k, i)[:, CHUNKS[d][s], 4 * d:4 * d + 4].unsqueeze(2).broadcast_to([P, HALF, P])

        def tt(dst, a, b, o):
            return lambda d: dve.tensor_tensor(dst(d), a(d), b(d), o)

        def B(n):
            return lambda d: k.buf[d][n]

        def ps(n):
            return lambda d: bank(k, d, n)

        T = B("t")
        op(s, "diff", tt(T, ps("gb"), lambda d: col(PRE, d), ALU.subtract), "gb", "-oa")
        op(s, "dlow", tt(B("low"), T, lambda d: heads(gmask[:, d, :]), ALU.add), "diff", "-y2")
        op(s, "low0", tt(B("low"), ps("kk"), B("low"), ALU.mult), "kk", "gam")
        op(s, "low", tt(B("low"), B("low"), lambda d: col(NBETA, d), ALU.mult), "low0")
        op(s, "qg", tt(B("qg"), ps("qk"), B("qg"), ALU.mult), "qk", "gamt")
        op(s, "x2a", tt(B("x"), ps("x2"), B("x"), ALU.add), "x2")
        op(s, "x4a", tt(B("x"), ps("x4"), B("x"), ALU.add), "x4")
        op(s, "x8a", tt(B("x"), ps("x8"), B("x"), ALU.add), "x8")
        for i in range(2):
            op(s, f"m{i}x", tt(T, ps(f"xx{i}"), lambda d: heads(level[:, i, :]), ALU.mult), f"xx{i}", f"w{i-1}a" if i else "x8a")
            op(s, f"x{i}a", tt(B("x"), B("x"), T, ALU.add), f"m{i}x", f"ww{i}")
            op(s, f"m{i}w", tt(T, ps(f"ww{i}"), lambda d: heads(level[:, i, :]), ALU.mult), f"x{i}a", f"ww{i}")
            op(s, f"w{i}a", tt(B("b2"), B("b2"), T, ALU.add), f"m{i}w")
        op(s, "r1", tt(T, ps("ks"), lambda d: col(NBE, d), ALU.mult), "ks", "w1a")
        op(s, "m2x", tt(B("up"), ps("xx2"), lambda d: heads(level[:, 2, :]), ALU.mult), "xx2")
        op(s, "x2f", tt(B("x"), B("x"), B("up"), ALU.add), "m2x")
        op(s, "rr", tt(B("b1"), B("b1"), T, ALU.add), "r1", "bv")
        op(s, "t1", tt(T, ps("o1"), lambda d: col(EPRE, d), ALU.mult), "o1", "rr")
        op(s, "t2", tt(T, ps("o2"), T, ALU.add), "o2", "t1")
        op(s, "s1", tt(lambda d: k.state[d], lambda d: k.state[d], lambda d: col(ETOT, d), ALU.mult), "o1")
        op(s, "s2", tt(lambda d: k.state[d], ps("su"), lambda d: k.state[d], ALU.add), "su", "s1")


def scan_pool(k, e, _):
    pool = e.eng
    imask = cols(C2, k.c2, "imask", 2, P)
    b16 = cols(C2, k.c2, "b16")
    e.link(pool.memset(k.oacc, 0.0))

    def heads(v):
        return v.unsqueeze(1).broadcast_to([P, HALF, P])

    for s in range(N_STEPS):
        def col(i, d):
            return st_(k, i)[:, CHUNKS[d][s], 4 * d:4 * d + 4].unsqueeze(2).broadcast_to([P, HALF, P])

        def op(name, dst, a, b, o, *needs):
            for d in range(2):
                for need in needs:
                    back = need.startswith("-")
                    seen(k, pool, need.lstrip("-"), s - back, d)
                pool.tensor_tensor(dst(d), a(d), b(d), o).then_inc(k.S.pool_events, 1)

        def B(n):
            return lambda d: k.buf[d][n]

        op("dup", B("qg"), B("t"), lambda d: heads(imask[:, d, :]), ALU.add, "diff", "-o2")
        op("ld", B("a1"), B("low"), lambda d: heads(b16), ALU.mult, "low", "-su")
        op("ud", B("a2"), B("up"), lambda d: heads(b16), ALU.mult, "up")
        op("x1", B("x"), B("a2"), lambda d: heads(k.ident), ALU.add, "ud")
        op("bv", B("b1"), lambda d: k.vc_[:, CHUNKS[d][s], :, :], lambda d: col(BETA, d), ALU.mult, "x8")
        op("kd", B("a2"), lambda d: k.kc_[:, CHUNKS[d][s], :, :], lambda d: col(EKD, d), ALU.mult, "ww1")
        for d in range(2):
            seen(k, pool, "t2", s, d)
            if s or d:
                seen(k, pool, "oa", s - (d == 0), 1 - d)
            o = k.oacc[:, CHUNKS[d][s], :, :]
            pool.tensor_tensor(o, o, k.buf[d]["t"], ALU.add).then_inc(k.S.pool_events, 1)


def opark_act(k, e, _):
    act, S = e.eng, k.S
    act.dma_start(k.T["o_park"][bass.ds(k.half, 1)].rearrange("a p t n -> (a p) t n"),
                  k.oacc.rearrange("p t h c -> p t (h c)")).then_inc(S.spilled, 16)
    act.wait_ge(S.spilled, 16)


def head_norm_act(k, e, mix, nt, sq):
    act, S = e.eng, k.S
    for t in range(nt):
        if t >= 2:
            act.wait_ge(S.head_sq_summed, t - 1)
        act.activation(sq[:, t % 2, :], mix[:, t, :], ACT.Square).then_inc(S.head_sq_ready, 1)
    act.wait_ge(S.head_ms_ready, 1)
    act.activation(k.small[:, 64:64 + 8 * nt], k.small[:, 64:64 + 8 * nt], ACT.Sqrt).then_inc(S.head_std_ready, 1)


def head_norm_dve(k, e, mix, nt, sq, gain, factor, split=()):
    dve, S = e.eng, k.S
    for t in range(nt):
        dve.wait_ge(S.head_sq_ready, t + 1)
        dve.tensor_reduce(k.small[:, 8 * t:8 * t + 8], sq[:, t % 2, :].rearrange("p (h c) -> p h c", c=P), AX.X,
                          ALU.add).then_inc(S.head_sq_summed, 1)
    dve.wait_ge(S.head_sq_summed, nt)
    dve.tensor_scalar(k.small[:, 64:64 + 8 * nt], k.small[:, 0:8 * nt], 1.0 / P, EPS, ALU.mult, ALU.add).then_inc(S.head_ms_ready, 1)
    for n in split:
        split_dve(k, e, n)
    dve.wait_ge(S.head_std_ready, 1)
    e.link(dve.reciprocal(k.small[:, 0:8 * nt], k.small[:, 64:64 + 8 * nt]))
    if factor != 1.0:
        e.link(dve.tensor_scalar(k.small[:, 0:8 * nt], k.small[:, 0:8 * nt], factor, None, ALU.mult))
    for t in range(nt):
        o = mix[:, t, :].rearrange("p (h c) -> p h c", c=P)
        e.link(dve.tensor_tensor(o, o, k.small[:, 8 * t:8 * t + 8].unsqueeze(2).broadcast_to([P, 8, P]), ALU.mult))
        e.link(dve.tensor_tensor(o, o, gain.unsqueeze(1).broadcast_to([P, 8, P]), ALU.mult))


def z_pe(k, e, slot, _):
    rows_pe(k, e, slot, k.both(NT2), NT2, 2)


def z_act(k, e, _):
    act, S, T = e.eng, k.S, k.T
    act.dma_start(k.omix.rearrange("p t (h n) -> p t h n", h=2), T["o_park"].rearrange("h p t n -> p t h n")).then_inc(S.loaded, 16)
    act.dma_start(k.x, T["x_park"]).then_inc(S.x_back, 16)
    act.dma_start(k.gt, T["gt_park"]).then_inc(S.x_back, 16)
    act.wait_ge(S.loaded, 16)
    head_norm_act(k, e, k.omix, NT2, k.osq2)
    for n in range(2 * NT2):
        c, t = divmod(n, NT2)
        act.wait_ge(S.mm_done, n + 1)
        act.activation(k.z[:, t, 512 * c:512 * c + 512], k.ps[:, n % 8, :], ACT.Silu).then_inc(S.mm_taken, 1)


def z_dve(k, e, _):
    dve, S = e.eng, k.S
    for n in range(2):
        split_dve(k, e, n)
    head_norm_dve(k, e, k.omix, NT2, k.osq2, cols(C2, k.c2, "norm_g"), 1.0, split=(2, 3))
    for n in range(2 * NT2):
        c, t = divmod(n, NT2)
        dve.wait_ge(S.mm_taken, n + 1)
        o = k.omix[:, t, 512 * c:512 * c + 512]
        dve.tensor_tensor(o, o, k.z[:, t, 512 * c:512 * c + 512], ALU.mult)


def omt_pe(k, e, slot, _):
    transposes_pe(k, e.eng, k.omix, NT2)


def omt_act(k, e, _):
    transposes_take(k, e, k.both(NT2), NT2, 1)


def omt_dve(k, e, _):
    transposes_take(k, e, k.both(NT2), NT2, 0)


def proj_pe(k, e, slot, arg):
    rows_pe(k, e, slot, k.both(arg[1]), arg[1], 2)


def proj_dve(k, e, arg):
    rows_split_dve(k, e)
    e.eng.wait_ge(k.S.x_back, 32)
    gated_add_dve(k, e, range(2 * arg[1]), 0, 0, arg[1], lambda n: n % 8)


def gated_add_dve(k, e, jobs, gate, t0, nt, bank_of):
    dve, S = e.eng, k.S
    for n in jobs:
        c, t = n // nt, t0 + n % nt
        dve.wait_ge(S.mm_done, n + 1)
        row = k.gt[:, gate + t // 4, 512 * c:512 * c + 512]
        dve.tensor_tensor(k.rt[:, n % 2, :], k.ps[:, bank_of(n), :], row, ALU.mult).then_inc(S.mm_taken, 1)
        dve.wait_ge(S.mm_taken, n + 1)
        xs = k.x[:, t, 512 * c:512 * c + 512]
        dve.scalar_tensor_tensor(xs, xs, ALPHA, k.rt[:, n % 2, :], ALU.mult, ALU.add)


def ln_act(k, e, arg):
    act, S = e.eng, k.S
    index, nt = arg
    act.dma_start(k.lnrow, k.T["ln"][index:index + 1].broadcast_to([P, 2, D])).then_inc(S.loaded, 16)
    act.wait_ge(S.var_ready, 1)
    act.activation(k.small[:, 120:120 + nt], k.small[:, 112:112 + nt], ACT.Sqrt).then_inc(S.dev_ready, 1)
    act.wait_ge(S.loaded, 16)
    for t in range(nt):
        act.wait_ge(S.shift_ready, t + 1)
        act.activation(k.x[:, t, :], k.x[:, t, :], ACT.Identity, bias=k.small[:, 136 + t:137 + t],
                       scale=k.small[:, 128 + t:129 + t]).then_inc(S.centred, 1)


def ln_dve(k, e, arg):
    dve, S = e.eng, k.S
    index, nt = arg
    for t in range(nt):
        for i in range(2):
            ins = dve.bn_stats(k.small[:, 12 * t + 6 * i:12 * t + 6 * i + 6], k.x[:, t, 512 * i:512 * i + 512])
        e.link(ins)
        ins = dve.bn_aggr(k.small[:, 80 + 2 * t:82 + 2 * t], k.small[:, 12 * t:12 * t + 12])
    e.link(ins)
    var = k.small[:, 80:80 + 2 * nt].rearrange("p (t b) -> p t b", b=2)
    dve.tensor_scalar(k.small[:, 112:112 + nt], var[:, :, 1], LN_EPS, None, ALU.add).then_inc(S.var_ready, 1)
    dve.wait_ge(S.dev_ready, 1)
    e.link(dve.reciprocal(k.small[:, 128:128 + nt], k.small[:, 120:120 + nt]))
    for t in range(nt):
        dve.scalar_tensor_tensor(k.small[:, 136 + t:137 + t], k.small[:, 80 + 2 * t:81 + 2 * t], -1.0,
                                 k.small[:, 128 + t:129 + t], ALU.mult, ALU.mult).then_inc(S.shift_ready, 1)
    dve.wait_ge(S.loaded, 16)
    for t in range(nt):
        dve.wait_ge(S.centred, t + 1)
        e.link(dve.tensor_tensor(k.x[:, t, :], k.x[:, t, :], k.lnrow[:, 0, :], ALU.mult))
        dve.tensor_tensor(k.x[:, t, :], k.x[:, t, :], k.lnrow[:, 1, :], ALU.add)


def hidden_buffers(k, nt):
    return k.hs if nt > 2 else k.hs_short


def ffn2_pe(k, e, slot, arg):
    t0, nt, of = arg
    ffn_pe(k, e, slot, pair(k.both(of), slice(None), slice(t0 * P, (t0 + nt) * P)), hidden_buffers(k, nt), nt)


def ffn2_act(k, e, arg):
    ffn_act(k, e, k.silu2, k.hid2, hidden_buffers(k, arg[1]), arg[1])


def ffn2_dve(k, e, arg):
    t0, nt, _ = arg
    ffn_dve(k, e, k.silu2, k.hid2, hidden_buffers(k, nt), nt,
            lambda jobs: gated_add_dve(k, e, jobs, 2, t0, nt, lambda n: 4 * (1 - n // nt) + n % nt))


V_BANKS = (6, 7, 0, 1, 2, 3, 4, 5)


def dap_pe(k, e, slot, _):
    pe, S = e.eng, k.S
    for n in range(16):
        head_columns_pe(k, pe, slot, n, SEGS if n >= 8 else SEGS[:1])
        if n >= 1:
            da_rotate_pe(k, pe, n - 1)
    da_rotate_pe(k, pe, 15)
    for c in range(2):
        for part in range(2):
            w = take_split(k, pe, slot, 8 + 2 * c + part)
            for t in range(NT2):
                n = c * NT2 + t
                if part == 0 and n >= 8:
                    pe.wait_ge(S.tok_taken, n - 7)
                if part == 0 and n == 6:
                    pe.wait_ge(S.rot_taken, 16)
                for i in range(4):
                    last = product3(k, pe, k.ps[:, V_BANKS[n % 8], :],
                                    pair((k.xTh, k.xTl), 4 * part + i, slice(t * P, (t + 1) * P)),
                                    pair(w, slice(512 * i, 512 * i + 512)), part == 0 and i == 0, part == 1 and i == 3)
                if part == 1:
                    last.then_inc(S.tok_done, 1)
            piece_used(k, slot)


def da_dst(k, n):
    return k.aq[:, n, :] if n < 8 else k.ak[:, n - 8, :]


def da_rotate_pe(k, pe, n):
    S = k.S
    pe.wait_ge(S.mm_taken, n + 1)
    if n >= 2:
        pe.wait_ge(S.rot_taken, n - 1)
    pe.matmul(k.ps[:, 4 + n % 2, :], cols(C3, k.c3, "rot"), da_dst(k, n)[:, 0:512], start=True,
              stop=True).then_inc(S.stat_done, 1)


def dap_act(k, e, _):
    act, S, T = e.eng, k.S, k.T
    act.dma_start(k.c3, T["c3"]).then_inc(S.loaded, 16)
    act.dma_start(k.rotary, T["rotary"]).then_inc(S.loaded, 16)
    act.dma_start(k.lamt[:, 0:128].rearrange("p (a b) -> p a b", b=64), T["lam"][0:1].broadcast_to([P, 2, 64])).then_inc(S.lam_loaded, 16)
    act.dma_start(k.rb.rearrange("p (a b) -> p a b", b=64)[:, 0:2, :], T["lam"][1:2].broadcast_to([P, 2, 64])).then_inc(S.lam_loaded, 16)
    act.wait_ge(S.loaded, 32)
    for n in range(16):
        act.wait_ge(S.mm_done, n + 1)
        ins = act.activation(da_dst(k, n)[:, 0:512], k.ps[:, 2 * (n % 2), :], ACT.Copy)
        if n >= 8:
            ins = act.activation(da_dst(k, n)[:, 512:768], k.ps[:, 2 * (n % 2) + 1, 0:256], ACT.Copy)
        ins.then_inc(S.mm_taken, 1)
    for n in range(2 * NT2):
        c, t = divmod(n, NT2)
        act.wait_ge(S.tok_done, n + 1)
        act.activation(k.av[:, t, 512 * c:512 * c + 512], k.ps[:, V_BANKS[n % 8], :], ACT.Copy).then_inc(S.tok_taken, 1)
    act.wait_ge(S.lam_sums_ready, 1)
    act.activation(k.lamt[:, 130:132], k.lamt[:, 128:130], ACT.Exp).then_inc(S.lam_exps_ready, 1)


def dap_dve(k, e, _):
    dve, S = e.eng, k.S
    for n in range(2):
        split_dve(k, e, n)
    dve.wait_ge(S.lam_loaded, 32)
    lam = k.lamt[:, 0:128].rearrange("p (a b) -> p a b", b=64)
    e.link(dve.tensor_tensor(lam, lam, k.rb.rearrange("p (a b) -> p a b", b=64)[:, 0:2, :], ALU.mult))
    dve.tensor_reduce(k.lamt[:, 128:130], lam, AX.X, ALU.add).then_inc(S.lam_sums_ready, 1)
    for n in range(16):
        if n % 2 == 0 and n >= 2:
            split_dve(k, e, n // 2 + 1)
        x = da_dst(k, n)[:, 0:512]
        dve.wait_ge(S.stat_done, n + 1)
        e.link(dve.tensor_tensor(k.ra, x, k.rotary[:, 0, :], ALU.mult))
        dve.tensor_tensor(k.rb, k.ps[:, 4 + n % 2, :], k.rotary[:, 1, :], ALU.mult).then_inc(S.rot_taken, 1)
        dve.wait_ge(S.rot_taken, n + 1)
        e.link(dve.tensor_tensor(x, k.ra, k.rb, ALU.add))
    for n in range(9, 12):
        split_dve(k, e, n)
    dve.wait_ge(S.lam_exps_ready, 1)
    e.link(dve.tensor_tensor(k.lamt[:, 132:133], k.lamt[:, 131:132], k.lamt[:, 130:131], ALU.subtract))
    e.link(dve.tensor_scalar(k.lamt[:, 133:134], k.lamt[:, 132:133], -LAMBDA_INIT, None, ALU.add))


AUNITS = [(h, i) for h in range(HEADS) for i in range(NT1)]
KEYS = NT2 * P


def da_pe(k, e, slot, _):
    pe, S = e.eng, k.S
    for u in range(len(AUNITS) + 2):
        if u < len(AUNITS):
            h, i = AUNITS[u]
            for c in range(2):
                if u:
                    pe.wait_ge(S.p_ready, 2 * u - 1 + c)
                rows = slice(64 * c, 64 * c + 64)
                for s, (at, m, _) in enumerate(SEGS):
                    last = pe.matmul(k.ps[:, 2 * c + s, 0:m], k.aq[rows, h, i * P:(i + 1) * P],
                                     k.ak[rows, h, at:at + m], start=True, stop=True)
                last.then_inc(S.s_ps, 1)
        if 1 <= u <= len(AUNITS):
            v = u - 1
            pe.wait_ge(S.s_ready, v + 1)
            if v:
                pe.wait_ge(S.pt_ready, v)
            for j in range(NT2):
                last = pe.transpose(k.ps[:, 4 + j // 4, (j % 4) * P:(j % 4) * P + P],
                                    k.ap[v % 2][:, 0, j * P:(j + 1) * P], k.ident)
            last.then_inc(S.pt_ps, 1)
        if u >= 2:
            v = u - 2
            h, i = AUNITS[v]
            pe.wait_ge(S.pt_ready, v + 1)
            if v >= 2:
                pe.wait_ge(S.ov_taken, v - 1)
            for j in range(NT2):
                last = pe.matmul(k.ps[:, 6 + v % 2, 0:P], k.apt[v % 2][:, j * P:(j + 1) * P],
                                 k.av[:, j, h * P:(h + 1) * P], start=j == 0, stop=j == NT2 - 1)
            last.then_inc(S.ov_ps, 1)


def da_act(k, e, _):
    act, S = e.eng, k.S

    def exponentials(u, c):
        act.wait_ge(S.o_ps, 2 * u + c + 1)
        act.activation(k.ap[u % 2][:, c, :], k.ps[:, 2 * c:2 * c + 2, :].rearrange("p a b -> p (a b)")[:, 0:KEYS],
                       ACT.Exp, bias=k.amx2[:, 2 * u + c:2 * u + c + 1], scale=HD ** -0.5,
                       accum_out=k.asum[:, 2 * u + c:2 * u + c + 1]).then_inc(S.p_ready, 1)

    for u in range(len(AUNITS) + 1):
        if u < len(AUNITS):
            exponentials(u, 0)
        if u:
            v = u - 1
            act.wait_ge(S.pt_ps, v + 1)
            if v >= 2:
                act.wait_ge(S.ov_ps, v - 1)
            act.activation(k.apt[v % 2], k.ps[:, 4:6, :].rearrange("p a b -> p (a b)")[:, 0:KEYS],
                           ACT.Copy).then_inc(S.pt_ready, 1)
        if u < len(AUNITS):
            exponentials(u, 1)


def da_dve(k, e, _):
    dve, S = e.eng, k.S
    for u in range(len(AUNITS) + 3):
        if u < len(AUNITS):
            h, i = AUNITS[u]
            for c in range(2):
                at = 2 * u + c
                dve.wait_ge(S.s_ps, at + 1)
                e.link(dve.tensor_reduce(k.amax[:, at:at + 1],
                                         k.ps[:, 2 * c:2 * c + 2, :].rearrange("p a b -> p (a b)")[:, 0:KEYS], AX.X, ALU.max))
                dve.tensor_scalar(k.amx2[:, at:at + 1], k.amax[:, at:at + 1], -HD ** -0.5, None,
                                  ALU.mult).then_inc(S.o_ps, 1)
            dve.wait_ge(S.p_ready, 2 * u + 2)
            rec, fac = k.arec[:, 2 * u:2 * u + 2], k.afac[:, u:u + 1]
            e.link(dve.reciprocal(rec, k.asum[:, 2 * u:2 * u + 2]))
            e.link(dve.tensor_tensor(fac, rec[:, 1:2], k.asum[:, 2 * u:2 * u + 1], ALU.mult))
            e.link(dve.tensor_tensor(fac, fac, k.lamt[:, 133:134], ALU.mult))
            p = k.ap[u % 2]
            dve.scalar_tensor_tensor(p[:, 0, :], p[:, 1, :], fac, p[:, 0, :], ALU.mult, ALU.add).then_inc(S.s_ready, 1)
        if u >= 3:
            v = u - 3
            h, i = AUNITS[v]
            dve.wait_ge(S.ov_ps, v + 1)
            dve.tensor_scalar(k.amix[:, i, h * P:(h + 1) * P], k.ps[:, 6 + v % 2, 0:P], k.arec[:, 2 * v:2 * v + 1],
                              None, ALU.mult).then_inc(S.ov_taken, 1)


def dan_act(k, e, _):
    head_norm_act(k, e, k.amix, NT1, k.av[:, 0:2, :])


def dan_dve(k, e, _):
    head_norm_dve(k, e, k.amix, NT1, k.av[:, 0:2, :], cols(C3, k.c3, "subln"), 1.0 - LAMBDA_INIT)


def amt_pe(k, e, slot, _):
    transposes_pe(k, e.eng, k.amix, NT1)


def amt_act(k, e, _):
    transposes_take(k, e, k.both(NT1), NT1, 1)


def amt_dve(k, e, _):
    transposes_take(k, e, k.both(NT1), NT1, 0)


BEFORE = [(ada_pe, ada_act, ada_dve, no_pool, 0), (modt_pe, park_act, modt_dve, modt_pool, (0, NT2))]
PER_HALF = [(gates_pe, gates_act, gates_dve, no_pool, None), (qkv_pe, qkv_act, qkv_dve, no_pool, None),
            (scan_pe, scan_act, scan_dve, scan_pool, None), (nothing_pe, opark_act, nothing, no_pool, None)]
AFTER = [(z_pe, z_act, z_dve, no_pool, None),
         (omt_pe, omt_act, omt_dve, modt_pool, (0, NT2)),
         (proj_pe, nothing, proj_dve, no_pool, (0, NT2)), (nothing_pe, ln_act, ln_dve, no_pool, (0, NT2)),
         (modt_pe, modt_act, modt_dve, modt_pool, (1, NT2)),
         (ffn2_pe, ffn2_act, ffn2_dve, no_pool, (0, NT1, NT2)),
         (ffn2_pe, ffn2_act, ffn2_dve, no_pool, (NT1, NT2 - NT1, NT2)),
         (nothing_pe, ln_act, ln_dve, no_pool, (1, NT2)),
         (ada_pe, ada_act, ada_dve, no_pool, 1), (modt_pe, modt_act, modt_dve, modt_pool, (0, NT2)),
         (dap_pe, dap_act, dap_dve, no_pool, None), (da_pe, da_act, da_dve, no_pool, None),
         (nothing_pe, dan_act, dan_dve, no_pool, None), (amt_pe, amt_act, amt_dve, xt_pool, None),
         (proj_pe, nothing, proj_dve, no_pool, (0, NT1)), (nothing_pe, ln_act, ln_dve, no_pool, (2, NT1)),
         (modt_pe, modt_act, modt_dve, modt_pool, (1, NT1)),
         (ffn2_pe, ffn2_act, ffn2_dve, no_pool, (0, NT1, NT1)), (nothing_pe, ln_act, ln_dve, no_pool, (3, NT1))]


def second_pe(k, e, slot):
    for f, _, _, _, arg in BEFORE:
        f(k, e, slot, arg)
        stage_end(k, e, "pe")
    with e.eng.Fori(0, 2):
        for f, _, _, _, arg in PER_HALF:
            f(k, e, slot, arg)
            stage_end(k, e, "pe")
    for f, _, _, _, arg in AFTER:
        f(k, e, slot, arg)
        stage_end(k, e, "pe")


def second_act(k, e):
    for _, f, _, _, arg in BEFORE:
        f(k, e, arg)
        stage_end(k, e, "act")
    with e.eng.Fori(0, 2) as k.half:
        for _, f, _, _, arg in PER_HALF:
            f(k, e, arg)
            stage_end(k, e, "act")
    for _, f, _, _, arg in AFTER:
        f(k, e, arg)
        stage_end(k, e, "act")
    e.eng.dma_start(k.T["out"].rearrange("(t p) d -> p t d", p=P), k.x[:, 0:NT1, :]).then_inc(k.S.stored, 16)
    e.eng.wait_ge(k.S.stored, 16)


def second_dve(k, e):
    for _, _, f, _, arg in BEFORE:
        f(k, e, arg)
        stage_end(k, e, "dve")
    with e.eng.Fori(0, 2):
        for _, _, f, _, arg in PER_HALF:
            f(k, e, arg)
            stage_end(k, e, "dve")
    for _, _, f, _, arg in AFTER:
        f(k, e, arg)
        stage_end(k, e, "dve")


def second_pool(k, e):
    for _, _, _, f, arg in BEFORE:
        f(k, e, arg)
        stage_end_pool(k, e)
    with e.eng.Fori(0, 2):
        for _, _, _, f, arg in PER_HALF:
            f(k, e, arg)
            stage_end_pool(k, e)
    for _, _, _, f, arg in AFTER:
        f(k, e, arg)
        stage_end_pool(k, e)


def k_tiles(w):
    return w.reshape(-1, P, w.shape[1]).transpose(1, 0, 2)


def chunk_slabs(w):
    return [k_tiles(w[:, c:c + 512]).reshape(P, SLAB) for c in range(0, w.shape[1], 512)]


def ffn_slabs(gate, up, down):
    out = []
    for f in range(0, FT, 2):
        out.append(np.concatenate([k_tiles(m[:, (f + i) * P:(f + i + 1) * P]).reshape(P, KT * P)
                                   for i in range(2) for m in (gate, up)], axis=1))
    for c in range(2):
        for f0, nf in ((0, 8), (8, 8), (16, 6)):
            part = k_tiles(down[f0 * P:(f0 + nf) * P, 512 * c:512 * c + 512]).reshape(P, nf * 512)
            out.append(np.concatenate([part, np.zeros((P, SLAB - nf * 512), np.float32)], axis=1))
    return out


def head_slabs(w):
    return [k_tiles(w[:, c:c + 512]).reshape(P, KT, 2, 256).transpose(0, 2, 1, 3).reshape(P, SLAB)
            for c in range(0, w.shape[1], 512)]


def layer_slabs(w_in, w_out, gate_up, w_down, w1):
    nq = [w_in[:, 1536 + 64 * h:1600 + 64 * h] for h in range(N_NSA)]
    kv = [w_in[:, 1920 + P * i:1920 + P * (i + 1)] for i in range(6)]
    groups = [w_in[:, P * i:P * (i + 1)] for i in range(6)]
    groups += [np.concatenate([nq[i], nq[i + 3]], axis=1) for i in range(3)]
    groups += [kv[0], kv[1], kv[2], kv[4]]
    tiles = [k_tiles(g).reshape(P, 1024) for g in groups]
    ng = k_tiles(w_in[:, 2688:2706]).reshape(P, KT * 18)
    out = [np.concatenate(tiles[4 * i:4 * i + 4], axis=1) for i in range(3)]
    out.append(np.concatenate([tiles[12], ng, np.zeros((P, SLAB - 1024 - KT * 18), np.float32)], axis=1))
    out += chunk_slabs(np.concatenate([w_in[:, 768:1152], kv[3], w_in[:, 1152:1536], kv[5], w_in[:, 2706:3218]], axis=1))
    one = w1.reshape(2, 32, 64, 64).transpose(2, 0, 1, 3).reshape(64, SLAB)
    out.append(np.concatenate([one, one], axis=0))
    out += chunk_slabs(w_out)
    out += ffn_slabs(gate_up[:, :F], gate_up[:, F:], w_down)
    return out


def constants1():
    c = np.zeros((P, N_C1), np.float32)

    def put(name, v):
        at, n = C1[name]
        c[:, at:at + n] = v

    m = np.arange(P)[:, None]
    f = np.arange(512)[None, :]
    for h in range(N_RET):
        gamma = math.log(1.0 - 2.0 ** (-5.0 - h))
        c[:, 512 * h:512 * h + 512] = np.where(f >= m, np.exp(np.maximum(f - m, 0) * gamma) * HD ** -0.5, 0.0)
    d = np.arange(P) % 32
    inv = (np.float32(10000.0) ** (-np.arange(32, dtype=np.float32) / np.float32(32))).astype(np.float32)
    ang = np.arange(512, dtype=np.float32)[None, :] * inv[d][:, None]
    put("cos", np.cos(ang.astype(np.float64)))
    put("sin", np.sin(ang.astype(np.float64)))
    q = np.arange(P)
    put("causal", (q[:, None] <= q[None, :]))
    rot = np.zeros((P, P))
    for j in range(P):
        if j % 64 < 32:
            rot[j + 32, j] = -1.0
        else:
            rot[j - 32, j] = 1.0
    put("rot", rot)
    put("blk", (q[:, None] // 64 == q[None, :] // 64) / 64.0)
    put("flip", q[:, None] + q[None, :] == P - 1)
    put("valid", (q[:, None] >= 31))
    return c


def bias_line():
    dist = 511 - np.arange(1024)
    hot = np.zeros((32, 1024), np.float32)
    hot[t5_bucket(dist), np.arange(1024)] = 1.0
    neg = np.broadcast_to(np.where(dist < 0, -BIG, 0.0).astype(np.float32), (6, 1024))
    return hot.reshape(32, 2, 512), np.ascontiguousarray(neg).reshape(6, 2, 512)


def small_params(v):
    out = np.zeros((DEPTH, P, N_SM), np.float32)
    for l in range(DEPTH):
        def put(name, a, rows=P):
            at, n = SM[name]
            out[l, :rows, at:at + n] = a
        put("attn_norm", v["attn_norm"][l].reshape(8, P).T)
        put("ffn_norm", v["ffn_norm"][l].reshape(8, P).T)
        put("q_gain", np.concatenate([v["nsa_q_gain"][l]] * 2)[:, None])
        put("k_gain", np.concatenate([v["nsa_k_gain"][l].T] * 2, axis=0))
        pe = v["cmp_pe"][l].transpose(2, 0, 1).reshape(64, 64)
        put("pe", np.concatenate([pe, pe], axis=0))
        at = SM["w2k"][0]
        out[l, 0:64, at:at + 64] = v["cmp_w2"][l, 0]
        out[l, 0:64, at + 192:at + 256] = v["cmp_w2"][l, 0]
        put("w2v", v["cmp_w2"][l, 1], 64)
        put("ws", v["gm_ws"][l].transpose(2, 0, 1).reshape(P, 512))
        put("gm_b", v["gm_b"][l].T)
    return out


def constants2(norm_g):
    p, f = np.arange(P)[:, None], np.arange(P)[None, :]
    parts = [(p <= f), (p >= f)]
    parts += [np.where(p > f, 0.0, BIG), np.where(p < f, 0.0, BIG)]
    parts += [np.where(p <= f, 0.0, -BIG), np.where(p >= f, 0.0, -BIG)]
    parts += [p // 16 == f // 16]
    parts += [(p // n == f // n) & (p // (n // 2) != f // (n // 2)) for n in (32, 64, 128)]
    parts += [np.broadcast_to(norm_g, (P, P))]
    return np.concatenate([np.asarray(a, np.float32) for a in parts], axis=1)


def constants3(subln):
    quarter = HD // 4
    inv = (np.float32(10000.0) ** (-np.arange(quarter, dtype=np.float32) / np.float32(quarter))).astype(np.float32)
    t = np.arange(SEQ)
    row, col = (t // 64).astype(np.float32), (t % 64).astype(np.float32)
    d = np.arange(P) % HD
    ang = np.where((d < 32)[:, None], row[None, :], col[None, :]).astype(np.float32) * inv[d % quarter][:, None]
    rot = np.zeros((P, P))
    for j in range(P):
        if j % 32 < 16:
            rot[j + 16, j] = -1.0
        else:
            rot[j - 16, j] = 1.0
    ang = ang.astype(np.float64)
    rotary = np.stack([np.cos(ang), np.sin(ang)], axis=1).astype(np.float32)
    return rotary, np.concatenate([rot, np.broadcast_to(subln, (P, P))], axis=1).astype(np.float32)


def half_params(v):
    out = []
    w = v["dn_w_in_2"][0]
    conv = v["dn_conv_2"][0]
    for half in range(2):
        heads = [half * HALF + h for h in range(HALF)]
        taps = np.stack([conv[:, base + P * h:base + P * (h + 1)].T for base in (0, D, 2 * D) for h in heads], axis=1)
        at = 4 * D
        pick = [at + 16 * m + 8 * d + h for m in range(2) for d in range(2) for h in heads]
        wab = k_tiles(w[:, pick]).reshape(P, KT * 16)
        alog = np.broadcast_to(np.concatenate([v["dn_a_log_2"][0, d, heads] for d in range(2)]), (P, 8))
        dt = np.broadcast_to(np.concatenate([v["dn_dt_bias_2"][0, d, heads] for d in range(2)]), (P, 8))
        out.append(np.concatenate([taps.reshape(P, 60), wab, alog, dt], axis=1))
    return np.stack(out)


def second_slabs(v):
    w = v["dn_w_in_2"][0]
    out = chunk_slabs(v["ada_w_2"][0])
    for half in range(2):
        for base in (0, D, 2 * D):
            out += head_slabs(w[:, base + 512 * half:base + 512 * half + 512])
    out += chunk_slabs(w[:, 3 * D:4 * D])
    out += chunk_slabs(v["dn_w_out_2"][0])
    for _ in range(2):
        out += ffn_slabs(v["ffn_w_gate_2"][0], v["ffn_w_up_2"][0], v["ffn_w_down_2"][0])
    out += chunk_slabs(v["ada_w_2"][1])
    out += head_slabs(v["da_w_in_2"][0][:, :2 * D]) + chunk_slabs(v["da_w_in_2"][0][:, 2 * D:])
    out += chunk_slabs(v["da_w_out_2"][0])
    out += ffn_slabs(v["ffn_w_gate_2"][1], v["ffn_w_up_2"][1], v["ffn_w_down_2"][1])
    return out


def kernel(**inputs):
    import concourse.bacc as bacc
    from concourse.bass_utils import run_bass_kernel_spmd

    v = {name: np.asarray(a) for name, a in inputs.items()}
    slabs = []
    for l in range(DEPTH):
        slabs += layer_slabs(v["w_in"][l], v["w_out"][l], v["w_gate_up"][l], v["w_down"][l], v["cmp_w1"][l])
    slabs += second_slabs(v)
    hot, neg = bias_line()
    cond = np.stack([v["c_2"][0].reshape(KT, P).T, v["c_ctx_2"].reshape(KT, P).T], axis=2)
    ln = np.stack([np.stack([v[f"ln{n}_g_2"][l], v[f"ln{n}_b_2"][l]]) for l in range(DEPTH) for n in (1, 2)])
    sel = np.zeros((2, 2, P), np.float32)
    sel[0, 0], sel[1, 1] = 1.0, 1.0
    lam = v["da_lambda_2"][0]
    rotary, c3 = constants3(v["da_subln_g_2"][0])
    c0 = np.concatenate([np.eye(P, dtype=np.float32), np.ones((P, P), np.float32)], axis=1)
    arrays = {
        "pieces": np.stack(slabs).reshape(-1, P, 2, PIECE).transpose(0, 2, 1, 3).reshape(-1, P, PIECE), "x": v["x"].reshape(SEQ, D), "c0": c0, "c1": constants1(), "onehot": hot,
        "negline": neg, "rel_bias": v["rel_bias"], "small1": small_params(v),
        "cond": cond, "ctx": v["ctx_2"].reshape(CTX, D), "ada_b": np.stack([v["ada_b_2"], v["ada_b_2"]], axis=1),
        "sel": sel, "ln": ln, "c2": constants2(v["dn_norm_g_2"][0]), "rotary": rotary, "c3": c3,
        "dn": half_params(v), "lam": np.stack([lam[0::2], lam[1::2]]),
    }
    nc = bacc.Bacc("TRN2", target_bir_lowering=False, num_devices=1)
    T = {}
    for name, a in arrays.items():
        arrays[name] = np.ascontiguousarray(a)
        T[name] = nc.dram_tensor(name, a.shape, F32, kind="ExternalInput").ap()
    T["out"] = nc.dram_tensor("out", (SEQ, D), F32, kind="ExternalOutput").ap()
    T["line"] = nc.dram_tensor("line", (N_NSA, 1024), F32).ap()
    T["x_park"] = nc.dram_tensor("x_park", (P, NT2, D), F32).ap()
    T["gt_park"] = nc.dram_tensor("gt_park", (P, 4, D), F32).ap()
    T["o_park"] = nc.dram_tensor("o_park", (2, P, NT2, HALF * P), F32).ap()
    build(nc, T)
    r = run_bass_kernel_spmd(nc, [arrays], core_ids=[0])
    return r.results[0]["out"].reshape(1, SEQ, D)
```
